# Optimizing a Trainium2 kernel written in Bass

```python
import math
import jax, jax.numpy as jnp
from jax import lax
import numpy as np

D_MODEL = 1024
BATCH = 1
SEQ = 256
DEPTH = 1

PLE_DIM = 256
DIFF_HEADS = 4
DIFF_HEAD_DIM = 64
DIFF_WIDTH = DIFF_HEADS * 2 * DIFF_HEAD_DIM
MOBA_HEADS = 8
MOBA_HEAD_DIM = 64
MOBA_WIDTH = MOBA_HEADS * MOBA_HEAD_DIM
MOBA_BLOCK = 256
MOBA_TOPK = 3
ROT_DIM = 16
ROPE_THETA = 500000.0
Q_CHUNK = 128
N_BRANCHES = 2
IN_COLS = 4 * DIFF_WIDTH + 4 * MOBA_WIDTH + N_BRANCHES * D_MODEL
EPS = 1e-6
SUBLN_EPS = 1e-5


def rms_norm(x, g, eps=EPS):
    xf = x.astype(jnp.float32)
    y = xf * lax.rsqrt(jnp.mean(xf * xf, axis=-1, keepdims=True) + eps)
    return (y * g.astype(jnp.float32)).astype(x.dtype)

def rope_tables(seq):
    inv = ROPE_THETA ** (-jnp.arange(0, ROT_DIM, 2, dtype=jnp.float32) / ROT_DIM)
    ang = jnp.arange(seq, dtype=jnp.float32)[:, None] * inv[None, :]
    return jnp.cos(ang), jnp.sin(ang)

def partial_rope(x, cos, sin):
    half = ROT_DIM // 2
    shape = (1, cos.shape[0]) + (1,) * (x.ndim - 3) + (half,)
    c = cos.reshape(shape).astype(x.dtype)
    s = sin.reshape(shape).astype(x.dtype)
    x1 = x[..., :half]
    x2 = x[..., half:ROT_DIM]
    rot = jnp.concatenate([x1 * c - x2 * s, x2 * c + x1 * s], axis=-1)
    return jnp.concatenate([rot, x[..., ROT_DIM:]], axis=-1)

def split_in_proj(proj):
    sizes = (DIFF_WIDTH,) * 4 + (MOBA_WIDTH,) * 4 + (N_BRANCHES * D_MODEL,)
    idx = []
    acc = 0
    for s in sizes[:-1]:
        acc += s
        idx.append(acc)
    return jnp.split(proj, idx, axis=-1)

def diff_attention(q, k, v, lam, lam_init, subln_g):
    B, S, H, _, dh = q.shape
    n_chunks = S // Q_CHUNK
    scale = dh ** -0.5
    key_pos = jnp.arange(S)
    qc = q.reshape(B, n_chunks, Q_CHUNK, H, 2, dh).transpose(1, 0, 2, 3, 4, 5)

    def one_chunk(args):
        c, q_blk = args
        s = jnp.einsum('bqhmd,bkhmd->bhmqk', q_blk, k).astype(jnp.float32) * scale
        q_pos = c * Q_CHUNK + jnp.arange(Q_CHUNK)
        s = jnp.where(key_pos[None, :] <= q_pos[:, None], s, -jnp.inf)
        a = jax.nn.softmax(s, axis=-1)
        w = a[:, :, 0] - lam * a[:, :, 1]
        return jnp.einsum('bhqk,bkhe->bqhe', w.astype(v.dtype), v)

    o = lax.map(one_chunk, (jnp.arange(n_chunks), qc))
    o = o.transpose(1, 0, 2, 3, 4).reshape(B, S, H, 2 * dh)
    o = rms_norm(o, subln_g, SUBLN_EPS) * (1.0 - lam_init)
    return o.reshape(B, S, H * 2 * dh)

def moba_attention(q, k, v):
    B, S, H, dh = q.shape
    nb = -(-S // MOBA_BLOCK)
    pad = nb * MOBA_BLOCK - S
    kp = jnp.pad(k, ((0, 0), (0, pad), (0, 0), (0, 0)))
    vp = jnp.pad(v, ((0, 0), (0, pad), (0, 0), (0, 0)))
    k_blocks = kp.reshape(B, nb, MOBA_BLOCK, H, dh).transpose(0, 3, 1, 2, 4)
    v_blocks = vp.reshape(B, nb, MOBA_BLOCK, H, dh).transpose(0, 3, 1, 2, 4)
    k_mean = jnp.mean(k_blocks.astype(jnp.float32), axis=3).astype(k.dtype)
    topk = min(MOBA_TOPK, nb)
    scale = dh ** -0.5
    n_chunks = S // Q_CHUNK
    qc = q.reshape(B, n_chunks, Q_CHUNK, H, dh).transpose(1, 0, 3, 2, 4)
    b_idx = jnp.arange(B)[:, None, None, None]
    h_idx = jnp.arange(H)[None, :, None, None]
    blk_ids = jnp.arange(nb)

    def one_chunk(args):
        c, q_blk = args
        q_start = c * Q_CHUNK
        own = q_start // MOBA_BLOCK
        q_pos = q_start + jnp.arange(Q_CHUNK)
        gate = jnp.einsum('bhqd,bhnd->bhqn', q_blk, k_mean).astype(jnp.float32)
        gate = jnp.where(blk_ids < own, gate, -jnp.inf)
        _, sel = lax.top_k(gate, topk)
        sel_valid = jnp.arange(topk) < own
        k_sel = k_blocks[b_idx, h_idx, sel]
        v_sel = v_blocks[b_idx, h_idx, sel]
        s_sel = jnp.einsum('bhqd,bhqrkd->bhqrk', q_blk, k_sel).astype(jnp.float32) * scale
        s_sel = jnp.where(sel_valid[:, None], s_sel, -jnp.inf).reshape(B, H, Q_CHUNK, topk * MOBA_BLOCK)
        k_own = lax.dynamic_index_in_dim(k_blocks, own, axis=2, keepdims=False)
        v_own = lax.dynamic_index_in_dim(v_blocks, own, axis=2, keepdims=False)
        s_own = jnp.einsum('bhqd,bhkd->bhqk', q_blk, k_own).astype(jnp.float32) * scale
        own_pos = own * MOBA_BLOCK + jnp.arange(MOBA_BLOCK)
        s_own = jnp.where(own_pos[None, :] <= q_pos[:, None], s_own, -jnp.inf)
        pr = jax.nn.softmax(jnp.concatenate([s_sel, s_own], axis=-1), axis=-1).astype(v.dtype)
        p_sel = pr[..., :topk * MOBA_BLOCK].reshape(B, H, Q_CHUNK, topk, MOBA_BLOCK)
        p_own = pr[..., topk * MOBA_BLOCK:]
        return (jnp.einsum('bhqrk,bhqrkd->bhqd', p_sel, v_sel)
                + jnp.einsum('bhqk,bhkd->bhqd', p_own, v_own))

    o = lax.map(one_chunk, (jnp.arange(n_chunks), qc))
    return o.transpose(1, 0, 3, 2, 4).reshape(B, S, H * dh)

def first_inputs(seed: int = 0) -> dict:
    key = jax.random.key(seed)
    ks = jax.random.split(key, 16)
    f32 = jnp.float32
    nrm = lambda k, shape, sc: jax.random.normal(k, shape, f32) * sc
    return {
        'x': nrm(ks[0], (BATCH, SEQ, D_MODEL), 1.0),
        'p': nrm(ks[1], (DEPTH, BATCH, SEQ, PLE_DIM), 1.0),
        'norm_g': 1.0 + nrm(ks[2], (DEPTH, D_MODEL), 0.02),
        'w_in': nrm(ks[3], (DEPTH, D_MODEL, IN_COLS), D_MODEL ** -0.5),
        'lambda_q1': nrm(ks[4], (DEPTH, DIFF_HEAD_DIM), 0.1),
        'lambda_k1': nrm(ks[5], (DEPTH, DIFF_HEAD_DIM), 0.1),
        'lambda_q2': nrm(ks[6], (DEPTH, DIFF_HEAD_DIM), 0.1),
        'lambda_k2': nrm(ks[7], (DEPTH, DIFF_HEAD_DIM), 0.1),
        'subln_g': 1.0 + nrm(ks[8], (DEPTH, 2 * DIFF_HEAD_DIM), 0.02),
        'w_branch_diff': nrm(ks[9], (DEPTH, DIFF_WIDTH, D_MODEL), DIFF_WIDTH ** -0.5),
        'w_branch_moba': nrm(ks[10], (DEPTH, MOBA_WIDTH, D_MODEL), MOBA_WIDTH ** -0.5),
        'w_out': nrm(ks[11], (DEPTH, D_MODEL, D_MODEL), D_MODEL ** -0.5),
        'w_ple': nrm(ks[12], (DEPTH, PLE_DIM, D_MODEL), PLE_DIM ** -0.5),
        'w_ple_gate': nrm(ks[13], (DEPTH, D_MODEL, D_MODEL), D_MODEL ** -0.5),
        'final_g': 1.0 + nrm(ks[14], (D_MODEL,), 0.02),
    }

def first_block(x, p, norm_g, w_in, lambda_q1, lambda_k1, lambda_q2, lambda_k2, subln_g,
              w_branch_diff, w_branch_moba, w_out, w_ple, w_ple_gate, final_g):
    B, S, _ = x.shape
    cos, sin = rope_tables(S)
    for i in range(DEPTH):
        lam_init = 0.8 - 0.6 * math.exp(-0.3 * i)
        h = rms_norm(x, norm_g[i])
        proj = h @ w_in[i]
        dq, dk, dv, dg, mq, mk, mv, mg, gates = split_in_proj(proj)
        dq = partial_rope(dq.reshape(B, S, DIFF_HEADS, 2, DIFF_HEAD_DIM), cos, sin)
        dk = partial_rope(dk.reshape(B, S, DIFF_HEADS, 2, DIFF_HEAD_DIM), cos, sin)
        dv = dv.reshape(B, S, DIFF_HEADS, 2 * DIFF_HEAD_DIM)
        lam = (jnp.exp(jnp.sum(lambda_q1[i].astype(jnp.float32) * lambda_k1[i].astype(jnp.float32)))
               - jnp.exp(jnp.sum(lambda_q2[i].astype(jnp.float32) * lambda_k2[i].astype(jnp.float32)))
               + lam_init)
        o_a = diff_attention(dq, dk, dv, lam, lam_init, subln_g[i]) * jax.nn.silu(dg)
        y_a = o_a @ w_branch_diff[i]
        mq = partial_rope(mq.reshape(B, S, MOBA_HEADS, MOBA_HEAD_DIM), cos, sin)
        mk = partial_rope(mk.reshape(B, S, MOBA_HEADS, MOBA_HEAD_DIM), cos, sin)
        mv = mv.reshape(B, S, MOBA_HEADS, MOBA_HEAD_DIM)
        o_b = moba_attention(mq, mk, mv) * jax.nn.silu(mg)
        y_b = o_b @ w_branch_moba[i]
        g_a, g_b = jnp.split(gates, N_BRANCHES, axis=-1)
        merged = jax.nn.sigmoid(g_a) * y_a + jax.nn.sigmoid(g_b) * y_b
        x = x + merged @ w_out[i]
        x = x + jax.nn.sigmoid(x @ w_ple_gate[i]) * (p[i] @ w_ple[i])
    return rms_norm(x, final_g)


D_MIX = D_MODEL
HEAD_DIM = 64
NSA_HEADS = 8
NSA_KV_HEADS = 2
NSA_WIDTH = NSA_HEADS * HEAD_DIM
KV_W = NSA_KV_HEADS * HEAD_DIM
CONV_GROUPS = 8
CONV_WIDTH = D_MIX - NSA_WIDTH
CONV_K = 3
CMP_BLK = 32
CMP_STRIDE = 16
SEL_BLK = 64
SEL_TOPN = 8
WINDOW = 512
Q_BLK = 64
FORCE_SCORE = 1e4
REL_BUCKETS = 32
REL_MAX_DIST = 128
PEER_HEADS = 8
PEER_NKEYS = 128
PEER_EXPERTS = PEER_NKEYS * PEER_NKEYS
PEER_QDIM = 128
PEER_TOPK = 16
PEER_CHUNK = 128

IN_SIZES = (NSA_WIDTH, KV_W, KV_W, KV_W, KV_W, KV_W, KV_W, NSA_HEADS * 3,
            CONV_WIDTH, CONV_WIDTH, CONV_WIDTH)
IN_COLS_2 = sum(IN_SIZES)
SPLIT_POINTS = tuple(int(v) for v in np.cumsum(IN_SIZES)[:-1])


def rmsnorm(x, g):
    x32 = x.astype(jnp.float32)
    y = x32 * lax.rsqrt(jnp.mean(x32 * x32, axis=-1, keepdims=True) + EPS)
    return y.astype(x.dtype) * g

def masked_softmax(logits, mask):
    logits = jnp.where(mask, logits.astype(jnp.float32), -1e30)
    p = jax.nn.softmax(logits, axis=-1)
    return jnp.where(jnp.any(mask, axis=-1, keepdims=True), p, 0.0)

def rel_bucket(dist):
    n = jnp.maximum(dist, 0)
    exact = REL_BUCKETS // 2
    log_ratio = jnp.log(jnp.maximum(n, 1).astype(jnp.float32) / exact) / math.log(REL_MAX_DIST / exact)
    large = exact + (log_ratio * (REL_BUCKETS - exact)).astype(jnp.int32)
    return jnp.where(n < exact, n, jnp.minimum(large, REL_BUCKETS - 1))

def nsa_mixer(q, kc_tok, vc_tok, ks_tok, vs_tok, kw_tok, vw_tok, gates,
              cmp_pe_k, cmp_pe_v, cmp_wk1, cmp_wk2, cmp_wv1, cmp_wv2, rel_table):
    B, S = q.shape[0], q.shape[1]
    G, R, dh = NSA_KV_HEADS, NSA_HEADS // NSA_KV_HEADS, HEAD_DIM

    n_cmp = (S - CMP_BLK) // CMP_STRIDE + 1
    cmp_start = np.arange(n_cmp) * CMP_STRIDE
    tok_idx = cmp_start[:, None] + np.arange(CMP_BLK)[None, :]
    cmp_end = jnp.asarray(cmp_start + CMP_BLK - 1, jnp.int32)

    def compress(tok, pe, w1, w2):
        blk = tok[:, tok_idx] + pe[None, None, :, None, :]
        flat = blk.transpose(0, 1, 3, 2, 4).reshape(B, n_cmp, G, CMP_BLK * dh)
        return jax.nn.gelu(flat @ w1) @ w2

    kc = compress(kc_tok, cmp_pe_k, cmp_wk1, cmp_wk2)
    vc = compress(vc_tok, cmp_pe_v, cmp_wv1, cmp_wv2)

    n_slc = S // SEL_BLK
    n_sel = min(SEL_TOPN, n_slc)
    slc_start = np.arange(n_slc) * SEL_BLK
    overlap = (cmp_start[:, None] < slc_start[None, :] + SEL_BLK) & (cmp_start[:, None] + CMP_BLK > slc_start[None, :])
    cmp_to_slc = jnp.asarray(overlap, jnp.float32)
    ks_blk = ks_tok.reshape(B, n_slc, SEL_BLK, G, dh).transpose(0, 3, 1, 2, 4)
    vs_blk = vs_tok.reshape(B, n_slc, SEL_BLK, G, dh).transpose(0, 3, 1, 2, 4)

    kw_pad = jnp.pad(kw_tok, ((0, 0), (WINDOW, 0), (0, 0), (0, 0)))
    vw_pad = jnp.pad(vw_tok, ((0, 0), (WINDOW, 0), (0, 0), (0, 0)))

    b_ix = jnp.arange(B)[:, None, None]
    g_ix = jnp.arange(G)[None, :, None]
    rel_g = rel_table.reshape(REL_BUCKETS, G, R)
    blk_ids = jnp.arange(n_slc)
    scale = HEAD_DIM ** -0.5

    def head_bias(dist):
        return jnp.transpose(rel_table[rel_bucket(dist)], (2, 0, 1)).reshape(G, R, *dist.shape)

    def query_block(i):
        t0 = i * Q_BLK
        t = t0 + jnp.arange(Q_BLK)
        qb = lax.dynamic_slice_in_dim(q, t0, Q_BLK, axis=1).reshape(B, Q_BLK, G, R, dh) * scale
        gb = jax.nn.sigmoid(lax.dynamic_slice_in_dim(gates, t0, Q_BLK, axis=1).astype(jnp.float32))
        gb = gb.reshape(B, Q_BLK, G, R, 3)

        s = jnp.einsum('bqgrd,bngd->bgrqn', qb, kc) + head_bias(t[:, None] - cmp_end[None, :])
        p_cmp = masked_softmax(s, cmp_end[None, :] <= t[:, None])
        o_cmp = jnp.einsum('bgrqn,bngd->bqgrd', p_cmp, vc)

        imp = jnp.einsum('bgrqn,nj->bgqj', p_cmp, cmp_to_slc)
        cur = t // SEL_BLK
        forced = (blk_ids[None, :] == 0) | (blk_ids[None, :] == cur[:, None]) | (blk_ids[None, :] == cur[:, None] - 1)
        allowed = blk_ids[None, :] * SEL_BLK <= t[:, None]
        imp = jnp.where(forced, FORCE_SCORE, jnp.where(allowed, imp, -jnp.inf))
        _, sel = lax.top_k(imp, n_sel)
        L = n_sel * SEL_BLK
        sel_flat = sel.reshape(B, G, Q_BLK * n_sel)
        ks = ks_blk[b_ix, g_ix, sel_flat].reshape(B, G, Q_BLK, L, dh)
        vs = vs_blk[b_ix, g_ix, sel_flat].reshape(B, G, Q_BLK, L, dh)
        kpos = (sel[..., None] * SEL_BLK + jnp.arange(SEL_BLK)).reshape(B, G, Q_BLK, L)
        dist = t[:, None] - kpos
        bias = rel_g[rel_bucket(dist), jnp.arange(G)[:, None, None]]
        s = jnp.einsum('bqgrd,bgqld->bgrql', qb, ks) + bias.transpose(0, 1, 4, 2, 3)
        p = masked_softmax(s, (dist >= 0)[:, :, None])
        o_slc = jnp.einsum('bgrql,bgqld->bqgrd', p, vs)

        kw = lax.dynamic_slice_in_dim(kw_pad, t0, Q_BLK + WINDOW, axis=1)
        vw = lax.dynamic_slice_in_dim(vw_pad, t0, Q_BLK + WINDOW, axis=1)
        kpos_w = t0 - WINDOW + jnp.arange(Q_BLK + WINDOW)
        dist_w = t[:, None] - kpos_w[None, :]
        mask_w = (dist_w >= 0) & (dist_w < WINDOW) & (kpos_w[None, :] >= 0)
        s = jnp.einsum('bqgrd,blgd->bgrql', qb, kw) + head_bias(dist_w)
        p = masked_softmax(s, mask_w)
        o_win = jnp.einsum('bgrql,blgd->bqgrd', p, vw)

        o = gb[..., 0:1] * o_cmp + gb[..., 1:2] * o_slc + gb[..., 2:3] * o_win
        return o.reshape(B, Q_BLK, NSA_WIDTH)

    out = lax.map(query_block, jnp.arange(S // Q_BLK))
    return out.transpose(1, 0, 2, 3).reshape(B, S, NSA_WIDTH)

def short_conv_mixer(h, b_gate, c_gate, conv_w):
    z = c_gate * h
    y = lax.conv_general_dilated(z, conv_w.astype(z.dtype), window_strides=(1,),
                                 padding=((CONV_K - 1, 0),),
                                 dimension_numbers=('NWC', 'WIO', 'NWC'),
                                 feature_group_count=CONV_WIDTH)
    return b_gate * y

def peer_ffn(xn, w_q, sub_keys, expert_u, expert_v):
    B, S, D = xn.shape
    q = (xn @ w_q).reshape(B, S, PEER_HEADS, 2, PEER_QDIM // 2)
    s = jnp.einsum('bshpd,hpkd->bshpk', q, sub_keys)
    v_half, i_half = lax.top_k(s, PEER_TOPK)
    cand = v_half[..., 0, :, None] + v_half[..., 1, None, :]
    top_s, top_c = lax.top_k(cand.reshape(B, S, PEER_HEADS, PEER_TOPK * PEER_TOPK), PEER_TOPK)
    i1 = jnp.take_along_axis(i_half[..., 0, :], top_c // PEER_TOPK, axis=-1)
    i2 = jnp.take_along_axis(i_half[..., 1, :], top_c % PEER_TOPK, axis=-1)
    experts = i1 * PEER_NKEYS + i2
    g = jax.nn.softmax(top_s.astype(jnp.float32), axis=-1)
    E = PEER_HEADS * PEER_TOPK
    n_chunk = (B * S) // PEER_CHUNK
    xs = xn.reshape(n_chunk, PEER_CHUNK, D)
    es = experts.reshape(n_chunk, PEER_CHUNK, E)
    gs = g.reshape(n_chunk, PEER_CHUNK, E)

    def chunk(args):
        xc, ec, gc = args
        u = expert_u[ec]
        act = jax.nn.gelu(jnp.einsum('cd,ced->ce', xc, u).astype(jnp.float32))
        return jnp.einsum('ce,ced->cd', gc * act, expert_v[ec])

    return lax.map(chunk, (xs, es, gs)).reshape(B, S, D)

def second_inputs(seed: int = 0) -> dict:
    key = jax.random.key(seed)
    ks = jax.random.split(key, 24)
    L, D, dh = DEPTH, D_MODEL, HEAD_DIM

    def nrm(k, shape, s):
        return jax.random.normal(k, shape, jnp.float32) * s

    def gain(k, shape):
        return 1.0 + 0.05 * jax.random.normal(k, shape, jnp.float32)

    return {
        'x': nrm(ks[0], (BATCH, SEQ, D), 1.0),
        'c': nrm(ks[1], (BATCH, D), 1.0),
        'ln_mix_g': gain(ks[2], (L, D)),
        'ln_ffn_g': gain(ks[3], (L, D)),
        'w_mod': nrm(ks[4], (L, D, 6 * D), 0.5 * D ** -0.5),
        'b_mod': nrm(ks[5], (L, 6 * D), 0.02),
        'w_in': nrm(ks[6], (L, D, IN_COLS_2), D ** -0.5),
        'cmp_pe_k': nrm(ks[7], (L, CMP_BLK, dh), 0.1),
        'cmp_pe_v': nrm(ks[8], (L, CMP_BLK, dh), 0.1),
        'cmp_wk1': nrm(ks[9], (L, CMP_BLK * dh, dh), (CMP_BLK * dh) ** -0.5),
        'cmp_wk2': nrm(ks[10], (L, dh, dh), dh ** -0.5),
        'cmp_wv1': nrm(ks[11], (L, CMP_BLK * dh, dh), (CMP_BLK * dh) ** -0.5),
        'cmp_wv2': nrm(ks[12], (L, dh, dh), dh ** -0.5),
        'conv_w': nrm(ks[13], (L, CONV_K, 1, CONV_WIDTH), CONV_K ** -0.5),
        'norm_attn_g': gain(ks[14], (L, NSA_WIDTH)),
        'norm_conv_g': gain(ks[15], (L, CONV_WIDTH)),
        'w_out': nrm(ks[16], (L, D_MIX, D), D_MIX ** -0.5),
        'peer_wq': nrm(ks[17], (L, D, PEER_HEADS * PEER_QDIM), D ** -0.5),
        'peer_keys': nrm(ks[18], (L, PEER_HEADS, 2, PEER_NKEYS, PEER_QDIM // 2), (PEER_QDIM // 2) ** -0.5),
        'peer_u': nrm(ks[19], (L, PEER_EXPERTS, D), D ** -0.5),
        'peer_v': nrm(ks[20], (L, PEER_EXPERTS, D), PEER_HEADS ** -0.5),
        'rel_table': nrm(ks[21], (REL_BUCKETS, NSA_HEADS), 0.5),
        'ln_final_g': gain(ks[22], (D,)),
    }

def second_block(x, c, ln_mix_g, ln_ffn_g, w_mod, b_mod, w_in, cmp_pe_k, cmp_pe_v,
              cmp_wk1, cmp_wk2, cmp_wv1, cmp_wv2, conv_w, norm_attn_g, norm_conv_g,
              w_out, peer_wq, peer_keys, peer_u, peer_v, rel_table, ln_final_g):
    B, S = x.shape[0], x.shape[1]
    c_act = jax.nn.silu(c)
    for l in range(DEPTH):
        mod = (c_act @ w_mod[l] + b_mod[l])[:, None, :]
        sh1, sc1, gt1, sh2, sc2, gt2 = jnp.split(mod, 6, axis=-1)

        h = rmsnorm(x, ln_mix_g[l]) * (1 + sc1) + sh1
        proj = h @ w_in[l]
        q, kc, vc, ksl, vsl, kw, vw, gts, cb, cc, ch = jnp.split(proj, SPLIT_POINTS, axis=-1)
        kv = lambda a: a.reshape(B, S, NSA_KV_HEADS, HEAD_DIM)
        o_attn = nsa_mixer(q.reshape(B, S, NSA_HEADS, HEAD_DIM), kv(kc), kv(vc), kv(ksl), kv(vsl),
                           kv(kw), kv(vw), gts.reshape(B, S, NSA_HEADS, 3),
                           cmp_pe_k[l], cmp_pe_v[l], cmp_wk1[l], cmp_wk2[l], cmp_wv1[l], cmp_wv2[l],
                           rel_table)
        o_conv = short_conv_mixer(ch, cb, cc, conv_w[l])
        mixed = jnp.concatenate([rmsnorm(o_attn, norm_attn_g[l]), rmsnorm(o_conv, norm_conv_g[l])], axis=-1)
        x = x + gt1 * (mixed @ w_out[l])

        h2 = rmsnorm(x, ln_ffn_g[l]) * (1 + sc2) + sh2
        x = x + gt2 * peer_ffn(h2, peer_wq[l], peer_keys[l], peer_u[l], peer_v[l])
    return rmsnorm(x, ln_final_g)


def setup_inputs(seed=0):
    out = dict(first_inputs(seed))
    for name, value in second_inputs(seed + 1).items():
        if name != "x":
            out[name + "_2"] = value
    return out


def reference(
    x, p, norm_g, w_in, lambda_q1, lambda_k1, lambda_q2, lambda_k2, subln_g, w_branch_diff,
    w_branch_moba, w_out, w_ple, w_ple_gate, final_g, c_2, ln_mix_g_2, ln_ffn_g_2, w_mod_2,
    b_mod_2, w_in_2, cmp_pe_k_2, cmp_pe_v_2, cmp_wk1_2, cmp_wk2_2, cmp_wv1_2, cmp_wv2_2,
    conv_w_2, norm_attn_g_2, norm_conv_g_2, w_out_2, peer_wq_2, peer_keys_2, peer_u_2, peer_v_2,
    rel_table_2, ln_final_g_2,
):
    x = first_block(
        x, p, norm_g, w_in, lambda_q1, lambda_k1, lambda_q2, lambda_k2, subln_g, w_branch_diff,
        w_branch_moba, w_out, w_ple, w_ple_gate, final_g,
    )
    return second_block(
        x, c_2, ln_mix_g_2, ln_ffn_g_2, w_mod_2, b_mod_2, w_in_2, cmp_pe_k_2, cmp_pe_v_2,
        cmp_wk1_2, cmp_wk2_2, cmp_wv1_2, cmp_wv2_2, conv_w_2, norm_attn_g_2, norm_conv_g_2,
        w_out_2, peer_wq_2, peer_keys_2, peer_u_2, peer_v_2, rel_table_2, ln_final_g_2,
    )


_drawn_inputs = setup_inputs


def setup_inputs(seed=0):
    import zlib

    import numpy as np

    out = dict(_drawn_inputs(seed))
    spreads = {}
    factors = {'norm_g': 4.678,
     'lambda_k1': 6.171,
     'lambda_q2': 6.301,
     'lambda_k2': 2.765,
     'subln_g': 8.0,
     'ln_ffn_g_2': 4.019,
     'cmp_pe_k_2': 8.0,
     'cmp_pe_v_2': 3.416,
     'norm_attn_g_2': 4.507,
     'norm_conv_g_2': 4.831}
    for name, (base, spread) in spreads.items():
        noise = np.random.default_rng([zlib.crc32(name.encode()), seed]).standard_normal(out[name].shape)
        drawn = base * np.exp(spread * noise) if base else spread * noise
        out[name] = __import__('jax').numpy.asarray(drawn.astype(out[name].dtype))
    for name, factor in factors.items():
        out[name] = (out[name] * factor).astype(out[name].dtype)
    return out
```

```python
from contextlib import ExitStack

import numpy as np

import concourse.bass as bass
from concourse import mybir

F32 = mybir.dt.float32
F32R = mybir.dt.float32r
U32 = mybir.dt.uint32
ALU = mybir.AluOpType
ACT = mybir.ActivationFunctionType
AX = mybir.AxisListType.X

P = 128
T = 256
TT = T // P
D = 1024
KC = D // P
DH = 64
HEADS = 8
HALF = HEADS // 2
NKEYS = 128
TOPK = 16
NEG = -1e30
LOWEST = -3.0e38
LAM_INIT = 0.8 - 0.6 * float(np.exp(-0.3 * 0))
EPS, SUBLN_EPS = 1e-6, 1e-5
SCALE = DH ** -0.5
UBANKS = (0, 1, 6, 7)
SOFT_TILE, SEL_TILE = 88, 96
TILE_STEPS = 12
SOFT_STEP = 2 * TILE_STEPS + 2
TOPK_STEPS = SOFT_STEP + 3
CMP_N, CMP_PAD = (T - 32) // 16 + 1, 32
RING = 4
HSLOT = D // 2
TRI = P + T

FILL1 = [f"{n}{b}" for n, k in (("dg", 4), ("mg", 4), ("ga", 8), ("gb", 8)) for b in range(k)]
FILL2 = [f"{n}{b}" for n in ("cb", "cc", "ch") for b in range(4)]
FIRST1 = [f"{n}{b}" for n in ("dq", "dk") for b in range(4)] + ["dv"] \
    + [f"{n}{b}" for n in ("mq", "mk") for b in range(4)] + ["mv"]
FIRST2 = [f"nq{b}" for b in range(4)] + ["kc", "vc", "ks", "kw", "nv", "gt"]
SLOTS_OF = {"dv": 4, "mv": 4, "nv": 2}
ROWS = {"dv": (4, 512, T), "mv": (4, 512, T), "nv": (2, T, T), "gt": (2, P, 24)}


def plan():
    steps = [("norm", 0), ("small",)]
    fill, mod = list(FILL1), list(range(24))
    for n in FIRST1:
        steps += [("proj", n)]
        if n[0] == "m" and n != "mv":
            steps.append(("mod", mod.pop(0)))
    steps += [("scores", 0), ("scores", 1)]
    for p in range(8):
        steps.append(("soft", p))
        steps += [("proj", fill.pop(0)) for _ in range(2)] + [("mod", mod.pop(0)) for _ in range(2)]
        steps.append(("turn", p))
        if p + 2 < 8:
            steps.append(("scores", p + 2))
        steps += [("proj", fill.pop(0))]
        steps.append(("pv", p))
        if p >= 4:
            steps.append(("subln", p - 4))
    steps += [("ple",), ("merge",), ("out1",), ("gate",)]
    steps += [("norm", 1), ("norm", 2)]
    steps += [("proj", n) for n in FIRST2]
    steps += [("scores", 8), ("scores", 9), ("cmpk",), ("cmpv",), ("cmps",)]
    fill = list(FILL2)
    for p in range(8, 16):
        steps += [("soft", p), ("proj", fill.pop(0))]
        if p == 8:
            steps.append(("cmpt",))
        steps.append(("turn", p))
        if p + 2 < 16:
            steps.append(("scores", p + 2))
        if p % 2 == 1 or p == 8:
            steps += [("proj", fill.pop(0))] if fill else []
        if p % 2 == 1:
            steps.append(("pv", p))
        if p == 15:
            steps += [("proj", n) for n in fill]
            fill = []
    steps += [("conv",), ("mixnorm",), ("out2",), ("norm", 3), ("wq",), ("route",)]
    assert not mod and not fill
    order = []
    for s in steps:
        k = {"proj": SLOTS_OF.get(s[-1], 1), "ple": 2, "merge": 8, "out1": 8, "gate": 8,
             "cmpk": 1, "cmpv": 1, "out2": 8, "wq": 8}.get(s[0], 0)
        order += [(s, i) for i in range(k)]
    return steps, order


STEPS, SLOTS = plan()
NSLOT = len(SLOTS)
SLOT_AT = {}
for _n, (_s, _i) in enumerate(SLOTS):
    SLOT_AT.setdefault(_s, _n)
SPLIT = {_n: _k for _k, _n in enumerate(n for n, (s, _) in enumerate(SLOTS) if s[0] in ("proj", "wq"))}
NSPLIT = len(SPLIT)
SLOT_OF_SPLIT = {_k: _n for _n, _k in SPLIT.items()}
POOL_TILES = P // 2

PAR = {}
_at = 0
for _name, _w in (("norm_g", 8), ("final_g", 8), ("ln_mix_g", 8), ("ln_ffn_g", 8), ("ln_final_g", 8),
                  ("attn_g", 4), ("conv_g", 4), ("subln_g", 1), ("conv_w", 12), ("b_mod", 48),
                  ("lam", 256), ("rel", 8)):
    PAR[_name] = (_at, _at + _w)
    _at += _w
NPAR = _at
CST = {}
_at = 0
for _name, _w in (("ident", P), ("perm", P), ("cos", T), ("sin", T), ("mask", TRI), ("iota", P),
                  ("valid", TT), ("rev", TRI), ("fwd", 512)):
    CST[_name] = (_at, _at + _w)
    _at += _w
NCST = _at


def block_program(nc, x_t, p_t, params, consts, weights, c_rows, mods, w2k, w2v, pe, keys, u_t, v_rows, bias_dram, out_t):
    with ExitStack() as ctx:
        def sb(name, shape, dt=F32):
            return ctx.enter_context(nc.sbuf_tensor(name, shape, dt))

        def sem(name):
            return ctx.enter_context(nc.semaphore(name))

        psum = ctx.enter_context(nc.psum_tensor("psum", [P, 8, 512], F32))
        arena = sb("arena", [P, P, T])
        ring = sb("ring", [P, RING, D])
        xres = sb("xres", [P, KC, T])
        w_hi = sb("w_hi", [P, 4, HSLOT], F32R)
        w_lo = sb("w_lo", [P, 4, HSLOT], F32R)
        h_hi = sb("h_hi", [P, KC, T], F32R)
        h_lo = sb("h_lo", [P, KC, T], F32R)
        s_sb = sb("s_sb", [P, TT * 2 * HEADS * NKEYS])
        par = sb("par", [P, NPAR])
        ident = sb("ident", [P, P])
        iota = sb("iota", [P, P])
        ones = sb("ones", [P, P])
        valid = sb("valid", [P, TT])
        mod = sb("mod", [P, 48])
        gm = sb("gm", [P, 2, KC])
        std = sb("std", [P, T])
        rstd = sb("rstd", [P, T])
        small = sb("small", [P, 64])
        nmax = sb("nmax", [P, 2, 4])
        sums = sb("sums", [P, 2, 4])
        rsum = sb("rsum", [P, 2, 4])
        gsig = sb("gsig", [P, TT, 24])
        cst1 = sb("cst1", [P, 3, 16])
        top_v = sb("top_v", [P, 2, HEADS, TOPK])
        gsum = sb("gsum", [P, 3, TT * HEADS])
        eps_c = sb("eps_c", [P, 2])

        def pcol(name, a=0, n=1):
            return par[:, PAR[name][0] + a:PAR[name][0] + a + n]

        def blk(a, n=1):
            return arena[:, a, :] if n == 1 else arena[:, a:a + n, :]

        def flat(a, n):
            return arena[:, a:a + n, :].rearrange("p a b -> p (a b)")

        QK, RAW, DV, MV, SIL, SIG, OT = 0, 16, 32, 36, 40, 48, 64
        SC, PT, EX, SQ, MERGED, PLE, PTOK, TAB, MSK, REL = 72, 78, 88, 94, 102, 110, 118, 120, 122, 124
        SHEET, NQ, KS, KW, KCW, VCW, NV, CONV = 0, 16, 20, 21, 22, 25, 28, 30
        CSC, CPT, CBIAS, BD, H1, PROD = 42, 44, 46, 48, 50, 52
        QP = 112
        MODR, CACT = (MERGED, PT), REL
        OUT = 0
        NTMP = SQ
        top_f = blk(104).rearrange("p (m h k) -> p m h k", m=2, h=HEADS)
        top_i = blk(105).bitcast(U32).rearrange("p (m h k) -> p m h k", m=2, h=HEADS)
        best_v = blk(106).rearrange("p (i h k) -> p i h k", i=TT, h=HEADS)
        best_p = blk(107).bitcast(U32).rearrange("p (m h k) -> p m h k", m=2, h=HEADS)
        best_f = blk(108).rearrange("p (m h k) -> p m h k", m=2, h=HEADS)
        best_i = blk(109)[:, 0:P].bitcast(U32).rearrange("p (h k) -> p h k", h=HEADS)
        sel = flat(100, 3).rearrange("p (i k j) -> p i k j", i=TT, k=3)
        cos_t, sin_t = blk(TAB), blk(TAB + 1)
        mask = flat(MSK, 2)[:, 0:TRI]
        rel_c = flat(REL, 4)[:, 0:TRI + 512]
        perm = flat(MSK, 2)[:, TRI:TRI + P]
        sheet = flat(SHEET, 8).rearrange("p (h j) -> p h j", h=HEADS)
        cbias = flat(CBIAS, 2).rearrange("p (i h n) -> p i h n", i=TT, h=HEADS)
        csc = flat(CSC, 2).rearrange("p (i g c) -> p i g c", i=TT, g=2)
        cpt = flat(CPT, 2).rearrange("p (g q) -> p g q", g=2)
        bd = flat(BD, 2).rearrange("p (g r d) -> p g r d", g=2, r=4)
        h1 = blk(H1)[0:DH, :].rearrange("p (w g n) -> p w g n", w=2, g=2)[:, :, :, 0:CMP_PAD]
        kct = blk(H1 + 1)[:, 0:CMP_PAD]
        pebias = blk(H1 + 1)[0:DH, 40:42]
        w2s = blk(H1 + 1)[0:DH, 64:192].rearrange("p (w d) -> p w d", w=2)
        junk = s_sb[:, 0:D]
        c_raw = s_sb[:, 2560:2560 + D]

        def sc_of(p):
            return flat(SC + 3 * (p % 2), 3).rearrange("p (m c) -> p m c", m=2)

        def ex_of(p):
            return flat(EX + 3 * (p % 2), 3).rearrange("p (m c) -> p m c", m=2)

        def pt_of(p):
            return flat(PT + 3 * (p % 3), 3).rearrange("p (m c) -> p m c", m=2)

        bias_rows = flat(SC, 12).rearrange("p (h j) -> p h j", h=HEADS)

        def scores_of(i):
            n = 2 * HEADS * NKEYS
            return s_sb[:, n * i:n * i + n].rearrange("p (m h k) -> p m h k", m=2, h=HEADS)

        def cmp_of(k):
            return flat(P - 16 + 8 * k, 8).rearrange("p (h k a) -> p h k a", h=HEADS, k=TOPK)

        ring_keys = flat(120, 4).rearrange("p (h k) -> p h k", h=HEADS)
        hot1 = s_sb[:, 0:1024].rearrange("p (t k) -> p t k", t=8)
        hot2 = s_sb[:, 1024:2048].rearrange("p (t k) -> p t k", t=8)

        sel_t = s_sb[:, 2048:2048 + 3 * T].rearrange("p (k t) -> p k t", k=3)

        def win_of(which):
            return arena[:, (KCW, VCW)[which]:(KCW, VCW)[which] + 3, :]

        def abuf(n):
            return psum[:, n % 2, 0:T]

        def vbuf(n):
            return psum[:, 2 + n % 4, 0:T]

        def scb(p):
            return psum[:, 2 + 2 * (p % 2):4 + 2 * (p % 2), 0:TRI]

        turned = psum[:, 6:8, 0:TRI]

        x_in = sem("x_in")
        small_in = sem("small_in")
        sheet_in = sem("sheet_in")
        cmp_in = sem("cmp_in")
        peer_in = sem("peer_in")
        slot_in = [sem(f"slot_in{i}") for i in range(RING)]
        const_set = sem("const_set")
        zero_set = sem("zero_set")
        cact_ready = sem("cact_ready")
        lam_step = sem("lam_step")
        rel_done = sem("rel_done")
        rel_read = sem("rel_read")
        a_done = sem("a_done")
        a_read = sem("a_read")
        v_done = sem("v_done")
        v_read = sem("v_read")
        mod_in = [sem(f"mod_in{i}") for i in range(2)]
        mod_done = sem("mod_done")
        mod_ready = sem("mod_ready")
        hi_done = sem("hi_done")
        lo0_done = sem("lo0_done")
        lo1_done = sem("lo1_done")
        lo2_done = sem("lo2_done")
        half_used = sem("half_used")
        t_ready = sem("t_ready")
        th_done = sem("th_done")
        x1_ready = sem("x1_ready")
        squared = sem("squared")
        rstd_ready = sem("rstd_ready")
        h_ready = sem("h_ready")
        cos_done = sem("cos_done")
        sin_done = sem("sin_done")
        rope_done = sem("rope_done")
        scores_done = sem("scores_done")
        masked_done = sem("masked_done")
        max_done = sem("max_done")
        exp_done = sem("exp_done")
        inv_done = sem("inv_done")
        lam_scaled = sem("lam_scaled")
        map0_done = sem("map0_done")
        gated_done = sem("gated_done")
        shift_in = sem("shift_in")
        probs_done = sem("probs_done")
        turn_done = sem("turn_done")
        pt_done = sem("pt_done")
        gates_ready = sem("gates_ready")
        osq_done = sem("osq_done")
        sub_done = sem("sub_done")
        o_ready = sem("o_ready")
        x_ready = sem("x_ready")
        merged_ready = sem("merged_ready")
        ple_step = sem("ple_step")
        cmp_step = sem("cmp_step")
        cmp_bias = sem("cmp_bias")
        cmp_exp = sem("cmp_exp")
        cmp_vec = sem("cmp_vec")
        z_done = sem("z_done")
        conv_step = sem("conv_step")
        conv_done = sem("conv_done")
        key_done = sem("key_done")
        key_read = sem("key_read")
        topk_step = sem("topk_step")
        picked = sem("picked")
        soft_exp = sem("soft_exp")
        act_done = sem("act_done")
        act_read = sem("act_read")
        sel_done = sem("sel_done")
        hot_ready = sem("hot_ready")
        route_done = sem("route_done")
        routed = sem("routed")
        act_hi = sem("act_hi")
        act_lo = sem("act_lo")
        y_done = sem("y_done")
        fin_step = sem("fin_step")
        out_ready = sem("out_ready")
        stored = sem("stored")

        a_order, v_order = [], []
        for s in STEPS:
            k = s[0]
            if k == "norm":
                a_order += [s + ("ssq",)]
            elif k == "proj" and s[1] in ("dv", "mv"):
                v_order += [s + (j,) for j in range(4)]
            elif k == "proj" and s[1] in ROWS:
                a_order += [s + (j,) for j in range(TT)]
            elif k == "proj":
                a_order += [s]
                if s[1] in FIRST1:
                    v_order += [("rope", s[1])]
            elif k in ("pv", "subln"):
                a_order += [s]
            elif k in ("ple", "gate", "wq"):
                a_order += [s + (j,) for j in range(KC)]
            elif k in ("cmpk", "cmpv"):
                a_order += [s + (0,), s + (1,)]
            elif k == "mixnorm":
                a_order += [s + (0,), s + (1,)]
            if k == "merge":
                v_order += [s + (j,) for j in range(2 * KC)]
            if k in ("out1", "out2"):
                v_order += [s + (j,) for j in range(KC)]
        a_order.append(("norm", 4, "ssq"))
        AT = {s: n for n, s in enumerate(a_order)}
        rope_blocks = [n for n in FIRST1 if n[1] in "qk" and n[0] in "dm"]
        VT = {s: n for n, s in enumerate(v_order)}
        NA, NVB = len(a_order), len(v_order)
        NORM_BASE = {0: 0, 1: 8, 2: 16, 3: 24, 4: 32}

        def filled(*s):
            return AT[s] + 1

        def slot_of(n):
            return n % RING, 16 * (n // RING + 1)

        def slot_count(n, more):
            return 16 * (n // RING + 1) + (16 // RING) * more

        def freer(n):
            s, i = SLOTS[n]
            k = s[0]
            if k == "ple":
                return a_done, filled(*s, 4 * i + 3)
            if k == "gate":
                return a_done, filled(*s, i)
            if k in ("cmpk", "cmpv"):
                return a_done, filled(*s, 0)
            if k == "merge":
                return v_done, VT[("merge", 4 * (i // 2) + 2 + i % 2)] + 1
            return v_done, VT[s + (i,)] + 1

        half_free = {}
        n_half = 0
        for k in range(NSPLIT):
            s, i = SLOTS[SLOT_OF_SPLIT[k]]
            last = i == SLOTS_OF.get(s[-1], 1) - 1 or s[0] == "wq"
            n_half += 1
            half_free[k, 0] = half_used, n_half
            if not last:
                n_half += 1
                half_free[k, 1] = half_used, n_half
            elif s[0] == "wq":
                half_free[k, 1] = a_done, filled(*s, i)
            elif s[1] in ("dv", "mv"):
                half_free[k, 1] = v_done, VT[s + (3,)] + 1
            elif s[1] in ROWS:
                half_free[k, 1] = a_done, filled(*s, TT - 1)
            else:
                half_free[k, 1] = a_done, filled(*s)
        NHALF = n_half

        first_wq = SPLIT[SLOT_AT[("wq",)]]
        first_2 = SPLIT[SLOT_AT[("proj", "nq0")]]

        def ahead(s):
            if s[0] == "norm" and s[1] != 1:
                return {0: 1, 2: first_2 + 1, 3: first_wq + 1}[s[1]]
            if s[0] == "proj":
                k = SPLIT[SLOT_AT[s]] + SLOTS_OF.get(s[1], 1)
                return min(k, first_2 - 1) if k - SLOTS_OF.get(s[1], 1) < first_2 else min(k, first_wq - 1)
            if s[0] == "wq":
                return NSPLIT - 1
            return -1

        block = ctx.enter_context(nc.Block())

        @block.sync
        def _(sp):
            def load_slot(n):
                if n >= RING:
                    if n - RING in SPLIT:
                        k = SPLIT[n - RING]
                        sp.wait_ge(lo0_done, k + 1)
                        sp.wait_ge(lo1_done, k + 1)
                    else:
                        who, value = freer(n - RING)
                        sp.wait_ge(who, value)
                sp.dma_start(ring[:, n % RING, :], weights[n]).then_inc(slot_in[n % RING], 16)

            sp.dma_start(xres[:, :, :], x_t).then_inc(x_in, 16)
            sp.dma_start(par[:, :], params).then_inc(x_in, 16)
            load_slot(0)
            for name, dst in (("ident", ident[:, :]), ("iota", iota[:, :]), ("valid", valid[:, :]),
                              ("cos", cos_t), ("sin", sin_t), ("mask", mask), ("perm", perm)):
                sp.dma_start(dst, consts[:, CST[name][0]:CST[name][1]]).then_inc(small_in, 16)
            sp.dma_start(rel_c[0:33, :], consts[0:33, CST["rev"][0]:CST["fwd"][1]]).then_inc(small_in, 16)
            sp.dma_start(blk(PTOK, 2), p_t).then_inc(small_in, 16)
            sp.dma_start(c_raw, c_rows).then_inc(small_in, 16)
            for n in range(1, RING):
                load_slot(n)
            sp.wait_ge(rel_read, 2)
            sp.dma_start(bias_dram, bias_rows).then_inc(sheet_in, 16)
            first2 = SLOT_AT[("proj", "nq0")]
            for n in range(RING, NSLOT):
                if n == first2:
                    sp.wait_ge(sheet_in, 16)
                    sp.wait_ge(turn_done, 8)
                    sp.wait_ge(a_done, filled("pv", 7))
                    sp.wait_ge(gates_ready, 3)
                    skew = bass.AP(bias_dram.tensor, bias_dram.offset + P - 1,
                                   [[HEADS * TRI - 1, P], [TRI, HEADS], [1, T]])
                    sp.dma_start(sheet, skew).then_inc(sheet_in, 16)
                    sp.wait_ge(x_ready, KC)
                    sp.dma_start(w2s[:, 0, :], w2k).then_inc(cmp_in, 16)
                    sp.dma_start(w2s[:, 1, :], w2v).then_inc(cmp_in, 16)
                    for w in range(2):
                        sp.dma_start(win_of(w)[:, 2, :], pe[w]).then_inc(cmp_in, 16)
                load_slot(n)

            def load_tile(src, base, s, n, waits):
                for who, value in waits:
                    sp.wait_ge(who, value)
                sp.dma_start(ring[:, (base + s) % RING, :], src[n]).then_inc(slot_in[(base + s) % RING], 16)

            for s in range(RING):
                k = NSPLIT - RING + s
                load_tile(u_t, NSLOT, s, s, ((lo0_done, k + 1), (lo1_done, k + 1)))
            with sp.Fori(1, POOL_TILES // RING + 1) as it:
                for s in range(RING):
                    n = it * RING + s
                    load_tile(u_t, NSLOT, s, n, ((lo1_done, NSPLIT + n - RING + 1),))
            with sp.Fori(POOL_TILES // RING + 1, P // RING) as it:
                for s in range(RING):
                    n = it * RING + s
                    load_tile(u_t, NSLOT, s, n, ((lo1_done, NSPLIT + n - RING + 1),))
            with sp.Fori(0, P // RING) as it:
                for s in range(RING):
                    n = it * RING + s
                    load_tile(v_rows, NSLOT + P, s, n, ((lo1_done, NSPLIT + P + n - RING + 1),))
            for c in range(KC):
                sp.wait_ge(out_ready, c + 1)
                sp.dma_start(out_t[c], blk(OUT + c)).then_inc(stored, 16)
            sp.wait_ge(stored, 16 * KC)

        @block.tensor
        def _(pe_):
            def slot_ready(n):
                i, value = slot_of(n)
                pe_.wait_ge(slot_in[i], value)
                return ring[:, i, :]

            def take_a(n):
                if n >= 2:
                    pe_.wait_ge(a_read, n - 1)
                return abuf(n)

            def take_v(n):
                if n >= 4:
                    pe_.wait_ge(v_read, n - 3)
                return vbuf(n)

            def mm(out, lhs, rhs, start, stop, **kw):
                return nc.tensor.matmul(out, lhs, rhs, start=start, stop=stop, **kw)

            def sum_squares(n, sq, chunks, ready):
                out = take_a(n)
                for c in range(chunks):
                    ready(c)
                    last = mm(out, ones[:, :], sq[:, c, :], c == 0, c == chunks - 1)
                last.then_inc(a_done, 1)

            def projection(n, slot, chunks, width, rhs, ready, take, done):
                w = slot_ready(slot)
                out = take(n)
                for c in range(chunks):
                    ready(c)
                    last = mm(out, w[:, width + c * P:width + c * P + P], rhs[:, c, :], c == 0, c == chunks - 1)
                last.then_inc(done, 1)

            def split_mms(out, half, at, rhs, first, last):
                w1, w0 = w_hi[:, half, at:at + P], w_lo[:, half, at:at + P]
                mm(out, w1, rhs[0], first, False)
                mm(out, w1, rhs[1], False, False)
                return mm(out, w0, rhs[0], False, last)

            def half_ready(k, b, low=None):
                pe_.wait_ge(hi_done, 2 * k + b + 1)
                who, value = low or ((lo0_done, lo1_done)[b], k + 1)
                pe_.wait_ge(who, value)
                return (2 * k + b) % 4

            def split_projection(n, k, ready):
                out = take_a(n)
                for b in range(2):
                    half = half_ready(k, b)
                    for c4 in range(4):
                        c = 4 * b + c4
                        ready(c)
                        last = split_mms(out, half, c4 * P, (h_hi[:, c, :], h_lo[:, c, :]), c == 0, c == KC - 1)
                    last.then_inc(a_done if b else half_used, 1)

            def rope_turn(b):
                pe_.wait_ge(a_read, filled("proj", rope_blocks[b]))
                out = take_v(VT[("rope", rope_blocks[b])])
                mm(out, perm, blk(RAW + b), True, True).then_inc(v_done, 1)

            pending = []
            for s in STEPS:
                kind = s[0]
                if kind == "small":
                    pe_.wait_ge(small_in, 16 * 10)
                    pe_.wait_ge(a_read, 1)
                    rel = par[0:33, PAR["rel"][0]:PAR["rel"][1]]
                    for hd in range(HEADS):
                        lhs = rel[:, hd:hd + 1].to_broadcast([33, P])
                        last = mm(psum[:, hd, 0:TRI], lhs, rel_c[0:33, 0:TRI], True, True)
                        if hd in (1, HEADS - 1):
                            last.then_inc(rel_done, 1)
                    pe_.wait_ge(rel_read, 2)
                    for i in range(TT):
                        for n in range(CMP_N):
                            at = TRI + P * i - 16 * n - 31 + 272
                            last = mm(psum[:, 7, (i * CMP_N + n) * HEADS:(i * CMP_N + n + 1) * HEADS],
                                      rel_c[0:33, at:at + P], rel, True, True)
                    last.then_inc(rel_done, 1)
                elif kind == "norm":
                    k = s[1]
                    pe_.wait_ge(const_set, 1)
                    sum_squares(AT[s + ("ssq",)], blk(SQ, 8), KC,
                                lambda c, k=k: pe_.wait_ge(squared, NORM_BASE[k] + c + 1))
                elif kind == "proj" and s[1] in ROWS:
                    while pending:
                        rope_turn(pending.pop(0))
                    jobs, width, cols = ROWS[s[1]]
                    k0, slots = SPLIT[SLOT_AT[s]], SLOTS_OF.get(s[1], 1)
                    take, at, done = (take_v, VT, v_done) if jobs == 4 else (take_a, AT, a_done)
                    pe_.wait_ge(h_ready, 8 if jobs == 4 else 16)
                    out = [take(at[s + (j,)]) for j in range(jobs)]
                    each = HSLOT // width
                    for x in range(2 * slots):
                        half = half_ready(k0 + x // 2, x % 2)
                        for j in range(jobs):
                            i, col = (j // 2, (j % 2) * T) if jobs == 4 else (j, 0)
                            for y in range(each):
                                c = x * each + y
                                t = slice(P * i, P * i + P)
                                w = slice(y * width + col, y * width + col + cols)
                                o, end = out[j][:, 0:cols], c == KC - 1
                                mm(o, h_hi[:, c, t], w_hi[:, half, w], c == 0, False)
                                mm(o, h_lo[:, c, t], w_hi[:, half, w], False, False)
                                last = mm(o, h_hi[:, c, t], w_lo[:, half, w], False, end)
                            if x == 2 * slots - 1:
                                last.then_inc(done, 1)
                        if x < 2 * slots - 1:
                            last.then_inc(half_used, 1)
                elif kind == "proj":
                    base = 0 if s[1] in FIRST1 + FILL1 else 8
                    split_projection(AT[s], SPLIT[SLOT_AT[s]], lambda c, base=base: pe_.wait_ge(h_ready, base + c + 1))
                    if s[1] in rope_blocks:
                        pending.append(rope_blocks.index(s[1]))
                        if len(pending) > 1:
                            rope_turn(pending.pop(0))
                elif kind == "scores":
                    p = s[1]
                    while pending:
                        rope_turn(pending.pop(0))
                    if p < 8:
                        pe_.wait_ge(rope_done, 16)
                        pe_.wait_ge(v_read, VT[("proj", "mv", 3)] + 1)
                        base = QK if p < 4 else QK + 8
                        b = p % 4
                        q, k = blk(base + b), blk(base + 4 + b)
                    else:
                        pe_.wait_ge(a_read, filled("proj", "kw"))
                        pe_.wait_ge(v_read, VT[("out1", 7)] + 1)
                        q, k = blk(NQ + (p - 8) // 2), blk(KS if p % 2 == 0 else KW)
                    if p >= 2:
                        pe_.wait_ge(masked_done, p - 1)
                    out = scb(p)
                    for m in range(2):
                        r = slice(DH * m, DH * m + DH)
                        mm(out[:, m, 0:P], q[r, 0:P], k[r, 0:P], True, True)
                        last = mm(out[:, m, P:TRI], q[r, P:T], k[r, :], True, True)
                    last.then_inc(scores_done, 1)
                elif kind == "turn":
                    p = s[1]
                    pe_.wait_ge(probs_done, p + 1)
                    if p:
                        pe_.wait_ge(pt_done, p if p < 8 else p + 1)
                    if p == 0:
                        pe_.wait_ge(rel_read, 3)
                    for m in range(1 if p < 4 else 2):
                        for c in range(3):
                            last = nc.tensor.transpose(turned[:, m, c * P:c * P + P],
                                                       ex_of(p)[:, m, c * P:c * P + P], ident[:, :])
                    last.then_inc(turn_done, 1)
                elif kind == "pv":
                    p = s[1]
                    pe_.wait_ge(pt_done, p + 1 if p < 8 else p + 2)
                    if p < 8:
                        pe_.wait_ge(v_read, VT[("proj", "dv" if p < 4 else "mv", 3)] + 1)
                    out = take_a(AT[s])
                    pt = pt_of(p)
                    if p < 4:
                        v = flat(DV, 4).rearrange("p (i n) -> p i n", i=TT)
                        mm(out, v[:, 0, P * p:P * p + P], pt[:, 0, 0:T], True, False)
                        last = mm(out[:, P:T], v[:, 1, P * p:P * p + P], pt[:, 0, T:TRI], False, True)
                    elif p < 8:
                        v = flat(MV, 4).rearrange("p (i n) -> p i n", i=TT)
                        for m in range(2):
                            o, at = out[DH * m:DH * m + DH, :], P * (p - 4) + DH * m
                            mm(o, v[:, 0, at:at + DH], pt[:, m, 0:T], True, False)
                            last = mm(o[:, P:T], v[:, 1, at:at + DH], pt[:, m, T:TRI], False, True)
                    else:
                        pe_.wait_ge(a_read, filled("proj", "nv", TT - 1))
                        v = flat(NV, 2).rearrange("p (i n) -> p i n", i=TT)
                        for m in range(2):
                            o = out[DH * m:DH * m + DH, :]
                            mm(o, bd[:, m, (p - 8) // 2, :], cpt[:, m, :], True, False)
                            for w, pp in ((0, pt_of(p - 1)), (1, pt)):
                                at = P * w + DH * m
                                mm(o, v[:, 0, at:at + DH], pp[:, m, 0:T], False, False)
                                last = mm(o[:, P:T], v[:, 1, at:at + DH], pp[:, m, T:TRI], False, w == 1)
                    last.then_inc(a_done, 1)
                elif kind == "subln":
                    pe_.wait_ge(osq_done, s[1] + 1)
                    out = take_a(AT[s])
                    mm(out, ones[:, :], blk(SQ + s[1]), True, True).then_inc(a_done, 1)
                elif kind == "ple":
                    for j in range(KC):
                        projection(AT[s + (j,)], SLOT_AT[s] + j // 4, 2, (j % 4) * T, blk(PTOK, 2), lambda c: None,
                                   take_a, a_done)
                elif kind == "merge":
                    pe_.wait_ge(masked_done, 8)
                    for nb in range(KC):
                        for ab in range(2):
                            slot = SLOT_AT[s] + 2 * (nb // 2) + ab
                            projection(VT[s + (2 * nb + ab,)], slot, 4, (nb % 2) * 512, blk(OT + 4 * ab, 4),
                                       lambda c, ab=ab: pe_.wait_ge(o_ready, 4) if ab else pe_.wait_ge(sub_done, 12),
                                       take_v, v_done)
                elif kind == "out1":
                    for nb in range(KC):
                        projection(VT[s + (nb,)], SLOT_AT[s] + nb, KC, 0, blk(MERGED, 8),
                                   lambda c: pe_.wait_ge(merged_ready, c + 1), take_v, v_done)
                elif kind == "gate":
                    for nb in range(KC):
                        projection(AT[s + (nb,)], SLOT_AT[s] + nb, KC, 0, xres[:, :, :],
                                   lambda c: pe_.wait_ge(v_read, VT[("out1", c)] + 1), take_a, a_done)
                elif kind in ("cmpk", "cmpv"):
                    which = 0 if kind == "cmpk" else 1
                    w1 = slot_ready(SLOT_AT[s])
                    pe_.wait_ge(a_read, filled("proj", ("kc", "vc")[which]))
                    pe_.wait_ge(cmp_in, 16 * 4)
                    win = win_of(which)
                    out = take_a(AT[s + (0,)])
                    for l2 in range(16):
                        last = mm(out[0:DH, 0:3 * CMP_N], w1[:, l2 * DH:l2 * DH + DH],
                                  win[:, :, 2 * l2:2 * l2 + 16 * (CMP_N - 1) + 1:16], l2 == 0, l2 == 15)
                    last.then_inc(a_done, 1)
                    pe_.wait_ge(a_read, filled(*s, 0))
                    out = take_a(AT[s + (1,)])
                    if which == 0:
                        for g in range(2):
                            last = mm(out[DH * g:DH * g + DH, 0:CMP_PAD], w2s[:, 0, :], h1[:, 0, g, :], True, True)
                    else:
                        for r in range(4):
                            for g in range(2):
                                last = mm(out[32 * r:32 * r + 32, DH * g:DH * g + DH], h1[:, 1, g, :], w2s[:, 1, :],
                                          True, True)
                    last.then_inc(a_done, 1)
                elif kind == "cmps":
                    pe_.wait_ge(a_read, filled("cmpk", 1))
                    pe_.wait_ge(pt_done, 8)
                    for g in range(2):
                        for i in range(TT):
                            for r in range(4):
                                at = (i * 4 + r) * CMP_PAD
                                last = mm(psum[:, 6 + g, at:at + CMP_PAD], blk(NQ + r)[DH * g:DH * g + DH, P * i:P * i + P],
                                          kct[DH * g:DH * g + DH, :], True, True)
                    last.then_inc(cmp_step, 1)
                elif kind == "cmpt":
                    pe_.wait_ge(cmp_vec, 8)
                    for g in range(2):
                        for i in range(TT):
                            last = nc.tensor.transpose(turned[:, g, P * i:P * i + P], csc[:, i, g, :], ident[:, :])
                    last.then_inc(cmp_step, 1)
                elif kind == "mixnorm":
                    for j in range(2):
                        sum_squares(AT[s + (j,)], blk(SQ + 4 * j, 4), 4,
                                    lambda c, j=j: pe_.wait_ge(osq_done, 4 + 4 * j + c + 1))
                elif kind == "out2":
                    for nb in range(KC):
                        projection(VT[s + (nb,)], SLOT_AT[s] + nb, KC, 0, blk(OT, 8),
                                   lambda c: pe_.wait_ge(o_ready, 4 + c + 1), take_v, v_done)
                elif kind == "wq":
                    for nb in range(KC):
                        split_projection(AT[s + (nb,)], SPLIT[SLOT_AT[s]] + nb,
                                         lambda c: pe_.wait_ge(h_ready, 16 + c + 1))
                elif kind == "route":
                    pe_.wait_ge(peer_in, 16)
                    pe_.wait_ge(v_read, NVB)
                    for x in range(4):
                        i, first = x // 2, 4 * (x % 2)
                        if x >= 2:
                            pe_.wait_ge(key_read, x - 1)
                        for m in range(2):
                            for j in range(4):
                                hd = first + j
                                pe_.wait_ge(a_read, filled("wq", hd))
                                last = mm(psum[:, 2 + 2 * (x % 2) + m, j * P:j * P + P],
                                          blk(QP + hd)[DH * m:DH * m + DH, P * i:P * i + P],
                                          ring_keys[DH * m:DH * m + DH, hd, :], True, True)
                        last.then_inc(key_done, 1)

            def u_tile(s, n, first, by_pool):
                k = NSPLIT + s
                if not first:
                    pe_.wait_ge(act_read, n - 3)
                out = psum[:, UBANKS[s % 4], 0:T]
                for b in range(2):
                    pe_.wait_ge(hi_done, 2 * (NSPLIT + n) + b + 1)
                    if b:
                        pe_.wait_ge(lo1_done, NSPLIT + n + 1)
                    elif by_pool:
                        pe_.wait_ge(lo2_done, n + 1)
                    else:
                        pe_.wait_ge(lo0_done, NSPLIT + n - POOL_TILES + 1)
                    for c4 in range(4):
                        c = 4 * b + c4
                        last = split_mms(out, (2 * k + b) % 4, c4 * P, (h_hi[:, c, :], h_lo[:, c, :]), c == 0, c == KC - 1)
                    last.then_inc(act_done if b else half_used, 1)

            def u_tiles(a, b):
                with pe_.Fori(a // 4, b // 4) as it:
                    for s in range(4):
                        u_tile(s, it * 4 + s, False, b <= POOL_TILES)

            pe_.wait_ge(a_read, NA - 1)
            for s in range(4):
                u_tile(s, s, True, True)
            u_tiles(4, POOL_TILES)
            u_tiles(POOL_TILES, SEL_TILE)

            pe_.wait_ge(topk_step, TOPK_STEPS)
            for k in range(3):
                for i in range(TT):
                    last = nc.tensor.transpose(psum[:, 4 + k // 2, ((k % 2) * TT + i) * P:((k % 2) * TT + i + 1) * P],
                                               sel[:, i, k, :], ident[:, :])
            last.then_inc(sel_done, 1)

            def route_four(half, n, first):
                pe_.wait_ge(hot_ready, n * 2 + half + 1)
                if not (first):
                    pe_.wait_ge(routed, n * 2 + half - 1)
                for j in range(4):
                    k = 4 * half + j
                    last = mm(psum[:, 2 + half, j * P:j * P + P], hot1[:, k, :], hot2[:, k, :], True, True)
                last.then_inc(route_done, 1)

            u_tiles(SEL_TILE, P)
            route_four(0, 0, True)
            route_four(1, 0, True)
            with pe_.Fori(1, T // 8) as it:
                for half in range(2):
                    route_four(half, it, False)

            def v_tile(s, n, first, final):
                k = NSPLIT + P + s
                pe_.wait_ge(act_hi, n + 1)
                pe_.wait_ge(act_lo, n + 1)
                for b in range(2):
                    pe_.wait_ge(hi_done, 2 * (NSPLIT + P + n) + b + 1)
                    if b:
                        pe_.wait_ge(lo1_done, NSPLIT + P + n + 1)
                    else:
                        pe_.wait_ge(lo0_done, NSPLIT + P - POOL_TILES + n + 1)
                    for x in range(4):
                        nb = 4 * b + x
                        out = psum[:, 2 + nb // 2, (nb % 2) * T:(nb % 2) * T + T]
                        w1, w0 = (w[:, (2 * k + b) % 4, x * P:x * P + P] for w in (w_hi, w_lo))
                        mm(out, w1, h_hi[:, s % 4, :], first and nb % 2 == 0, False, skip_group_check=True)
                        mm(out, w1, h_lo[:, s % 4, :], False, False, skip_group_check=True)
                        last = mm(out, w0, h_hi[:, s % 4, :], False, final, skip_group_check=True)
                    last.then_inc(y_done if b else half_used, 1)

            for s in range(4):
                v_tile(s, s, s == 0, False)
            with pe_.Fori(1, P // 4 - 1) as it:
                for s in range(4):
                    v_tile(s, it * 4 + s, False, False)
            for s in range(4):
                v_tile(s, P - 4 + s, False, True)

            sum_squares(AT[("norm", 4, "ssq")], blk(SQ, 8), KC, lambda c: pe_.wait_ge(squared, NORM_BASE[4] + c + 1))

        @block.scalar
        def _(act):
            def empty(n, dst, func=ACT.Copy, cols=None, **kw):
                act.wait_ge(a_done, n + 1)
                src = abuf(n) if cols is None else abuf(n)[:, 0:cols]
                nc.scalar.activation(dst, src, func, **kw).then_inc(a_read, 1)

            def square(src, dst, done):
                nc.scalar.activation(dst, src, ACT.Square).then_inc(done, 1)

            dest = {}
            for b in range(4):
                dest[f"dq{b}"], dest[f"dk{b}"] = RAW + b, RAW + 4 + b
                dest[f"mq{b}"], dest[f"mk{b}"] = RAW + 8 + b, RAW + 12 + b
                dest[f"dg{b}"], dest[f"mg{b}"] = SIL + b, SIL + 4 + b
                dest[f"nq{b}"] = NQ + b
                dest[f"cb{b}"], dest[f"cc{b}"], dest[f"ch{b}"] = CONV + b, CONV + 4 + b, CONV + 8 + b
            for b in range(8):
                dest[f"ga{b}"], dest[f"gb{b}"] = SIG + b, SIG + 8 + b
            dest["ks"], dest["kw"] = KS, KW

            def high(half, src):
                nc.scalar.activation(w_hi[:, half, :], src, ACT.Copy).then_inc(hi_done, 1)

            def high_slot(k, b, n):
                i, value = slot_of(n)
                act.wait_ge(slot_in[i], value)
                if k >= 2:
                    who, value = half_free[k - 2, b]
                    act.wait_ge(who, value)
                high((2 * k + b) % 4, ring[:, i, b * HSLOT:b * HSLOT + HSLOT])

            def high_u(s, n, first):
                for b in range(2):
                    act.wait_ge(slot_in[(NSLOT + s) % RING], slot_count(NSLOT + s, n - s))
                    if first:
                        act.wait_ge(*half_free[NSPLIT - 2 + s, b])
                    elif b:
                        act.wait_ge(act_done, n - 1)
                    else:
                        act.wait_ge(half_used, NHALF + n - 1)
                    at = b * HSLOT
                    high((2 * (NSPLIT + s) + b) % 4, ring[:, (NSLOT + s) % RING, at:at + HSLOT])

            k_hi = 0
            for s in STEPS:
                kind = s[0]
                while kind != "wq" and k_hi <= ahead(s):
                    for b in range(2):
                        high_slot(k_hi, b, SLOT_OF_SPLIT[k_hi])
                    k_hi += 1
                if kind == "small":
                    act.wait_ge(small_in, 16 * 10)
                    act.wait_ge(lam_step, 2)
                    nc.scalar.activation(small[:, 2:4], small[:, 0:2], ACT.Exp).then_inc(cact_ready, 1)
                    act.wait_ge(rel_done, 3)
                    nc.scalar.activation(flat(CACT, 4), c_raw, ACT.Silu).then_inc(cact_ready, 1)
                elif kind == "norm":
                    k = s[1]
                    if k == 0:
                        act.wait_ge(x_in, 32)
                        act.wait_ge(const_set, 2)
                    for c in range(KC):
                        if k == 1:
                            act.wait_ge(x_ready, c + 1)
                        if k == 2:
                            act.wait_ge(x1_ready, c + 1)
                        if k == 3:
                            act.wait_ge(v_read, VT[("out2", c)] + 1)
                        if k and c == 0:
                            act.wait_ge(a_done, {1: filled("subln", 3), 2: filled("norm", 1, "ssq"),
                                                 3: filled("mixnorm", 1)}[k])
                        square(xres[:, c, :], blk(SQ + c), squared)
                    if k == 1:
                        act.wait_ge(sub_done, 10)
                    elif k:
                        act.wait_ge(rstd_ready, {2: 2, 3: 5}[k])
                    empty(AT[s + ("ssq",)], std[:, :], ACT.Sqrt, scale=1.0 / D, bias=eps_c[:, 0:1])
                    if k != 1:
                        first = {0: 0, 2: 8, 3: 16}[k]
                        for c in range(KC):
                            act.wait_ge(t_ready, first + c + 1)
                            if c == 0 and k:
                                act.wait_ge(a_done, filled("proj", "gb7" if k == 2 else "ch3"))
                            nc.scalar.activation(h_hi[:, c, :], blk(NTMP + c), ACT.Copy).then_inc(th_done, 1)
                elif kind == "proj" and s[1] in ("dv", "mv"):
                    pass
                elif kind == "proj" and s[1] == "gt":
                    for i in range(TT):
                        empty(AT[s + (i,)], gsig[:, i, :], ACT.Sigmoid, cols=24)
                elif kind == "proj" and s[1] == "nv":
                    for j in range(TT):
                        empty(AT[s + (j,)], blk(NV + j))
                elif kind == "proj" and s[1] in ("kc", "vc"):
                    act.wait_ge(a_done, AT[s] + 1)
                    win = win_of(0 if s[1] == "kc" else 1)
                    for g in range(2):
                        src = abuf(AT[s])[DH * g:DH * g + DH, :]
                        nc.scalar.activation(win[0:DH, g, :], src, ACT.Copy)
                        last = nc.scalar.activation(win[DH:P, g, 0:T - 1], src[:, 1:T], ACT.Copy)
                    last.then_inc(a_read, 1)
                elif kind == "proj":
                    if s[1] == "ga0":
                        act.wait_ge(rope_done, 16)
                    empty(AT[s], blk(dest[s[1]]))
                elif kind == "soft":
                    p = s[1]
                    act.wait_ge(max_done, 2 * p + 2)
                    if p >= 2:
                        act.wait_ge(turn_done, p - 1)
                    for m in range(2):
                        for i in range(TT):
                            cols = slice(0, P) if i == 0 else slice(P, TRI)
                            n = 2 * m + i
                            nc.scalar.activation(ex_of(p)[:, m, cols], sc_of(p)[:, m, cols], ACT.Exp,
                                                 bias=nmax[:, p % 2, n:n + 1], accum_out=sums[:, p % 2, n:n + 1])\
                                .then_inc(exp_done, 1)
                elif kind == "turn":
                    p = s[1]
                    if p == 8:
                        act.wait_ge(cmp_step, 2)
                        nc.scalar.activation(cpt, turned[:, :, 0:T], ACT.Copy).then_inc(pt_done, 1)
                    act.wait_ge(turn_done, p + 1)
                    if p >= 3:
                        act.wait_ge(a_done, filled("pv", p - 3) if p < 11 else filled("pv", (p - 3) | 1))
                    m = 1 if p < 4 else 2
                    nc.scalar.activation(pt_of(p)[:, 0:m, :], turned[:, 0:m, :], ACT.Copy).then_inc(pt_done, 1)
                    if p == 3:
                        nc.scalar.activation(blk(SIL, 8), blk(SIL, 8), ACT.Silu).then_inc(gates_ready, 1)
                elif kind == "pv":
                    p = s[1]
                    empty(AT[s], blk(OT + (p if p < 8 else (p - 9) // 2)))
                    if p < 4:
                        act.wait_ge(a_read, filled("pv", p))
                        act.wait_ge(a_done, filled("norm", 0, "ssq"))
                        square(blk(OT + p), blk(SQ + p), osq_done)
                    if p == 7:
                        act.wait_ge(a_read, filled("proj", "gb7"))
                        for ab in range(2):
                            nc.scalar.activation(blk(SIG + 8 * ab, 8), blk(SIG + 8 * ab, 8), ACT.Sigmoid)\
                                .then_inc(gates_ready, 1)
                    if p > 8:
                        act.wait_ge(a_read, filled("pv", p))
                        act.wait_ge(a_done, filled("norm", 2, "ssq"))
                        square(blk(OT + (p - 9) // 2), blk(SQ + (p - 9) // 2), osq_done)
                elif kind == "subln":
                    if s[1]:
                        act.wait_ge(sub_done, 3 * s[1] - 2)
                    else:
                        act.wait_ge(rstd_ready, 1)
                    empty(AT[s], std[:, :], ACT.Sqrt, scale=1.0 / P, bias=eps_c[:, 1:2])
                elif kind == "ple":
                    for j in range(KC):
                        empty(AT[s + (j,)], blk(PLE + j))
                elif kind == "gate":
                    for j in range(KC):
                        act.wait_ge(v_read, VT[("merge", 2 * j + 1)] + 1)
                        empty(AT[s + (j,)], blk(SIG + j), ACT.Sigmoid)
                elif kind in ("cmpk", "cmpv"):
                    which = 0 if kind == "cmpk" else 1
                    n = AT[s + (0,)]
                    act.wait_ge(a_done, n + 1)
                    hid = abuf(n)[0:DH, 0:3 * CMP_N].rearrange("p (g n) -> p g n", g=3)
                    nc.scalar.activation(pebias[:, which:which + 1], hid[:, 2, 0:1], ACT.Copy).then_inc(cmp_bias, 1)
                    act.wait_ge(cmp_bias, which + 1)
                    act.wait_ge(zero_set, 1)
                    nc.scalar.activation(h1[:, which, :, 0:CMP_N], hid[:, 0:2, :], ACT.Gelu_apprx_tanh,
                                         bias=pebias[:, which:which + 1]).then_inc(a_read, 1)
                    if which == 0:
                        empty(AT[s + (1,)], kct, cols=CMP_PAD)
                    else:
                        n = AT[s + (1,)]
                        act.wait_ge(a_done, n + 1)
                        for r in range(4):
                            rows = slice(32 * r, 32 * r + 32)
                            last = nc.scalar.activation(bd[rows, :, r, :],
                                                        abuf(n)[rows, 0:P].rearrange("p (g d) -> p g d", g=2), ACT.Copy)
                        last.then_inc(a_read, 1)
                elif kind == "cmps":
                    act.wait_ge(cmp_vec, 4)
                    nc.scalar.activation(flat(CSC, 2), flat(CSC, 2), ACT.Exp).then_inc(cmp_exp, 1)
                elif kind == "conv":
                    for b in range(4):
                        act.wait_ge(conv_done, b + 1)
                        square(blk(OT + 4 + b), blk(SQ + 4 + b), osq_done)
                elif kind == "mixnorm":
                    for j in range(2):
                        act.wait_ge(rstd_ready, 3 + j)
                        empty(AT[s + (j,)], std[:, :], ACT.Sqrt, scale=1.0 / 512, bias=eps_c[:, 0:1])
                elif kind == "wq":
                    for j in range(KC):
                        while k_hi <= min(first_wq + j + 1, NSPLIT - 1):
                            for b in range(2):
                                high_slot(k_hi, b, SLOT_OF_SPLIT[k_hi])
                            k_hi += 1
                        empty(AT[s + (j,)], blk(QP + j))
                elif kind == "route":
                    for n in range(2):
                        high_u(n, n, True)
                    for x in range(4):
                        i, first = x // 2, 4 * (x % 2)
                        act.wait_ge(key_done, x + 1)
                        banks = psum[:, 2 + 2 * (x % 2):4 + 2 * (x % 2), :]
                        nc.scalar.activation(scores_of(i)[:, :, first:first + 4, :],
                                             banks.rearrange("p m (j k) -> p m j k", j=4), ACT.Copy)\
                            .then_inc(key_read, 1)

            def gelu(s, n):
                act.wait_ge(act_done, n + 1)
                nc.scalar.activation(arena[:, n, :], psum[:, UBANKS[s % 4], 0:T], ACT.Gelu_apprx_tanh)\
                    .then_inc(act_read, 1)

            def u_loop(a, b):
                with act.Fori(a // 4, b // 4) as it:
                    for s in range(4):
                        high_u(s, it * 4 + s, False)
                        gelu(s + 2, it * 4 + s - 2)

            act.wait_ge(key_done, 4)
            for s in range(4):
                if s >= 2:
                    high_u(s, s, False)
                    gelu(s + 2, s - 2)
            u_loop(4, SOFT_TILE)
            act.wait_ge(topk_step, SOFT_STEP)
            nc.scalar.activation(blk(106), blk(106), ACT.Exp).then_inc(soft_exp, 1)
            u_loop(SOFT_TILE, SEL_TILE)
            act.wait_ge(sel_done, 1)
            u_loop(SEL_TILE, P)
            for s in range(2):
                gelu(s + 2, P - 2 + s)

            def high_v(s, n, first):
                for b in range(2):
                    act.wait_ge(slot_in[(NSLOT + P + s) % RING], slot_count(NSLOT + P + s, n - s))
                    if first:
                        act.wait_ge(*((half_used, NHALF + P + n - 1), (act_done, P + n - 1))[b])
                    elif b:
                        act.wait_ge(y_done, n - 1)
                    else:
                        act.wait_ge(half_used, NHALF + P + n - 1)
                    at = b * HSLOT
                    high((2 * (NSPLIT + P + s) + b) % 4, ring[:, (NSLOT + P + s) % RING, at:at + HSLOT])

            def high_act(s, n, first):
                if first:
                    act.wait_ge(act_done, P)
                    act.wait_ge(routed, T // 4)
                else:
                    act.wait_ge(y_done, n - 3)
                nc.scalar.activation(h_hi[:, s, :], arena[:, n, :], ACT.Copy).then_inc(act_hi, 1)

            for s in range(4):
                high_v(s, s, s < 2)
                high_act(s, s, True)
            with act.Fori(1, P // 4) as it:
                for s in range(4):
                    high_v(s, it * 4 + s, False)
                    high_act(s, it * 4 + s, False)

            act.wait_ge(y_done, P)
            for c in range(KC):
                act.wait_ge(x_ready, KC + c + 1)
                square(xres[:, c, :], blk(SQ + c), squared)
            act.wait_ge(rstd_ready, 6)
            empty(AT[("norm", 4, "ssq")], std[:, :], ACT.Sqrt, scale=1.0 / D, bias=eps_c[:, 0:1])

        @block.gpsimd
        def _(pool):
            def low(k, half, src, hi_value, done):
                pool.wait_ge(hi_done, hi_value)
                nc.gpsimd.tensor_tensor(w_lo[:, half, :], src, w_hi[:, half, :].bitcast(F32), ALU.subtract)\
                    .then_inc(done, 1)

            def load_mod(m):
                if m >= 2:
                    pool.wait_ge(mod_done, m - 1)
                pool.dma_start(flat(MODR[m // 24] + 4 * (m % 2), 4), mods[m]).then_inc(mod_in[m % 2], 16)

            k_lo = 0
            for s in STEPS:
                kind = s[0]
                while k_lo <= ahead(s):
                    src = ring[:, SLOT_OF_SPLIT[k_lo] % RING, HSLOT:D]
                    low(k_lo, (2 * k_lo + 1) % 4, src, 2 * k_lo + 2, lo1_done)
                    k_lo += 1
                if kind == "small":
                    load_mod(0)
                    load_mod(1)
                elif kind == "mod" and s[1] + 2 < 24:
                    load_mod(s[1] + 2)
                elif kind == "ple":
                    pool.wait_ge(a_done, filled("pv", 7))
                    for m in range(24, 48):
                        load_mod(m)
                elif kind == "proj" and s[1] in rope_blocks:
                    b = rope_blocks.index(s[1])
                    pool.wait_ge(small_in, 16 * 10)
                    pool.wait_ge(a_read, filled(*s))
                    nc.gpsimd.tensor_tensor(blk(QK + b), blk(RAW + b), cos_t, ALU.mult).then_inc(cos_done, 1)
                elif kind == "soft" and s[1] >= 4:
                    p = s[1]
                    if p < 8:
                        pool.wait_ge(inv_done, p + 1)
                    else:
                        pool.wait_ge(gated_done, p - 7)
                    for m in range(2):
                        for i in range(TT):
                            cols = slice(0, P) if i == 0 else slice(P, TRI)
                            n = 2 * m + i
                            e = ex_of(p)[:, m, cols]
                            last = nc.gpsimd.tensor_scalar(e, e, rsum[:, p % 2, n:n + 1], 1.0, ALU.mult, ALU.mult)
                    last.then_inc(probs_done, 1)
                elif kind == "norm" and s[1] == 1:
                    pool.wait_ge(x_ready, KC)
                    nc.gpsimd.memset(blk(BD, 3), 0.0).then_inc(zero_set, 1)
                elif kind == "conv":
                    for b in range(4):
                        pool.wait_ge(a_read, filled("proj", f"ch{b}"))
                        nc.gpsimd.tensor_tensor(blk(CONV + 4 + b), blk(CONV + 4 + b), blk(CONV + 8 + b), ALU.mult)\
                            .then_inc(z_done, 1)
                    for b in range(4):
                        pool.wait_ge(conv_step, 3 * b + 3)
                        nc.gpsimd.tensor_tensor(blk(OT + 4 + b), blk(PROD + b), blk(CONV + b), ALU.mult)\
                            .then_inc(conv_done, 1)
                elif kind == "mixnorm":
                    pool.wait_ge(masked_done, 8)
                    pool.wait_ge(rope_done, 16)
                    pool.dma_start(ring_keys, keys).then_inc(peer_in, 16)

            def low_tile(base, s, n, both):
                src = ring[:, (NSLOT + base + s) % RING, :]
                k = NSPLIT + base + s
                if both:
                    low(k, 2 * k % 4, src[:, 0:HSLOT], 2 * (NSPLIT + base + n) + 1, lo2_done)
                else:
                    pool.wait_ge(lo0_done, NSPLIT + base - POOL_TILES + n + 1)
                low(k, (2 * k + 1) % 4, src[:, HSLOT:D], 2 * (NSPLIT + base + n) + 2, lo1_done)

            with pool.Fori(0, POOL_TILES // 4) as it:
                for s in range(4):
                    low_tile(0, s, it * 4 + s, True)
            with pool.Fori(POOL_TILES // 4, P // 4) as it:
                for s in range(4):
                    low_tile(0, s, it * 4 + s, False)
            with pool.Fori(0, P // 4) as it:
                for s in range(4):
                    low_tile(P, s, it * 4 + s, False)

        @block.vector
        def _(dve):
            v = nc.vector

            def bc(ap, shape):
                return ap.to_broadcast(shape)

            def inverse(std_value, ready):
                dve.wait_ge(a_read, std_value)
                v.reciprocal(rstd[:, :], std[:, :]).then_inc(rstd_ready, 1)
                dve.wait_ge(rstd_ready, ready)

            def low(half, src, hi_value):
                dve.wait_ge(hi_done, hi_value)
                v.tensor_tensor(w_lo[:, half, :], src, w_hi[:, half, :].bitcast(F32), ALU.subtract)\
                    .then_inc(lo0_done, 1)

            def modulation(m):
                dve.wait_ge(mod_in[m % 2], 16 * (m // 2 + 1))
                dve.wait_ge(cact_ready, 2)
                if m:
                    dve.wait_ge(mod_done, m)
                v.tensor_tensor_reduce(junk, flat(MODR[m // 24] + 4 * (m % 2), 4), flat(CACT, 4), 1.0, pcol("b_mod", m),
                                       ALU.mult, ALU.add, mod[:, m:m + 1]).then_inc(mod_done, 1)

            def rope(b):
                n = VT[("rope", rope_blocks[b])]
                dve.wait_ge(v_done, n + 1)
                tmp = blk(SIG + b)
                v.tensor_tensor(tmp, vbuf(n), sin_t, ALU.mult).then_inc(v_read, 1)
                dve.wait_ge(v_read, n + 1)
                dve.wait_ge(cos_done, b + 1)
                v.tensor_tensor(blk(QK + b), blk(QK + b), tmp, ALU.add).then_inc(rope_done, 1)

            v.memset(ones[:, :], 1.0).then_inc(const_set, 1)
            v.memset(eps_c[:, 0:1], EPS)
            v.memset(eps_c[:, 1:2], SUBLN_EPS).then_inc(const_set, 1)

            k_lo, ropes = 0, []
            for s in STEPS:
                kind = s[0]
                while ropes and not (kind == "mod" or kind == "proj" and s[1] in rope_blocks):
                    rope(ropes.pop(0))
                while k_lo <= ahead(s):
                    low(2 * k_lo % 4, ring[:, SLOT_OF_SPLIT[k_lo] % RING, 0:HSLOT], 2 * k_lo + 1)
                    k_lo += 1
                if kind == "small":
                    dve.wait_ge(small_in, 16 * 10)
                    for j in range(2):
                        a, b = pcol("lam", 128 * j, 64), pcol("lam", 128 * j + 64, 64)
                        v.tensor_tensor_reduce(s_sb[:, 2048 + 64 * j:2112 + 64 * j], a, b, 1.0, 0.0, ALU.mult, ALU.add,
                                               small[:, j:j + 1]).then_inc(lam_step, 1)
                    dve.wait_ge(cact_ready, 1)
                    v.tensor_tensor(small[:, 4:5], small[:, 3:4], small[:, 2:3], ALU.subtract).then_inc(lam_step, 1)
                    dve.wait_ge(lam_step, 3)
                    v.tensor_scalar(small[:, 5:6], small[:, 4:5], -LAM_INIT, None, ALU.add).then_inc(lam_step, 1)
                    v.tensor_scalar(small[:, 6:7], pcol("subln_g"), 1.0 - LAM_INIT, None, ALU.mult).then_inc(lam_step, 1)
                    for n, heads in enumerate((slice(0, 2), slice(2, HEADS))):
                        dve.wait_ge(rel_done, n + 1)
                        v.tensor_copy(bias_rows[:, heads, :], psum[:, heads, 0:TRI]).then_inc(rel_read, 1)
                    dve.wait_ge(rel_done, 3)
                    cb = s_sb[:, 1536:1536 + 512].rearrange("p (i h n) -> p i h n", i=TT, h=HEADS)
                    v.memset(s_sb[:, 1536:2048], NEG).then_inc(const_set, 1)
                    dve.wait_ge(const_set, 3)
                    for i in range(TT):
                        src = psum[:, 7, i * CMP_N * HEADS:(i + 1) * CMP_N * HEADS]
                        last = v.tensor_copy(cb[:, i, :, 0:CMP_N], src.rearrange("p (n h) -> p h n", h=HEADS))
                    last.then_inc(rel_read, 1)
                elif kind == "norm":
                    k = s[1]
                    if k == 0:
                        dve.wait_ge(x_in, 32)
                    if k >= 2:
                        dve.wait_ge(mod_done, 24 * (k - 1))
                        at = (8, 32)[k - 2]
                        v.scalar_tensor_tensor(gm[:, k - 2, :], mod[:, at:at + 8], 1.0,
                                               pcol(("ln_mix_g", "ln_ffn_g")[k - 2], 0, 8), ALU.add, ALU.mult)\
                            .then_inc(mod_ready, 1)
                        dve.wait_ge(mod_ready, k - 1)
                    if k == 2:
                        dve.wait_ge(x1_ready, 8)
                    if k == 3:
                        dve.wait_ge(o_ready, 12)
                    inverse(filled(*s, "ssq"), {0: 1, 1: 2, 2: 3, 3: 6}[k])
                    if k == 1:
                        for c in range(KC):
                            v.scalar_tensor_tensor(xres[:, c, :], xres[:, c, :], pcol("final_g", c), rstd[:, :],
                                                   ALU.mult, ALU.mult).then_inc(x1_ready, 1)
                        continue
                    first = {0: 0, 2: 8, 3: 16}[k]
                    for c in range(KC + 1):
                        if c < KC:
                            t = blk(NTMP + c)
                            gain = pcol("norm_g", c) if k == 0 else gm[:, k - 2, c:c + 1]
                            ins = v.scalar_tensor_tensor(t, xres[:, c, :], gain, rstd[:, :], ALU.mult, ALU.mult)
                            if k:
                                ins.then_inc(shift_in, 1)
                                sh = (0 if k == 2 else 24) + c
                                dve.wait_ge(shift_in, KC * (k - 2) + c + 1)
                                ins = v.tensor_scalar(t, t, mod[:, sh:sh + 1], None, ALU.add)
                            ins.then_inc(t_ready, 1)
                        if c:
                            dve.wait_ge(th_done, first + c)
                            v.tensor_tensor(h_lo[:, c - 1, :], blk(NTMP + c - 1), h_hi[:, c - 1, :].bitcast(F32),
                                            ALU.subtract).then_inc(h_ready, 1)
                elif kind == "mod":
                    modulation(s[1])
                elif kind == "proj" and s[1] in ("dv", "mv"):
                    rows = flat(DV if s[1] == "dv" else MV, 4).rearrange("p (i n) -> p i n", i=TT)
                    for j in range(4):
                        n = VT[s + (j,)]
                        dve.wait_ge(v_done, n + 1)
                        v.tensor_copy(rows[:, j // 2, (j % 2) * T:(j % 2) * T + T], vbuf(n)).then_inc(v_read, 1)
                elif kind == "proj" and s[1] in rope_blocks:
                    ropes.append(rope_blocks.index(s[1]))
                    if len(ropes) > 1:
                        rope(ropes.pop(0))
                elif kind == "scores":
                    p = s[1]
                    dve.wait_ge(scores_done, p + 1)
                    if p == 0:
                        dve.wait_ge(sheet_in, 16)
                    if p >= 2:
                        dve.wait_ge(exp_done, 4 * (p - 1))
                    sc = sc_of(p)
                    if p < 8:
                        m3 = bc(mask.unsqueeze(1), [P, 2, TRI])
                        v.scalar_tensor_tensor(sc, scb(p), SCALE, m3, ALU.mult, ALU.add).then_inc(masked_done, 1)
                    else:
                        if p == 8:
                            dve.wait_ge(sheet_in, 32)
                        j = (p - 8) // 2
                        bias = sheet[:, j:j + 5:4, :]
                        v.scalar_tensor_tensor(sc[:, :, 0:P], scb(p)[:, :, 0:P], SCALE, bias[:, :, P:T], ALU.mult, ALU.add)
                        v.scalar_tensor_tensor(sc[:, :, P:TRI], scb(p)[:, :, P:TRI], SCALE, bias, ALU.mult, ALU.add)\
                            .then_inc(masked_done, 1)
                    dve.wait_ge(masked_done, p + 1)
                    nm = nmax[:, p % 2, :].rearrange("p (m i) -> p m i", m=2)
                    v.tensor_reduce(nm[:, :, 0], sc[:, :, 0:P], AX, ALU.max, negate=True).then_inc(max_done, 1)
                    v.tensor_reduce(nm[:, :, 1], sc[:, :, P:TRI], AX, ALU.max, negate=True).then_inc(max_done, 1)
                elif kind == "soft":
                    p = s[1]
                    dve.wait_ge(exp_done, 4 * p + 4)
                    rs = rsum[:, p % 2, :]
                    if p >= 2:
                        dve.wait_ge(probs_done, p - 1)
                    v.reciprocal(rs, sums[:, p % 2, :]).then_inc(inv_done, 1)
                    dve.wait_ge(inv_done, p + 1)
                    if p < 4:
                        e = ex_of(p)
                        v.tensor_scalar(rs[:, 2:4], rs[:, 2:4], small[:, 5:6], None, ALU.mult).then_inc(lam_scaled, 1)
                        for i in range(TT):
                            cols = slice(0, P) if i == 0 else slice(P, TRI)
                            v.tensor_scalar(e[:, 0, cols], e[:, 0, cols], rs[:, i:i + 1], None, ALU.mult)\
                                .then_inc(map0_done, 1)
                        dve.wait_ge(lam_scaled, p + 1)
                        dve.wait_ge(map0_done, 2 * p + 2)
                        for i in range(TT):
                            cols = slice(0, P) if i == 0 else slice(P, TRI)
                            last = v.scalar_tensor_tensor(e[:, 0, cols], e[:, 1, cols], rs[:, 2 + i:3 + i], e[:, 0, cols],
                                                          ALU.mult, ALU.add)
                        last.then_inc(probs_done, 1)
                    elif p >= 8:
                        j, br = (p - 8) // 2, 1 + p % 2
                        g = gsig[:, :, :].rearrange("p i (h b) -> p h i b", b=3)[:, j:j + 5:4, :, br]
                        dve.wait_ge(a_read, filled("proj", "gt", TT - 1))
                        rr = rs.rearrange("p (m i) -> p m i", m=2)
                        v.tensor_tensor(rr, rr, g, ALU.mult).then_inc(gated_done, 1)
                elif kind == "pv" and 4 <= s[1] < 8:
                    p = s[1]
                    dve.wait_ge(a_read, filled(*s))
                    dve.wait_ge(gates_ready, 1)
                    v.tensor_tensor(blk(OT + p), blk(OT + p), blk(SIL + p), ALU.mult).then_inc(o_ready, 1)
                elif kind == "subln":
                    hd = s[1]
                    dve.wait_ge(a_read, filled(*s))
                    if hd:
                        dve.wait_ge(sub_done, 3 * hd)
                    v.reciprocal(rstd[:, :], std[:, :]).then_inc(sub_done, 1)
                    dve.wait_ge(sub_done, 3 * hd + 1)
                    dve.wait_ge(osq_done, hd + 1)
                    v.scalar_tensor_tensor(blk(OT + hd), blk(OT + hd), small[:, 6:7], rstd[:, :], ALU.mult, ALU.mult)\
                        .then_inc(sub_done, 1)
                    dve.wait_ge(sub_done, 3 * hd + 2)
                    v.tensor_tensor(blk(OT + hd), blk(OT + hd), blk(SIL + hd), ALU.mult).then_inc(sub_done, 1)
                elif kind == "merge":
                    dve.wait_ge(gates_ready, 3)
                    for nb in range(KC):
                        na, nb_ = VT[s + (2 * nb,)], VT[s + (2 * nb + 1,)]
                        m_, sa, sb_ = blk(MERGED + nb), blk(SIG + nb), blk(SIG + 8 + nb)
                        dve.wait_ge(v_done, na + 1)
                        v.tensor_tensor(m_, vbuf(na), sa, ALU.mult).then_inc(v_read, 1)
                        dve.wait_ge(v_done, nb_ + 1)
                        v.tensor_tensor(sb_, vbuf(nb_), sb_, ALU.mult).then_inc(v_read, 1)
                        dve.wait_ge(v_read, nb_ + 1)
                        v.tensor_tensor(m_, m_, sb_, ALU.add).then_inc(merged_ready, 1)
                        modulation(24 + nb)
                elif kind == "out1":
                    for nb in range(KC):
                        n = VT[s + (nb,)]
                        dve.wait_ge(v_done, n + 1)
                        v.tensor_tensor(xres[:, nb, :], vbuf(n), xres[:, nb, :], ALU.add).then_inc(v_read, 1)
                        modulation(32 + nb)
                elif kind == "gate":
                    for nb in range(KC):
                        dve.wait_ge(a_read, filled(*s, nb))
                        v.tensor_tensor(blk(PLE + nb), blk(PLE + nb), blk(SIG + nb), ALU.mult).then_inc(ple_step, 1)
                        modulation(40 + nb)
                    for nb in range(KC):
                        if nb == 0:
                            dve.wait_ge(a_done, filled(*s, KC - 1))
                        dve.wait_ge(ple_step, nb + 1)
                        v.tensor_tensor(xres[:, nb, :], xres[:, nb, :], blk(PLE + nb), ALU.add).then_inc(x_ready, 1)
                elif kind == "cmps":
                    v.tensor_copy(flat(CBIAS, 2), s_sb[:, 1536:2048]).then_inc(cmp_vec, 1)
                    dve.wait_ge(cmp_step, 1)
                    dve.wait_ge(cmp_vec, 1)
                    for g in range(2):
                        src = psum[:, 6 + g, 0:T].rearrange("p (i c) -> p i c", i=TT)
                        b = cbias[:, :, 4 * g:4 * g + 4, :].rearrange("p i h n -> p i (h n)")
                        last = v.scalar_tensor_tensor(csc[:, :, g, :], src, SCALE, b, ALU.mult, ALU.add)
                    last.then_inc(cmp_vec, 1)
                    dve.wait_ge(cmp_vec, 2)
                    maps = flat(CSC, 2).rearrange("p (k n) -> p k n", n=CMP_PAD)
                    v.tensor_reduce(cst1[:, 0, :], maps, AX, ALU.max).then_inc(cmp_vec, 1)
                    dve.wait_ge(cmp_vec, 3)
                    v.tensor_tensor(maps, maps, bc(cst1[:, 0, :].unsqueeze(2), [P, 16, CMP_PAD]), ALU.subtract)\
                        .then_inc(cmp_vec, 1)
                    dve.wait_ge(cmp_exp, 1)
                    v.tensor_reduce(cst1[:, 1, :], maps, AX, ALU.add).then_inc(cmp_vec, 1)
                    dve.wait_ge(cmp_vec, 5)
                    v.reciprocal(cst1[:, 2, :], cst1[:, 1, :]).then_inc(cmp_vec, 1)
                    dve.wait_ge(cmp_vec, 6)
                    for i in range(TT):
                        g = gsig[:, i, :].rearrange("p (h b) -> p h b", b=3)[:, :, 0]
                        dve.wait_ge(a_read, filled("proj", "gt", TT - 1))
                        last = v.scalar_tensor_tensor(cst1[:, 1, 8 * i:8 * i + 8], cst1[:, 2, 8 * i:8 * i + 8],
                                                      valid[:, i:i + 1], g, ALU.mult, ALU.mult)
                    last.then_inc(cmp_vec, 1)
                    dve.wait_ge(cmp_vec, 7)
                    v.tensor_tensor(maps, maps, bc(cst1[:, 1, :].unsqueeze(2), [P, 16, CMP_PAD]), ALU.mult)\
                        .then_inc(cmp_vec, 1)
                elif kind == "conv":
                    for b in range(4):
                        dve.wait_ge(z_done, b + 1)
                        z, y = blk(CONV + 4 + b), blk(PROD + b)
                        w = [pcol("conv_w", 4 * k + b) for k in range(3)]
                        v.tensor_scalar(y, z, w[2], None, ALU.mult).then_inc(conv_step, 1)
                        dve.wait_ge(conv_step, 3 * b + 1)
                        v.scalar_tensor_tensor(y[:, 1:T], z[:, 0:T - 1], w[1], y[:, 1:T], ALU.mult, ALU.add)\
                            .then_inc(conv_step, 1)
                        dve.wait_ge(conv_step, 3 * b + 2)
                        v.scalar_tensor_tensor(y[:, 2:T], z[:, 0:T - 2], w[0], y[:, 2:T], ALU.mult, ALU.add)\
                            .then_inc(conv_step, 1)
                elif kind == "mixnorm":
                    for j in range(2):
                        if j:
                            dve.wait_ge(o_ready, 8)
                        inverse(filled(*s, j), 4 + j)
                        for c in range(4):
                            g = pcol(("attn_g", "conv_g")[j], c)
                            o = blk(OT + 4 * j + c)
                            v.scalar_tensor_tensor(o, o, g, rstd[:, :], ALU.mult, ALU.mult).then_inc(o_ready, 1)
                elif kind == "out2":
                    for nb in range(KC):
                        n = VT[s + (nb,)]
                        dve.wait_ge(v_done, n + 1)
                        v.scalar_tensor_tensor(xres[:, nb, :], vbuf(n), mod[:, 16 + nb:17 + nb], xres[:, nb, :],
                                               ALU.mult, ALU.add).then_inc(v_read, 1)

            def best16(pieces, values, index):
                for s_, v_ in zip(pieces, values):
                    last = v.max(v_[:, 0:8], s_)
                last.then_inc(topk_step, 1)
                yield
                for s_, v_, i_ in zip(pieces, values, index):
                    v.max_index(i_[:, 0:8], v_[:, 0:8], s_)
                for s_, v_ in zip(pieces, values):
                    last = v.match_replace(s_, v_[:, 0:8], s_, LOWEST)
                last.then_inc(topk_step, 1)
                yield
                for s_, v_ in zip(pieces, values):
                    last = v.max(v_[:, 8:16], s_)
                last.then_inc(topk_step, 1)
                yield
                for s_, v_, i_ in zip(pieces, values, index):
                    last = v.max_index(i_[:, 8:16], v_[:, 8:16], s_)
                last.then_inc(topk_step, 1)
                yield

            for i in range(TT):
                dve.wait_ge(key_read, 2 * i + 2)
                at = TILE_STEPS * i
                mh = [(m, hd) for m in range(2) for hd in range(HEADS)]
                for _ in best16([scores_of(i)[:, m, hd, :] for m, hd in mh], [top_v[:, m, hd, :] for m, hd in mh],
                                [top_i[:, m, hd, :] for m, hd in mh]):
                    at += 1
                    dve.wait_ge(topk_step, at)
                v.tensor_copy(top_f[:, :, :, :], top_i[:, :, :, :])
                n = 2 * HEADS * NKEYS
                cand = s_sb[:, n * i:n * i + n].rearrange("p (h a b) -> p h a b", h=HEADS, a=TOPK)
                v.tensor_tensor(cand, bc(top_v[:, 0, :, :].unsqueeze(3), [P, HEADS, TOPK, TOPK]),
                                bc(top_v[:, 1, :, :].unsqueeze(2), [P, HEADS, TOPK, TOPK]), ALU.add)\
                    .then_inc(topk_step, 1)
                at += 1
                dve.wait_ge(topk_step, at)
                cands = s_sb[:, n * i:n * i + n].rearrange("p (h c) -> p h c", h=HEADS)
                for _ in best16([cands[:, hd, :] for hd in range(HEADS)], [best_v[:, i, hd, :] for hd in range(HEADS)],
                                [best_i[:, hd, :] for hd in range(HEADS)]):
                    at += 1
                    dve.wait_ge(topk_step, at)
                v.tensor_single_scalar(best_p[:, 0, :, :], best_i[:, :, :], 4, ALU.logical_shift_right)
                v.tensor_single_scalar(best_p[:, 1, :, :], best_i[:, :, :], 15, ALU.bitwise_and).then_inc(topk_step, 1)
                dve.wait_ge(topk_step, at + 1)
                v.tensor_copy(best_f[:, :, :, :], best_p[:, :, :, :]).then_inc(topk_step, 1)
                dve.wait_ge(topk_step, at + 2)
                dve.wait_ge(key_done, 4)
                for k in range(2):
                    v.tensor_tensor(cmp_of(k), bc(best_f[:, k, :, :].unsqueeze(3), [P, HEADS, TOPK, TOPK]),
                                    bc(iota[:, 0:TOPK].unsqueeze(1).unsqueeze(1), [P, HEADS, TOPK, TOPK]), ALU.is_equal)\
                        .then_inc(picked, 1)
                for k in range(2):
                    dve.wait_ge(picked, 4 * i + k + 1)
                    v.tensor_tensor(cmp_of(k), cmp_of(k), bc(top_f[:, k, :, :].unsqueeze(2), [P, HEADS, TOPK, TOPK]),
                                    ALU.mult).then_inc(picked, 1)
                for k in range(2):
                    dve.wait_ge(picked, 4 * i + k + 3)
                    last = v.tensor_reduce(sel[:, i, k, :].rearrange("p (h k) -> p h k", h=HEADS), cmp_of(k), AX, ALU.add)
                last.then_inc(topk_step, 1)
                dve.wait_ge(topk_step, at + 3)
            low_u = lambda s, n: low(2 * (NSPLIT + s) % 4, ring[:, (NSLOT + s) % RING, 0:HSLOT], 2 * (NSPLIT + n) + 1)
            at = 2 * TILE_STEPS
            best = best_v[:, :, :, :].rearrange("p i h k -> p (i h) k")
            v.tensor_copy(gsum[:, 0, :], best[:, :, 0]).then_inc(topk_step, 1)
            dve.wait_ge(topk_step, at + 1)
            v.tensor_tensor(best, best, bc(gsum[:, 0, :].unsqueeze(2), [P, TT * HEADS, TOPK]), ALU.subtract)\
                .then_inc(topk_step, 1)
            with dve.Fori(POOL_TILES // 4, SOFT_TILE // 4) as it:
                for s in range(4):
                    low_u(s, it * 4 + s)
            dve.wait_ge(soft_exp, 1)
            v.tensor_reduce(gsum[:, 1, :], best, AX, ALU.add).then_inc(topk_step, 1)
            dve.wait_ge(topk_step, at + 3)
            v.reciprocal(gsum[:, 2, :], gsum[:, 1, :]).then_inc(topk_step, 1)
            dve.wait_ge(topk_step, at + 4)
            for i in range(TT):
                last = v.tensor_tensor(sel[:, i, 2, :].rearrange("p (h k) -> p h k", h=HEADS), best_v[:, i, :, :],
                                       bc(gsum[:, 2, HEADS * i:HEADS * i + HEADS].unsqueeze(2), [P, HEADS, TOPK]), ALU.mult)
            last.then_inc(topk_step, 1)
            with dve.Fori(SOFT_TILE // 4, P // 4) as it:
                for s in range(4):
                    low_u(s, it * 4 + s)
            dve.wait_ge(sel_done, 1)
            v.tensor_copy(sel_t[:, 0:2, :], psum[:, 4, :].rearrange("p (k t) -> p k t", k=2)).then_inc(topk_step, 1)
            v.tensor_copy(sel_t[:, 2, :], psum[:, 5, 0:T]).then_inc(topk_step, 1)
            dve.wait_ge(topk_step, TOPK_STEPS + 2)

            def weighted(half, n, value):
                if value is not None:
                    dve.wait_ge(route_done, value)
                for j in range(4):
                    k = 4 * half + j
                    t = n * 8 + k
                    v.tensor_scalar(hot1[:, k, :], iota[:, :], sel_t[:, 0, bass.ds(t, 1)], None, ALU.is_equal)
                    last = v.tensor_scalar(hot2[:, k, :], iota[:, :], sel_t[:, 1, bass.ds(t, 1)], sel_t[:, 2, bass.ds(t, 1)],
                                           ALU.is_equal, ALU.mult)
                last.then_inc(hot_ready, 1)

            def route(half, n):
                dve.wait_ge(act_read, P)
                dve.wait_ge(route_done, n * 2 + half + 1)
                a = arena[:, :, bass.ds(n * 8 + 4 * half, 4)].rearrange("p i t -> p t i")
                w = psum[:, 2 + half, :].rearrange("p (t i) -> p t i", t=4)
                v.tensor_tensor(a, w, a, ALU.mult).then_inc(routed, 1)

            weighted(0, 0, None)
            weighted(1, 0, None)
            with dve.Fori(1, T // 8) as it:
                for half in range(2):
                    route(half, it - 1)
                    weighted(half, it, it * 2 + half - 1)
            for half in range(2):
                route(half, T // 8 - 1)

            def low_v(s, n, first):
                low(2 * (NSPLIT + P + s) % 4, ring[:, (NSLOT + P + s) % RING, 0:HSLOT], 2 * (NSPLIT + P + n) + 1)
                dve.wait_ge(act_hi, n + 1)
                v.tensor_tensor(h_lo[:, s, :], arena[:, n, :], h_hi[:, s, :].bitcast(F32), ALU.subtract)\
                    .then_inc(act_lo, 1)

            dve.wait_ge(routed, T // 4)
            with dve.Fori(0, P // 4) as it:
                for s in range(4):
                    low_v(s, it * 4 + s, False)

            dve.wait_ge(y_done, P)
            for nb in range(KC):
                v.scalar_tensor_tensor(xres[:, nb, :], psum[:, 2 + nb // 2, (nb % 2) * T:(nb % 2) * T + T],
                                       mod[:, 40 + nb:41 + nb], xres[:, nb, :], ALU.mult, ALU.add).then_inc(x_ready, 1)
            dve.wait_ge(x_ready, 2 * KC)
            inverse(filled("norm", 4, "ssq"), 7)
            for c in range(KC):
                v.scalar_tensor_tensor(blk(OUT + c), xres[:, c, :], pcol("ln_final_g", c), rstd[:, :], ALU.mult, ALU.mult)\
                    .then_inc(out_ready, 1)


def rel_bucket(dist):
    n = np.maximum(dist, 0)
    ratio = (np.log(np.maximum(n, 1).astype(np.float32) / np.float32(16)) / np.float32(np.log(8.0))).astype(np.float32)
    large = 16 + (ratio * np.float32(16)).astype(np.int32)
    return np.where(n < 16, n, np.minimum(large, 31))


def constants():
    c = np.zeros((P, NCST), np.float32)

    def put(name, a):
        c[:a.shape[0], CST[name][0]:CST[name][0] + a.shape[1]] = a

    put("ident", np.eye(P, dtype=np.float32))
    put("iota", np.tile(np.arange(P, dtype=np.float32), (P, 1)))
    inv = np.float32(500000.0) ** (-np.arange(0, 16, 2, dtype=np.float32) / np.float32(16))
    ang = np.arange(T, dtype=np.float32)[:, None] * inv[None, :]
    cos, sin = np.ones((P, T), np.float32), np.zeros((P, T), np.float32)
    swap = np.eye(P, dtype=np.float32)
    for base in (0, DH):
        for d in range(8):
            cos[base + d] = cos[base + 8 + d] = np.cos(ang[:, d])
            sin[base + d], sin[base + 8 + d] = -np.sin(ang[:, d]), np.sin(ang[:, d])
            a, b = base + d, base + 8 + d
            swap[a, a] = swap[b, b] = 0
            swap[a, b] = swap[b, a] = 1
    put("perm", swap)
    put("cos", cos)
    put("sin", sin)
    q, k = np.arange(P)[:, None], np.arange(T)[None, :]
    put("mask", np.concatenate([np.where(k[:, :P] <= q, 0, NEG), np.where(k <= q + P, 0, NEG)], 1).astype(np.float32))
    t = np.arange(TT)[None, :] * P + np.arange(P)[:, None]
    put("valid", (t >= 31).astype(np.float32))

    def one_hot(dist):
        o = np.zeros((33, dist.size), np.float32)
        o[rel_bucket(dist), np.arange(dist.size)] = 1
        o[32] = np.where(dist < 0, NEG, 0)
        return o

    put("rev", one_hot(255 - np.arange(TRI)))
    put("fwd", one_hot(np.arange(512) - 272))
    return c


def stream(x):
    w1, w2 = x["w_in"][0], x["w_in_2"][0]
    heads = [0, 4, 1, 5, 2, 6, 3, 7]
    at = np.cumsum([0, 512, 128, 128, 128, 128, 128, 128, 24, 512, 512, 512])

    def cols(w):
        return w.reshape(-1, P, w.shape[1]).transpose(1, 0, 2).reshape(P, -1)

    def head_rows(w):
        return w.reshape(8, DH, -1)[heads].reshape(512, -1)

    base1 = {"dq": 0, "dk": 512, "dg": 1536, "mq": 2048, "mk": 2560, "mg": 3584, "ga": 4096, "gb": 5120}
    nq = w2[:, :512].reshape(D, 8, DH)[:, heads].reshape(D, 512)
    wo2 = np.concatenate([head_rows(x["w_out_2"][0][:512]), x["w_out_2"][0][512:]])
    out = np.empty((NSLOT, P, D), np.float32)
    for n, (s, i) in enumerate(SLOTS):
        k, a = s[0], s[1] if len(s) > 1 else None
        if k == "proj" and a in ("dv", "mv"):
            v = cols(w1[:, 1024:1536] if a == "dv" else w1[:, 3072:3584])
            out[n] = v[:, i * D:i * D + D]
        elif k == "proj" and a == "nv":
            v = cols(np.concatenate([w2[:, at[4]:at[5]], w2[:, at[6]:at[7]]], 1))
            out[n] = v[:, i * D:i * D + D]
        elif k == "proj" and a == "gt":
            v = np.zeros((D, P), np.float32)
            v[:, 0:24] = w2[:, at[7]:at[8]]
            out[n] = cols(v)
        elif k == "proj" and a[:2] in base1:
            c = base1[a[:2]] + P * int(a[2:])
            out[n] = cols(w1[:, c:c + P])
        elif k == "proj" and a[:2] == "nq":
            out[n] = cols(nq[:, P * int(a[2:]):][:, :P])
        elif k == "proj" and a in ("kc", "vc", "ks", "kw"):
            c = at[{"kc": 1, "vc": 2, "ks": 3, "kw": 5}[a]]
            out[n] = cols(w2[:, c:c + P])
        elif k == "proj":
            c = at[{"cb": 8, "cc": 9, "ch": 10}[a[:2]]] + P * int(a[2:])
            out[n] = cols(w2[:, c:c + P])
        elif k == "ple":
            out[n] = np.concatenate([cols(x["w_ple"][0][:, P * j:P * j + P]) for j in range(4 * i, 4 * i + 4)], 1)
        elif k == "merge":
            w = x["w_branch_moba" if i % 2 else "w_branch_diff"][0]
            out[n] = np.concatenate([cols(w[:, P * j:P * j + P]) for j in (2 * (i // 2), 2 * (i // 2) + 1)], 1)
        elif k in ("cmpk", "cmpv"):
            w = x["cmp_wk1_2" if k == "cmpk" else "cmp_wv1_2"][0]
            out[n] = w.reshape(16, P, DH).transpose(1, 0, 2).reshape(P, D)
        else:
            w = {"out1": x["w_out"][0], "gate": x["w_ple_gate"][0], "out2": wo2, "wq": x["peer_wq_2"][0]}[k]
            out[n] = cols(w[:, P * i:P * i + P])
    return out


def kernel(**inputs):
    import concourse.bacc as bacc
    from concourse.bass_utils import run_bass_kernel_spmd

    x = {k: np.asarray(v) for k, v in inputs.items()}
    heads = [0, 4, 1, 5, 2, 6, 3, 7]

    def col(v):
        return np.asarray(v).reshape(-1, P).T

    par = np.zeros((P, NPAR), np.float32)
    rel = np.ones((33, 8), np.float32)
    rel[:32] = x["rel_table_2"]
    lam = np.concatenate([x[n][0] for n in ("lambda_q1", "lambda_k1", "lambda_q2", "lambda_k2")])
    for name, v in (("norm_g", col(x["norm_g"])), ("final_g", col(x["final_g"])), ("ln_mix_g", col(x["ln_mix_g_2"])),
                    ("ln_ffn_g", col(x["ln_ffn_g_2"])), ("ln_final_g", col(x["ln_final_g_2"])),
                    ("attn_g", col(x["norm_attn_g_2"].reshape(8, DH)[heads])), ("conv_g", col(x["norm_conv_g_2"])),
                    ("subln_g", col(x["subln_g"])), ("conv_w", col(x["conv_w_2"])), ("b_mod", col(x["b_mod_2"])),
                    ("lam", np.tile(lam, (P, 1))), ("rel", rel)):
        par[:v.shape[0], PAR[name][0]:PAR[name][1]] = v
    pe = np.zeros((2, P, T), np.float32)
    for w, n in enumerate(("cmp_pe_k_2", "cmp_pe_v_2")):
        pe[w, :, 0:32:2] = x[n][0].reshape(16, P).T
    arrays = {
        "x_t": x["x"][0].T.reshape(KC, P, T).transpose(1, 0, 2),
        "p_t": x["p"][0, 0].T.reshape(2, P, T).transpose(1, 0, 2),
        "params": par,
        "consts": constants(),
        "weights": stream(x),
        "c_rows": np.tile(x["c_2"], (P, 1)),
        "mods": x["w_mod_2"][0].T.reshape(48, P, D),
        "w2k": x["cmp_wk2_2"][0],
        "w2v": x["cmp_wv2_2"][0],
        "pe": pe,
        "keys": x["peer_keys_2"][0].transpose(1, 3, 0, 2).reshape(P, HEADS, NKEYS),
        "u_t": x["peer_u_2"][0].reshape(P, P, KC, P).transpose(1, 3, 2, 0).reshape(P, P, D),
        "v_rows": x["peer_v_2"][0].reshape(P, P, D).transpose(1, 0, 2),
    }
    nc = bacc.Bacc("TRN2", target_bir_lowering=False, num_devices=1)
    arrays = {k: np.ascontiguousarray(v) for k, v in arrays.items()}
    args = [nc.dram_tensor(k, v.shape, F32, kind="ExternalInput").ap() for k, v in arrays.items()]
    bias_dram = nc.dram_tensor("bias_rows", (P, HEADS, TRI), F32, kind="Internal").ap()
    out_t = nc.dram_tensor("out_t", (KC, P, T), F32, kind="ExternalOutput").ap()
    names = list(arrays)
    block_program(nc, **dict(zip(names, args)), bias_dram=bias_dram, out_t=out_t)
    r = run_bass_kernel_spmd(nc, [arrays], core_ids=[0])
    return r.results[0]["out_t"].reshape(D, T).T.reshape(1, T, D)
```

```python
from contextlib import ExitStack

import numpy as np

import concourse.bass as bass
from concourse import mybir

F32 = mybir.dt.float32
F32R = mybir.dt.float32r
BF16 = mybir.dt.bfloat16
U32 = mybir.dt.uint32
ALU = mybir.AluOpType
ACT = mybir.ActivationFunctionType
AX = mybir.AxisListType.X

P = 128
T = 256
TT = T // P
D = 1024
KC = D // P
DH = 64
HEADS = 8
HALF = HEADS // 2
NKEYS = 128
TOPK = 16
NEG = -1e30
LOWEST = -3.0e38
LAM_INIT = 0.8 - 0.6 * float(np.exp(-0.3 * 0))
EPS, SUBLN_EPS = 1e-6, 1e-5
SCALE = DH ** -0.5
UBANKS = (0, 1, 6, 7)
SOFT_TILE = 36
TILE_STEPS = 12
SOFT_STEP = 2 * TILE_STEPS + 2
TOPK_STEPS = SOFT_STEP + 3
CMP_N, CMP_PAD = (T - 32) // 16 + 1, 32
RING = 4
HSLOT = D // 2
TRI = P + T

FILL1 = [f"{n}{b}" for n, k in (("dg", 4), ("mg", 4), ("ga", 8), ("gb", 8)) for b in range(k)]
FILL2 = [f"{n}{b}" for n in ("cb", "cc", "ch") for b in range(4)]
FIRST1 = [f"{n}{b}" for n in ("dq", "dk") for b in range(4)] + ["dv"] \
    + [f"{n}{b}" for n in ("mq", "mk") for b in range(4)] + ["mv"]
FIRST2 = [f"nq{b}" for b in range(4)] + ["kc", "vc", "ks", "kw", "nv", "gt"]
SLOTS_OF = {"dv": 4, "mv": 4, "nv": 2}
ROWS = {"dv": (4, 512, T), "mv": (4, 512, T), "nv": (2, T, T), "gt": (2, P, 24)}


def plan():
    steps = [("norm", 0), ("small",)]
    fill, mod = list(FILL1), list(range(24))
    for n in FIRST1:
        steps += [("proj", n)]
        if n[0] == "m" and n != "mv":
            steps.append(("mod", mod.pop(0)))
    steps += [("scores", 0), ("scores", 1)]
    for p in range(8):
        steps.append(("soft", p))
        steps += [("proj", fill.pop(0)) for _ in range(2)] + [("mod", mod.pop(0)) for _ in range(2)]
        steps.append(("turn", p))
        if p + 2 < 8:
            steps.append(("scores", p + 2))
        steps += [("proj", fill.pop(0))]
        steps.append(("pv", p))
    steps += [("subln",), ("ple",), ("merge",), ("out1",), ("gate",)]
    steps += [("norm", 1), ("bias", 0), ("norm", 2), ("bias", 1)]
    steps += [("proj", n) for n in FIRST2]
    steps += [("scores", 8), ("scores", 9), ("cmpk",), ("cmpv",)]
    fill = list(FILL2)
    steps += [("proj", fill.pop(0)), ("cmpk1",), ("cmpv1",), ("proj", fill.pop(0)), ("cmps",)]
    steps += [("soft", 8), ("proj", fill.pop(0)), ("cmpt",)]
    for p in range(8, 16):
        steps.append(("turn", p))
        if p + 2 < 16:
            steps.append(("scores", p + 2))
        if p + 1 < 16:
            steps += [("soft", p + 1), ("proj", fill.pop(0))]
        if p in (10, 12):
            steps.append(("proj", fill.pop(0)))
        if p % 2 == 1:
            steps.append(("pv", p))
    steps += [("conv",), ("mixnorm",), ("out2",), ("norm", 3), ("wq",), ("route",)]
    assert not mod and not fill
    order = []
    for s in steps:
        k = {"proj": SLOTS_OF.get(s[-1], 1), "ple": 2, "merge": 8, "out1": 8, "gate": 8,
             "cmpk": 1, "cmpv": 1, "out2": 8, "wq": 8}.get(s[0], 0)
        order += [(s, i) for i in range(k)]
    return steps, order


STEPS, SLOTS = plan()
NSLOT = len(SLOTS)
SLOT_AT = {}
for _n, (_s, _i) in enumerate(SLOTS):
    SLOT_AT.setdefault(_s, _n)
SPLIT = {_n: _k for _k, _n in enumerate(n for n, (s, _) in enumerate(SLOTS) if s[0] in ("proj", "wq"))}
NSPLIT = len(SPLIT)
SLOT_OF_SPLIT = {_k: _n for _n, _k in SPLIT.items()}
POOL_TILES = 44
QUADS = T // 4
COPY_LAG = 4
GRP = 16
GROUPS = P // GRP

PAR = {}
_at = 0
for _name, _w in (("norm_g", 8), ("final_g", 8), ("ln_mix_g", 8), ("ln_ffn_g", 8), ("ln_final_g", 8),
                  ("attn_g", 4), ("conv_g", 4), ("subln_g", 1), ("conv_w", 12), ("b_mod", 48),
                  ("lam", 256), ("rel", 8)):
    PAR[_name] = (_at, _at + _w)
    _at += _w
NPAR = _at
CST = {}
_at = 0
for _name, _w in (("ident", P), ("perm", P), ("cos", T), ("sin", T), ("mask", TRI), ("iota", P),
                  ("valid", TT), ("rev", TRI), ("fwd", 512)):
    CST[_name] = (_at, _at + _w)
    _at += _w
NCST = _at


def block_program(nc, x_t, p_t, params, consts, weights, c_rows, mods, w2k, w2v, pe, keys, u_t, v_rows, bias_dram,
                  g_dram, out_t):
    with ExitStack() as ctx:
        def sb(name, shape, dt=F32):
            return ctx.enter_context(nc.sbuf_tensor(name, shape, dt))

        def sem(name):
            return ctx.enter_context(nc.semaphore(name))

        psum = ctx.enter_context(nc.psum_tensor("psum", [P, 8, 512], F32))
        arena = sb("arena", [P, P, T])
        ring = sb("ring", [P, RING, D])
        xres = sb("xres", [P, KC, T])
        w_hi = sb("w_hi", [P, 4, HSLOT], F32R)
        w_lo = sb("w_lo", [P, 4, HSLOT], F32R)
        h_hi = sb("h_hi", [P, KC, T], F32R)
        h_lo = sb("h_lo", [P, KC, T], F32R)
        s_sb = sb("s_sb", [P, TT * 2 * HEADS * NKEYS])
        par = sb("par", [P, NPAR])
        ident = sb("ident", [P, P])
        iota = sb("iota", [P, P])
        ones = sb("ones", [P, P])
        valid = sb("valid", [P, TT])
        mod = sb("mod", [P, 48])
        gm = sb("gm", [P, 2, KC])
        std = sb("std", [P, T])
        rstd = sb("rstd", [P, T])
        small = sb("small", [P, 64])
        nmax = sb("nmax", [P, 2, 4])
        sums = sb("sums", [P, 2, 4])
        rsum = sb("rsum", [P, 2, 4])
        gsig = sb("gsig", [P, TT, 24])
        cst1 = sb("cst1", [P, 3, 16])
        top_v = sb("top_v", [P, 2, HEADS, TOPK])
        gsum = sb("gsum", [P, 3, TT * HEADS])
        eps_c = sb("eps_c", [P, 2])

        def pcol(name, a=0, n=1):
            return par[:, PAR[name][0] + a:PAR[name][0] + a + n]

        def blk(a, n=1):
            return arena[:, a, :] if n == 1 else arena[:, a:a + n, :]

        def flat(a, n):
            return arena[:, a:a + n, :].rearrange("p a b -> p (a b)")

        QK, RAW, DV, MV, SIL, SIG, OT = 0, 16, 32, 36, 40, 48, 64
        SC, PT, EX, SQ, MERGED, PLE, PTOK, TAB, MSK, REL = 72, 78, 88, 94, 102, 110, 118, 120, 122, 124
        SHEET, NQ, KS, KW, KCW, VCW, NV, CONV = 0, 16, 20, 21, 22, 25, 28, 30
        CSC, CPT, CBIAS, BD, H1, PROD = 42, 44, 46, 48, 50, 52
        QP = 112
        MODR = MERGED, PT
        OUT = 0
        NTMP = SQ
        top_f = blk(104).rearrange("p (m h k) -> p m h k", m=2, h=HEADS)
        top_i = blk(105).bitcast(U32).rearrange("p (m h k) -> p m h k", m=2, h=HEADS)
        best_v = blk(106).rearrange("p (i h k) -> p i h k", i=TT, h=HEADS)
        best_p = blk(107).bitcast(U32).rearrange("p (m h k) -> p m h k", m=2, h=HEADS)
        best_f = blk(108).rearrange("p (m h k) -> p m h k", m=2, h=HEADS)
        best_i = blk(109)[:, 0:P].bitcast(U32).rearrange("p (h k) -> p h k", h=HEADS)
        sel = flat(100, 3).rearrange("p (i k j) -> p i k j", i=TT, k=3)
        cos_t, sin_t = blk(TAB), blk(TAB + 1)
        mask = flat(MSK, 2)[:, 0:TRI]
        rel_c = flat(REL, 4)[:, 0:TRI + 512]
        perm = flat(MSK, 2)[:, TRI:TRI + P]
        sheet = flat(SHEET, 8).rearrange("p (h j) -> p h j", h=HEADS)
        cbias = flat(CBIAS, 2).rearrange("p (i h n) -> p i h n", i=TT, h=HEADS)
        csc = flat(CSC, 2).rearrange("p (i g c) -> p i g c", i=TT, g=2)
        cpt = flat(CPT, 2).rearrange("p (g q) -> p g q", g=2)
        bd = flat(BD, 2).rearrange("p (g r d) -> p g r d", g=2, r=4)
        h1 = blk(H1)[0:DH, :].rearrange("p (w g n) -> p w g n", w=2, g=2)[:, :, :, 0:CMP_PAD]
        kct = blk(H1 + 1)[:, 0:CMP_PAD]
        pebias = blk(H1 + 1)[0:DH, 40:42]
        w2s = blk(H1 + 1)[0:DH, 64:192].rearrange("p (w d) -> p w d", w=2)
        junk = s_sb[:, 0:D]
        c_act = s_sb[:, 2560:2560 + D]

        def sc_of(p):
            return flat(SC + 3 * (p % 2), 3).rearrange("p (m c) -> p m c", m=2)

        def ex_of(p):
            return flat(EX + 3 * (p % 2), 3).rearrange("p (m c) -> p m c", m=2)

        def pt_of(p):
            return flat(PT + 3 * (p % 3), 3).rearrange("p (m c) -> p m c", m=2)

        bias_rows = flat(SC, 12).rearrange("p (h j) -> p h j", h=HEADS)

        def scores_of(i):
            n = 2 * HEADS * NKEYS
            return s_sb[:, n * i:n * i + n].rearrange("p (m h k) -> p m h k", m=2, h=HEADS)

        def cmp_of(k):
            return flat(P - 16 + 8 * k, 8).rearrange("p (h k a) -> p h k a", h=HEADS, k=TOPK)

        ring_keys = flat(120, 4).rearrange("p (h k) -> p h k", h=HEADS)
        def quads(a):
            return a.bitcast(BF16).rearrange("p (b t k) -> p b t k", b=2, t=4)

        hot1, hot2 = quads(flat(120, 2)), quads(s_sb[:, 0:512])
        wgt = [quads(flat(122 + 2 * x, 2)) for x in range(3)]
        sel_w = [s_sb[:, 512 + 128 * x:640 + 128 * x].bitcast(BF16) for x in range(3)]
        rest = [s_sb[:, 1024 + T * x:1024 + T * x + T] for x in range(2)]
        sel_1, sel_2 = std, rstd
        stage = s_sb[:, 2048:4096].rearrange("p (b r t g) -> p b r t g", b=2, r=GROUPS, t=8)
        g_back = s_sb[:, :].rearrange("p (t g) -> p g t", g=GRP)

        def win_of(which):
            return arena[:, (KCW, VCW)[which]:(KCW, VCW)[which] + 3, :]

        def abuf(n):
            return psum[:, n % 2, 0:T]

        def vbuf(n):
            return psum[:, 2 + n % 4, 0:T]

        def scb(p):
            return psum[:, 2 + 2 * (p % 2):4 + 2 * (p % 2), 0:TRI]

        turned = psum[:, 6:8, 0:TRI]

        x_in = sem("x_in")
        small_in = sem("small_in")
        sheet_in = sem("sheet_in")
        cmp_in = sem("cmp_in")
        peer_in = sem("peer_in")
        slot_in = [sem(f"slot_in{i}") for i in range(RING)]
        const_set = sem("const_set")
        zero_set = sem("zero_set")
        cact_ready = sem("cact_ready")
        lam_step = sem("lam_step")
        rel_done = sem("rel_done")
        a_done = sem("a_done")
        a_read = sem("a_read")
        v_done = sem("v_done")
        v_read = sem("v_read")
        mod_in = [sem(f"mod_in{i}") for i in range(2)]
        mod_done = sem("mod_done")
        mod_ready = sem("mod_ready")
        hi_done = sem("hi_done")
        lo0_done = sem("lo0_done")
        lo1_done = sem("lo1_done")
        lo2_done = sem("lo2_done")
        half_used = sem("half_used")
        t_ready = sem("t_ready")
        th_done = sem("th_done")
        x1_ready = sem("x1_ready")
        squared = sem("squared")
        rstd_ready = sem("rstd_ready")
        h_ready = sem("h_ready")
        cos_done = sem("cos_done")
        sin_done = sem("sin_done")
        rope_done = sem("rope_done")
        scores_done = sem("scores_done")
        masked_done = sem("masked_done")
        max_done = sem("max_done")
        exp_done = sem("exp_done")
        inv_done = sem("inv_done")
        lam_scaled = sem("lam_scaled")
        map0_done = sem("map0_done")
        gated_done = sem("gated_done")
        shift_in = sem("shift_in")
        probs_done = sem("probs_done")
        turn_done = sem("turn_done")
        pt_done = sem("pt_done")
        gates_ready = sem("gates_ready")
        osq_done = sem("osq_done")
        sub_done = sem("sub_done")
        o_ready = sem("o_ready")
        x_ready = sem("x_ready")
        merged_ready = sem("merged_ready")
        ple_step = sem("ple_step")
        cmp_step = sem("cmp_step")
        cmp_bias = sem("cmp_bias")
        cmp_exp = sem("cmp_exp")
        cmp_vec = sem("cmp_vec")
        z_done = sem("z_done")
        conv_step = sem("conv_step")
        conv_done = sem("conv_done")
        key_done = sem("key_done")
        key_read = sem("key_read")
        topk_step = sem("topk_step")
        picked = sem("picked")
        soft_exp = sem("soft_exp")
        act_done = sem("act_done")
        act_read = sem("act_read")
        sel_done = sem("sel_done")
        sel_read = sem("sel_read")
        hot2_ready = sem("hot2_ready")
        hot1_ready = sem("hot1_ready")
        wgt0_ready = sem("wgt0_ready")
        wgt_ready = sem("wgt_ready")
        route_done = sem("route_done")
        g_read = sem("g_read")
        spilled = [sem(f"spilled{i}") for i in range(2)]
        g_in = sem("g_in")
        weighted = sem("weighted")
        act_hi = sem("act_hi")
        act_lo = sem("act_lo")
        y_done = sem("y_done")
        fin_step = sem("fin_step")
        out_ready = sem("out_ready")
        stored = sem("stored")

        a_order, v_order = [], []
        for s in STEPS:
            k = s[0]
            if k == "norm":
                a_order += [s + ("ssq",)]
            elif k == "proj" and s[1] in ("dv", "mv"):
                v_order += [s + (j,) for j in range(4)]
            elif k == "proj" and s[1] in ROWS:
                a_order += [s + (j,) for j in range(TT)]
            elif k == "proj":
                a_order += [s]
                if s[1] in FIRST1:
                    v_order += [("rope", s[1])]
            elif k == "pv":
                a_order += [s]
            elif k == "subln":
                a_order += [s + (j,) for j in range(2)]
            elif k in ("ple", "gate", "wq"):
                a_order += [s + (j,) for j in range(KC)]
            elif k in ("cmpk", "cmpv"):
                a_order += [s + (0,)]
            elif k in ("cmpk1", "cmpv1"):
                a_order += [(k[:4], 1)]
            elif k == "mixnorm":
                a_order += [s + (0,), s + (1,)]
            if k == "merge":
                v_order += [s + (j,) for j in range(2 * KC)]
            if k in ("out1", "out2"):
                v_order += [s + (j,) for j in range(KC)]
            if k == "bias":
                v_order += [("bias_row", 4 * s[1] + j) for j in range(4)]
        a_order.append(("norm", 4, "ssq"))
        AT = {s: n for n, s in enumerate(a_order)}
        rope_blocks = [n for n in FIRST1 if n[1] in "qk" and n[0] in "dm"]
        VT = {s: n for n, s in enumerate(v_order)}
        NA, NVB = len(a_order), len(v_order)
        NORM_BASE = {0: 0, 1: 8, 2: 16, 3: 24, 4: 32}

        def filled(*s):
            return AT[s] + 1

        def slot_of(n):
            return n % RING, 16 * (n // RING + 1)

        def slot_count(n, more):
            return 16 * (n // RING + 1) + (16 // RING) * more

        def freer(n):
            s, i = SLOTS[n]
            k = s[0]
            if k == "ple":
                return a_done, filled(*s, 4 * i + 3)
            if k == "gate":
                return a_done, filled(*s, i)
            if k in ("cmpk", "cmpv"):
                return a_done, filled(*s, 0)
            if k == "merge":
                return v_done, VT[("merge", 4 * (i // 2) + 2 + i % 2)] + 1
            return v_done, VT[s + (i,)] + 1

        half_free = {}
        n_half = 0
        for k in range(NSPLIT):
            s, i = SLOTS[SLOT_OF_SPLIT[k]]
            last = i == SLOTS_OF.get(s[-1], 1) - 1 or s[0] == "wq"
            n_half += 1
            half_free[k, 0] = half_used, n_half
            if not last:
                n_half += 1
                half_free[k, 1] = half_used, n_half
            elif s[0] == "wq":
                half_free[k, 1] = a_done, filled(*s, i)
            elif s[1] in ("dv", "mv"):
                half_free[k, 1] = v_done, VT[s + (3,)] + 1
            elif s[1] in ROWS:
                half_free[k, 1] = a_done, filled(*s, TT - 1)
            else:
                half_free[k, 1] = a_done, filled(*s)
        NHALF = n_half

        first_wq = SPLIT[SLOT_AT[("wq",)]]
        first_2 = SPLIT[SLOT_AT[("proj", "nq0")]]

        def ahead(s):
            if s[0] == "soft":
                later = [x for x in STEPS[STEPS.index(s):] if x[0] == "proj"]
                return ahead(later[0]) if later else -1
            if s == ("scores", 9):
                return SPLIT[SLOT_AT[("proj", "cb0")]]
            if s == ("proj", "gt"):
                return SPLIT[SLOT_AT[s]]
            if s[0] == "small":
                return 1
            if s[0] == "norm":
                return {0: -1, 1: -1, 2: first_2 + 1, 3: first_wq + 1}[s[1]]
            if s[0] == "proj":
                k = SPLIT[SLOT_AT[s]] + SLOTS_OF.get(s[1], 1)
                return min(k, first_2 - 1) if k - SLOTS_OF.get(s[1], 1) < first_2 else min(k, first_wq - 1)
            if s[0] == "wq":
                return NSPLIT - 1
            return -1

        block = ctx.enter_context(nc.Block())

        @block.sync
        def _(sp):
            def load_slot(n):
                if n >= RING:
                    if n - RING in SPLIT:
                        k = SPLIT[n - RING]
                        sp.wait_ge(lo0_done, k + 1)
                        sp.wait_ge(lo1_done, k + 1)
                    else:
                        who, value = freer(n - RING)
                        sp.wait_ge(who, value)
                sp.dma_start(ring[:, n % RING, :], weights[n]).then_inc(slot_in[n % RING], 16)

            sp.dma_start(xres[:, :, :], x_t).then_inc(x_in, 16)
            sp.dma_start(par[:, :], params).then_inc(x_in, 16)
            load_slot(0)
            load_slot(1)
            for name, dst in (("ident", ident[:, :]), ("iota", iota[:, :]), ("valid", valid[:, :]),
                              ("cos", cos_t), ("sin", sin_t), ("mask", mask), ("perm", perm)):
                sp.dma_start(dst, consts[:, CST[name][0]:CST[name][1]]).then_inc(small_in, 16)
            sp.dma_start(rel_c[0:33, :], consts[0:33, CST["rev"][0]:CST["fwd"][1]]).then_inc(small_in, 16)
            sp.dma_start(blk(PTOK, 2), p_t).then_inc(small_in, 16)
            sp.dma_start(c_act, c_rows).then_inc(small_in, 16)
            for n in range(2, RING):
                load_slot(n)
            first2 = SLOT_AT[("proj", "nq0")]
            for n in range(RING, NSLOT):
                if n == first2:
                    sp.wait_ge(x_ready, KC)
                    sp.dma_start(w2s[:, 0, :], w2k).then_inc(cmp_in, 16)
                    sp.dma_start(w2s[:, 1, :], w2v).then_inc(cmp_in, 16)
                    for w in range(2):
                        sp.dma_start(win_of(w)[:, 2, :], pe[w]).then_inc(cmp_in, 16)
                load_slot(n)

            def load_tile(src, base, s, n, waits):
                for who, value in waits:
                    sp.wait_ge(who, value)
                sp.dma_start(ring[:, (base + s) % RING, :], src[n]).then_inc(slot_in[(base + s) % RING], 16)

            for s in range(RING):
                k = NSPLIT - RING + s
                load_tile(u_t, NSLOT, s, s, ((lo0_done, k + 1), (lo1_done, k + 1)))
            spill_from = POOL_TILES + 2 * COPY_LAG
            with sp.Fori(1, spill_from // RING) as it:
                for s in range(RING):
                    n = it * RING + s
                    load_tile(u_t, NSLOT, s, n, ((lo1_done, NSPLIT + n - RING + 1),))
            with sp.Fori(spill_from // RING, (spill_from + QUADS) // RING) as it:
                for s in range(RING):
                    n = it * RING + s
                    load_tile(u_t, NSLOT, s, n, ((lo1_done, NSPLIT + n - RING + 1),))
                    if s % 2:
                        sp.wait_ge(g_read, n - spill_from + 1)
                        at = (it * 2 + s // 2 - spill_from // 2) * (8 * GRP)
                        sp.dma_start(g_dram[:, :, bass.ds(at, 8 * GRP)],
                                     stage[:, s // 2].rearrange("p r t g -> p r (t g)")).then_inc(spilled[s // 2], 16)

            def reload(j):
                sp.dma_start(s_sb[:, :], g_dram[:, j, :]).then_inc(g_in, 16)

            for n in range(spill_from + QUADS, P):
                load_tile(u_t, NSLOT, n % RING, n, ((lo1_done, NSPLIT + n - RING + 1),))
                if n == spill_from + QUADS:
                    for i in range(2):
                        sp.wait_ge(spilled[i], 16 * (QUADS // 4))
                    sp.wait_ge(route_done, QUADS)
                    reload(0)

            def load_v_group(j, more):
                for s in range(GRP):
                    n = j * GRP + s
                    load_tile(v_rows, NSLOT + P, s, n, ((lo1_done, NSPLIT + P + n - RING + 1),))
                    if s == 0 and more == 2:
                        sp.wait_ge(weighted, GRP // 2)
                        reload(1)
                    if s == GRP - 1 and more:
                        sp.wait_ge(weighted, j * (GRP // 2) + GRP)
                        reload(j + 2)

            load_v_group(0, 2)
            with sp.Fori(1, GROUPS - 2) as j:
                load_v_group(j, 1)
            with sp.Fori(GROUPS - 2, GROUPS) as j:
                load_v_group(j, 0)
            for c in range(KC):
                sp.wait_ge(out_ready, c + 1)
                sp.dma_start(out_t[c], blk(OUT + c)).then_inc(stored, 16)
            sp.wait_ge(stored, 16 * KC)

        @block.tensor
        def _(pe_):
            def slot_ready(n):
                i, value = slot_of(n)
                pe_.wait_ge(slot_in[i], value)
                return ring[:, i, :]

            def take_a(n):
                if n >= 2:
                    pe_.wait_ge(a_read, n - 1)
                return abuf(n)

            def take_v(n):
                if n >= 4:
                    pe_.wait_ge(v_read, n - 3)
                return vbuf(n)

            def mm(out, lhs, rhs, start, stop, **kw):
                return nc.tensor.matmul(out, lhs, rhs, start=start, stop=stop, **kw)

            def sum_squares(n, sq, chunks, ready):
                out = take_a(n)
                for c in range(chunks):
                    ready(c)
                    last = mm(out, ones[:, :], sq[:, c, :], c == 0, c == chunks - 1)
                last.then_inc(a_done, 1)

            def projection(n, slot, chunks, width, rhs, ready, take, done):
                w = slot_ready(slot)
                out = take(n)
                for c in range(chunks):
                    ready(c)
                    last = mm(out, w[:, width + c * P:width + c * P + P], rhs[:, c, :], c == 0, c == chunks - 1)
                last.then_inc(done, 1)

            def split_mms(out, half, at, rhs, first, last):
                w1, w0 = w_hi[:, half, at:at + P], w_lo[:, half, at:at + P]
                mm(out, w1, rhs[0], first, False)
                mm(out, w1, rhs[1], False, False)
                return mm(out, w0, rhs[0], False, last)

            def half_ready(k, b, low=None):
                pe_.wait_ge(hi_done, 2 * k + b + 1)
                who, value = low or ((lo0_done, lo1_done)[b], k + 1)
                pe_.wait_ge(who, value)
                return (2 * k + b) % 4

            def split_projection(n, k, ready):
                out = take_a(n)
                for b in range(2):
                    half = half_ready(k, b)
                    for c4 in range(4):
                        c = 4 * b + c4
                        ready(c)
                        last = split_mms(out, half, c4 * P, (h_hi[:, c, :], h_lo[:, c, :]), c == 0, c == KC - 1)
                    last.then_inc(a_done if b else half_used, 1)

            def rope_turn(b):
                pe_.wait_ge(a_read, filled("proj", rope_blocks[b]))
                out = take_v(VT[("rope", rope_blocks[b])])
                mm(out, perm, blk(RAW + b), True, True).then_inc(v_done, 1)

            pending = []
            for s in STEPS:
                kind = s[0]
                if kind == "small":
                    pe_.wait_ge(small_in, 16 * 10)
                elif kind == "bias":
                    rel = par[0:33, PAR["rel"][0]:PAR["rel"][1]]
                    for hd in range(4 * s[1], 4 * s[1] + 4):
                        n = VT[("bias_row", hd)]
                        take_v(n)
                        lhs = rel[:, hd:hd + 1].to_broadcast([33, P])
                        mm(psum[:, 2 + n % 4, 0:TRI], lhs, rel_c[0:33, 0:TRI], True, True).then_inc(v_done, 1)
                    if s[1]:
                        pe_.wait_ge(pt_done, 8)
                        for n in range(CMP_N + 8):
                            at = TRI - 16 * (n - 8) - 31 + 272
                            last = mm(psum[:, 7, n * HEADS:(n + 1) * HEADS], rel_c[0:33, at:at + P], rel, True, True)
                        last.then_inc(rel_done, 1)
                elif kind == "norm":
                    k = s[1]
                    pe_.wait_ge(const_set, 1)
                    sum_squares(AT[s + ("ssq",)], blk(SQ, 8), KC,
                                lambda c, k=k: pe_.wait_ge(squared, NORM_BASE[k] + c + 1))
                elif kind == "proj" and s[1] in ROWS:
                    while pending:
                        rope_turn(pending.pop(0))
                    jobs, width, cols = ROWS[s[1]]
                    k0, slots = SPLIT[SLOT_AT[s]], SLOTS_OF.get(s[1], 1)
                    take, at, done = (take_v, VT, v_done) if jobs == 4 else (take_a, AT, a_done)
                    pe_.wait_ge(h_ready, 8 if jobs == 4 else 16)
                    out = [take(at[s + (j,)]) for j in range(jobs)]
                    each = HSLOT // width
                    for x in range(2 * slots):
                        half = half_ready(k0 + x // 2, x % 2)
                        for j in range(jobs):
                            i, col = (j // 2, (j % 2) * T) if jobs == 4 else (j, 0)
                            for y in range(each):
                                c = x * each + y
                                t = slice(P * i, P * i + P)
                                w = slice(y * width + col, y * width + col + cols)
                                o, end = out[j][:, 0:cols], c == KC - 1
                                mm(o, h_hi[:, c, t], w_hi[:, half, w], c == 0, False)
                                mm(o, h_lo[:, c, t], w_hi[:, half, w], False, False)
                                last = mm(o, h_hi[:, c, t], w_lo[:, half, w], False, end)
                            if x == 2 * slots - 1:
                                last.then_inc(done, 1)
                        if x < 2 * slots - 1:
                            last.then_inc(half_used, 1)
                elif kind == "proj":
                    base = 0 if s[1] in FIRST1 + FILL1 else 8
                    split_projection(AT[s], SPLIT[SLOT_AT[s]], lambda c, base=base: pe_.wait_ge(h_ready, base + c + 1))
                    if s[1] in rope_blocks:
                        pending.append(rope_blocks.index(s[1]))
                        if len(pending) > 1:
                            rope_turn(pending.pop(0))
                elif kind == "scores":
                    p = s[1]
                    while pending:
                        rope_turn(pending.pop(0))
                    if p < 8:
                        pe_.wait_ge(rope_done, 16)
                        pe_.wait_ge(v_read, VT[("proj", "mv", 3)] + 1)
                        base = QK if p < 4 else QK + 8
                        b = p % 4
                        q, k = blk(base + b), blk(base + 4 + b)
                    else:
                        pe_.wait_ge(a_read, filled("proj", "kw"))
                        pe_.wait_ge(v_read, VT[("bias_row", 7)] + 1)
                        q, k = blk(NQ + (p - 8) // 2), blk(KS if p % 2 == 0 else KW)
                    if p >= 2:
                        pe_.wait_ge(masked_done, p - 1)
                    out = scb(p)
                    for m in range(2):
                        r = slice(DH * m, DH * m + DH)
                        mm(out[:, m, 0:P], q[r, 0:P], k[r, 0:P], True, True)
                        last = mm(out[:, m, P:TRI], q[r, P:T], k[r, :], True, True)
                    last.then_inc(scores_done, 1)
                elif kind == "turn":
                    p = s[1]
                    pe_.wait_ge(probs_done, p + 1)
                    if p:
                        pe_.wait_ge(pt_done, p if p < 8 else p + 1)
                    for m in range(1 if p < 4 else 2):
                        for c in range(3):
                            last = nc.tensor.transpose(turned[:, m, c * P:c * P + P],
                                                       ex_of(p)[:, m, c * P:c * P + P], ident[:, :])
                    last.then_inc(turn_done, 1)
                elif kind == "pv":
                    p = s[1]
                    pe_.wait_ge(pt_done, p + 1 if p < 8 else p + 2)
                    if p < 8:
                        pe_.wait_ge(v_read, VT[("proj", "dv" if p < 4 else "mv", 3)] + 1)
                    out = take_a(AT[s])
                    pt = pt_of(p)
                    if p < 4:
                        v = flat(DV, 4).rearrange("p (i n) -> p i n", i=TT)
                        mm(out, v[:, 0, P * p:P * p + P], pt[:, 0, 0:T], True, False)
                        last = mm(out[:, P:T], v[:, 1, P * p:P * p + P], pt[:, 0, T:TRI], False, True)
                    elif p < 8:
                        v = flat(MV, 4).rearrange("p (i n) -> p i n", i=TT)
                        for m in range(2):
                            o, at = out[DH * m:DH * m + DH, :], P * (p - 4) + DH * m
                            mm(o, v[:, 0, at:at + DH], pt[:, m, 0:T], True, False)
                            last = mm(o[:, P:T], v[:, 1, at:at + DH], pt[:, m, T:TRI], False, True)
                    else:
                        pe_.wait_ge(a_read, filled("proj", "nv", TT - 1))
                        v = flat(NV, 2).rearrange("p (i n) -> p i n", i=TT)
                        for m in range(2):
                            o = out[DH * m:DH * m + DH, :]
                            mm(o, bd[:, m, (p - 8) // 2, :], cpt[:, m, :], True, False)
                            for w, pp in ((0, pt_of(p - 1)), (1, pt)):
                                at = P * w + DH * m
                                mm(o, v[:, 0, at:at + DH], pp[:, m, 0:T], False, False)
                                last = mm(o[:, P:T], v[:, 1, at:at + DH], pp[:, m, T:TRI], False, w == 1)
                    last.then_inc(a_done, 1)
                elif kind == "subln":
                    for j in range(2):
                        pe_.wait_ge(osq_done, 2 * j + 2)
                        take_a(AT[s + (j,)])
                        mm(psum[:, AT[s + (j,)] % 2, :], ones[:, :], flat(SQ + 2 * j, 2), True, True).then_inc(a_done, 1)
                elif kind == "ple":
                    for j in range(KC):
                        projection(AT[s + (j,)], SLOT_AT[s] + j // 4, 2, (j % 4) * T, blk(PTOK, 2), lambda c: None,
                                   take_a, a_done)
                elif kind == "merge":
                    pe_.wait_ge(masked_done, 8)
                    for nb in range(KC):
                        for ab in range(2):
                            slot = SLOT_AT[s] + 2 * (nb // 2) + ab
                            projection(VT[s + (2 * nb + ab,)], slot, 4, (nb % 2) * 512, blk(OT + 4 * ab, 4),
                                       lambda c, ab=ab: pe_.wait_ge(o_ready, 4) if ab else pe_.wait_ge(sub_done, 12),
                                       take_v, v_done)
                elif kind == "out1":
                    for nb in range(KC):
                        projection(VT[s + (nb,)], SLOT_AT[s] + nb, KC, 0, blk(MERGED, 8),
                                   lambda c: pe_.wait_ge(merged_ready, c + 1), take_v, v_done)
                elif kind == "gate":
                    for nb in range(KC):
                        projection(AT[s + (nb,)], SLOT_AT[s] + nb, KC, 0, xres[:, :, :],
                                   lambda c: pe_.wait_ge(v_read, VT[("out1", c)] + 1), take_a, a_done)
                elif kind in ("cmpk", "cmpv"):
                    which = 0 if kind == "cmpk" else 1
                    w1 = slot_ready(SLOT_AT[s])
                    pe_.wait_ge(a_read, filled("proj", ("kc", "vc")[which]))
                    pe_.wait_ge(cmp_in, 16 * 4)
                    win = win_of(which)
                    out = take_a(AT[s + (0,)])
                    for l2 in range(16):
                        last = mm(out[0:DH, 0:3 * CMP_N], w1[:, l2 * DH:l2 * DH + DH],
                                  win[:, :, 2 * l2:2 * l2 + 16 * (CMP_N - 1) + 1:16], l2 == 0, l2 == 15)
                    last.then_inc(a_done, 1)
                elif kind in ("cmpk1", "cmpv1"):
                    s = (kind[:4],)
                    which = 0 if kind == "cmpk1" else 1
                    pe_.wait_ge(a_read, filled(*s, 0))
                    out = take_a(AT[s + (1,)])
                    if which == 0:
                        for g in range(2):
                            last = mm(out[DH * g:DH * g + DH, 0:CMP_PAD], w2s[:, 0, :], h1[:, 0, g, :], True, True)
                    else:
                        for r in range(4):
                            for g in range(2):
                                last = mm(out[32 * r:32 * r + 32, DH * g:DH * g + DH], h1[:, 1, g, :], w2s[:, 1, :],
                                          True, True)
                    last.then_inc(a_done, 1)
                elif kind == "cmps":
                    pe_.wait_ge(a_read, filled("cmpk", 1))
                    pe_.wait_ge(cmp_vec, 1)
                    for g in range(2):
                        for i in range(TT):
                            for r in range(4):
                                at = (i * 4 + r) * CMP_PAD
                                last = mm(psum[:, 6 + g, at:at + CMP_PAD], blk(NQ + r)[DH * g:DH * g + DH, P * i:P * i + P],
                                          kct[DH * g:DH * g + DH, :], True, True)
                    last.then_inc(cmp_step, 1)
                elif kind == "cmpt":
                    pe_.wait_ge(cmp_vec, 8)
                    for g in range(2):
                        for i in range(TT):
                            last = nc.tensor.transpose(turned[:, g, P * i:P * i + P], csc[:, i, g, :], ident[:, :])
                    last.then_inc(cmp_step, 1)
                elif kind == "mixnorm":
                    for j in range(2):
                        sum_squares(AT[s + (j,)], blk(SQ + 4 * j, 4), 4,
                                    lambda c, j=j: pe_.wait_ge(osq_done, 4 + 4 * j + c + 1))
                elif kind == "out2":
                    for nb in range(KC):
                        projection(VT[s + (nb,)], SLOT_AT[s] + nb, KC, 0, blk(OT, 8),
                                   lambda c: pe_.wait_ge(o_ready, 4 + c + 1), take_v, v_done)
                elif kind == "wq":
                    for nb in range(KC):
                        split_projection(AT[s + (nb,)], SPLIT[SLOT_AT[s]] + nb,
                                         lambda c: pe_.wait_ge(h_ready, 16 + c + 1))
                elif kind == "route":
                    pe_.wait_ge(peer_in, 16)
                    pe_.wait_ge(v_read, NVB)
                    for x in range(4):
                        i, first = x // 2, 4 * (x % 2)
                        if x >= 2:
                            pe_.wait_ge(key_read, x - 1)
                        for m in range(2):
                            for j in range(4):
                                hd = first + j
                                pe_.wait_ge(a_read, filled("wq", hd))
                                last = mm(psum[:, 2 + 2 * (x % 2) + m, j * P:j * P + P],
                                          blk(QP + hd)[DH * m:DH * m + DH, P * i:P * i + P],
                                          ring_keys[DH * m:DH * m + DH, hd, :], True, True)
                        last.then_inc(key_done, 1)

            def u_tile(s, n, first, by_pool):
                k = NSPLIT + s
                if not first:
                    pe_.wait_ge(act_read, n - 3)
                out = psum[:, UBANKS[s % 4], 0:T]
                for b in range(2):
                    pe_.wait_ge(hi_done, 2 * (NSPLIT + n) + b + 1)
                    if b:
                        pe_.wait_ge(lo1_done, NSPLIT + n + 1)
                    elif by_pool:
                        pe_.wait_ge(lo2_done, n + 1)
                    else:
                        pe_.wait_ge(lo0_done, NSPLIT + n - POOL_TILES + 1)
                    for c4 in range(4):
                        c = 4 * b + c4
                        last = split_mms(out, (2 * k + b) % 4, c4 * P, (h_hi[:, c, :], h_lo[:, c, :]), c == 0, c == KC - 1)
                    last.then_inc(act_done if b else half_used, 1)

            def u_tiles(a, b):
                with pe_.Fori(a // 4, b // 4) as it:
                    for s in range(4):
                        u_tile(s, it * 4 + s, False, b <= POOL_TILES)

            pe_.wait_ge(a_read, NA - 1)
            for s in range(4):
                u_tile(s, s, True, True)
            u_tiles(4, POOL_TILES)

            pe_.wait_ge(topk_step, TOPK_STEPS)
            for k in range(3):
                for i in range(TT):
                    last = nc.tensor.transpose(psum[:, 4 + k // 2, ((k % 2) * TT + i) * P:((k % 2) * TT + i + 1) * P],
                                               sel[:, i, k, :], ident[:, :])
            last.then_inc(sel_done, 1)

            def quad(s, q, first):
                pe_.wait_ge(hot1_ready, q + 1)
                pe_.wait_ge(wgt0_ready, q + 1)
                pe_.wait_ge(wgt_ready, q + 1)
                if not first:
                    pe_.wait_ge(g_read, q - 3)
                for j in range(4):
                    out = psum[:, 2 + s, j * P:j * P + P]
                    for x in range(3):
                        last = mm(out, hot1[:, s % 2, j, :], wgt[x][:, s % 2, j, :], x == 0, x == 2)
                last.then_inc(route_done, 1)

            for s in range(4):
                u_tile(s, POOL_TILES + s, False, False)
                quad(s, s, True)
            with pe_.Fori(POOL_TILES // 4 + 1, (POOL_TILES + QUADS) // 4) as it:
                for s in range(4):
                    u_tile(s, it * 4 + s, False, False)
                    quad(s, it * 4 + s - POOL_TILES, False)
            u_tiles(POOL_TILES + QUADS, P)

            def v_tile(s, n, first, final):
                k = NSPLIT + P + s
                pe_.wait_ge(act_hi, n + 1)
                pe_.wait_ge(act_lo, n + 1)
                for b in range(2):
                    pe_.wait_ge(hi_done, 2 * (NSPLIT + P + n) + b + 1)
                    if b:
                        pe_.wait_ge(lo1_done, NSPLIT + P + n + 1)
                    else:
                        pe_.wait_ge(lo0_done, NSPLIT + P - POOL_TILES + n + 1)
                    for x in range(4):
                        nb = 4 * b + x
                        out = psum[:, 2 + nb // 2, (nb % 2) * T:(nb % 2) * T + T]
                        w1, w0 = (w[:, (2 * k + b) % 4, x * P:x * P + P] for w in (w_hi, w_lo))
                        mm(out, w1, h_hi[:, s % 4, :], first and nb % 2 == 0, False, skip_group_check=True)
                        mm(out, w1, h_lo[:, s % 4, :], False, False, skip_group_check=True)
                        last = mm(out, w0, h_hi[:, s % 4, :], False, final, skip_group_check=True)
                    last.then_inc(y_done if b else half_used, 1)

            for s in range(4):
                v_tile(s, s, s == 0, False)
            with pe_.Fori(1, P // 4 - 1) as it:
                for s in range(4):
                    v_tile(s, it * 4 + s, False, False)
            for s in range(4):
                v_tile(s, P - 4 + s, False, True)

            sum_squares(AT[("norm", 4, "ssq")], blk(SQ, 8), KC, lambda c: pe_.wait_ge(squared, NORM_BASE[4] + c + 1))

        @block.scalar
        def _(act):
            def empty(n, dst, func=ACT.Copy, cols=None, **kw):
                act.wait_ge(a_done, n + 1)
                src = abuf(n) if cols is None else abuf(n)[:, 0:cols]
                nc.scalar.activation(dst, src, func, **kw).then_inc(a_read, 1)

            def square(src, dst, done):
                nc.scalar.activation(dst, src, ACT.Square).then_inc(done, 1)

            dest = {}
            for b in range(4):
                dest[f"dq{b}"], dest[f"dk{b}"] = RAW + b, RAW + 4 + b
                dest[f"mq{b}"], dest[f"mk{b}"] = RAW + 8 + b, RAW + 12 + b
                dest[f"dg{b}"], dest[f"mg{b}"] = SIL + b, SIL + 4 + b
                dest[f"nq{b}"] = NQ + b
                dest[f"cb{b}"], dest[f"cc{b}"], dest[f"ch{b}"] = CONV + b, CONV + 4 + b, CONV + 8 + b
            for b in range(8):
                dest[f"ga{b}"], dest[f"gb{b}"] = SIG + b, SIG + 8 + b
            dest["ks"], dest["kw"] = KS, KW

            def high(half, src):
                nc.scalar.activation(w_hi[:, half, :], src, ACT.Copy).then_inc(hi_done, 1)

            def high_slot(k, b, n):
                i, value = slot_of(n)
                act.wait_ge(slot_in[i], value)
                if k >= 2:
                    who, value = half_free[k - 2, b]
                    act.wait_ge(who, value)
                high((2 * k + b) % 4, ring[:, i, b * HSLOT:b * HSLOT + HSLOT])

            def high_u(s, n, first):
                for b in range(2):
                    act.wait_ge(slot_in[(NSLOT + s) % RING], slot_count(NSLOT + s, n - s))
                    if first:
                        act.wait_ge(*half_free[NSPLIT - 2 + s, b])
                    elif b:
                        act.wait_ge(act_done, n - 1)
                    else:
                        act.wait_ge(half_used, NHALF + n - 1)
                    at = b * HSLOT
                    high((2 * (NSPLIT + s) + b) % 4, ring[:, (NSLOT + s) % RING, at:at + HSLOT])

            k_hi = 0
            for s in STEPS:
                kind = s[0]
                while kind != "wq" and k_hi <= ahead(s):
                    for b in range(2):
                        high_slot(k_hi, b, SLOT_OF_SPLIT[k_hi])
                    k_hi += 1
                if kind == "small":
                    act.wait_ge(small_in, 16 * 10)
                    act.wait_ge(lam_step, 2)
                    nc.scalar.activation(small[:, 2:4], small[:, 0:2], ACT.Exp).then_inc(cact_ready, 1)
                    nc.scalar.activation(c_act, c_act, ACT.Silu).then_inc(cact_ready, 1)
                elif kind == "norm":
                    k = s[1]
                    if k == 0:
                        act.wait_ge(x_in, 32)
                        act.wait_ge(const_set, 2)
                    for c in range(KC):
                        if k == 1:
                            act.wait_ge(x_ready, c + 1)
                        if k == 2:
                            act.wait_ge(x1_ready, c + 1)
                        if k == 3:
                            act.wait_ge(v_read, VT[("out2", c)] + 1)
                        if k == 1 and c == 0:
                            act.wait_ge(sub_done, 12)
                        if k and c == 0:
                            act.wait_ge(a_done, {1: filled("subln", 1), 2: filled("norm", 1, "ssq"),
                                                 3: filled("mixnorm", 1)}[k])
                        square(xres[:, c, :] if k != 1 else blk(MERGED + c), blk(SQ + c), squared)
                    if k:
                        act.wait_ge(rstd_ready, {1: 1, 2: 2, 3: 5}[k])
                    empty(AT[s + ("ssq",)], std[:, :], ACT.Sqrt, scale=1.0 / D, bias=eps_c[:, 0:1])
                    if k != 1:
                        first = {0: 0, 2: 8, 3: 16}[k]
                        for c in range(KC):
                            act.wait_ge(t_ready, first + c + 1)
                            if c == 0 and k:
                                act.wait_ge(a_done, filled("proj", "gb7" if k == 2 else "ch3"))
                            nc.scalar.activation(h_hi[:, c, :], blk(NTMP + c), ACT.Copy).then_inc(th_done, 1)
                elif kind == "proj" and s[1] in ("dv", "mv"):
                    pass
                elif kind == "proj" and s[1] == "gt":
                    for i in range(TT):
                        empty(AT[s + (i,)], gsig[:, i, :], ACT.Sigmoid, cols=24)
                elif kind == "proj" and s[1] == "nv":
                    for j in range(TT):
                        empty(AT[s + (j,)], blk(NV + j))
                elif kind == "proj" and s[1] in ("kc", "vc"):
                    act.wait_ge(a_done, AT[s] + 1)
                    win = win_of(0 if s[1] == "kc" else 1)
                    for g in range(2):
                        src = abuf(AT[s])[DH * g:DH * g + DH, :]
                        nc.scalar.activation(win[0:DH, g, :], src, ACT.Copy)
                        last = nc.scalar.activation(win[DH:P, g, 0:T - 1], src[:, 1:T], ACT.Copy)
                    last.then_inc(a_read, 1)
                elif kind == "proj":
                    if s[1] == "ga0":
                        act.wait_ge(rope_done, 16)
                    empty(AT[s], blk(dest[s[1]]))
                elif kind == "soft":
                    p = s[1]
                    act.wait_ge(max_done, 2 * p + 2)
                    if p >= 2:
                        act.wait_ge(turn_done, p - 1)
                    for m in range(2):
                        for i in range(TT):
                            cols = slice(0, P) if i == 0 else slice(P, TRI)
                            n = 2 * m + i
                            nc.scalar.activation(ex_of(p)[:, m, cols], sc_of(p)[:, m, cols], ACT.Exp,
                                                 bias=nmax[:, p % 2, n:n + 1], accum_out=sums[:, p % 2, n:n + 1])\
                                .then_inc(exp_done, 1)
                elif kind == "turn":
                    p = s[1]
                    if p == 8:
                        act.wait_ge(cmp_step, 2)
                        nc.scalar.activation(cpt, turned[:, :, 0:T], ACT.Copy).then_inc(pt_done, 1)
                    act.wait_ge(turn_done, p + 1)
                    if p >= 3:
                        act.wait_ge(a_done, filled("pv", p - 3) if p < 11 else filled("pv", (p - 3) | 1))
                    m = 1 if p < 4 else 2
                    nc.scalar.activation(pt_of(p)[:, 0:m, :], turned[:, 0:m, :], ACT.Copy).then_inc(pt_done, 1)
                    if p == 3:
                        nc.scalar.activation(blk(SIL, 8), blk(SIL, 8), ACT.Silu).then_inc(gates_ready, 1)
                elif kind == "pv":
                    p = s[1]
                    empty(AT[s], blk(OT + (p if p < 8 else (p - 9) // 2)))
                    if p < 4:
                        act.wait_ge(a_read, filled("pv", p))
                        act.wait_ge(a_done, filled("norm", 0, "ssq"))
                        square(blk(OT + p), blk(SQ + p), osq_done)
                    if p > 8:
                        act.wait_ge(a_read, filled("pv", p))
                        act.wait_ge(a_done, filled("norm", 2, "ssq"))
                        square(blk(OT + (p - 9) // 2), blk(SQ + (p - 9) // 2), osq_done)
                elif kind == "subln":
                    for j in range(2):
                        n = AT[s + (j,)]
                        act.wait_ge(a_done, n + 1)
                        nc.scalar.activation(flat(SQ + 2 * j, 2), psum[:, n % 2, :], ACT.Sqrt, scale=1.0 / P,
                                             bias=eps_c[:, 1:2]).then_inc(a_read, 1)
                elif kind == "ple":
                    for j in range(KC):
                        empty(AT[s + (j,)], blk(PLE + j))
                    for ab in range(2):
                        nc.scalar.activation(blk(SIG + 8 * ab, 8), blk(SIG + 8 * ab, 8), ACT.Sigmoid)\
                            .then_inc(gates_ready, 1)
                elif kind == "gate":
                    for j in range(KC):
                        act.wait_ge(v_read, VT[("merge", 2 * j + 1)] + 1)
                        empty(AT[s + (j,)], blk(SIG + j), ACT.Sigmoid)
                elif kind in ("cmpk", "cmpv"):
                    which = 0 if kind == "cmpk" else 1
                    n = AT[s + (0,)]
                    act.wait_ge(a_done, n + 1)
                    hid = abuf(n)[0:DH, 0:3 * CMP_N].rearrange("p (g n) -> p g n", g=3)
                    nc.scalar.activation(pebias[:, which:which + 1], hid[:, 2, 0:1], ACT.Copy).then_inc(cmp_bias, 1)
                    act.wait_ge(cmp_bias, which + 1)
                    act.wait_ge(zero_set, 1)
                    nc.scalar.activation(h1[:, which, :, 0:CMP_N], hid[:, 0:2, :], ACT.Gelu_apprx_tanh,
                                         bias=pebias[:, which:which + 1]).then_inc(a_read, 1)
                elif kind in ("cmpk1", "cmpv1"):
                    s = (kind[:4],)
                    if kind == "cmpk1":
                        empty(AT[s + (1,)], kct, cols=CMP_PAD)
                    else:
                        n = AT[s + (1,)]
                        act.wait_ge(a_done, n + 1)
                        for r in range(4):
                            rows = slice(32 * r, 32 * r + 32)
                            last = nc.scalar.activation(bd[rows, :, r, :],
                                                        abuf(n)[rows, 0:P].rearrange("p (g d) -> p g d", g=2), ACT.Copy)
                        last.then_inc(a_read, 1)
                elif kind == "cmps":
                    act.wait_ge(cmp_vec, 4)
                    nc.scalar.activation(flat(CSC, 2), flat(CSC, 2), ACT.Exp).then_inc(cmp_exp, 1)
                elif kind == "conv":
                    for b in range(4):
                        act.wait_ge(conv_done, b + 1)
                        square(blk(OT + 4 + b), blk(SQ + 4 + b), osq_done)
                elif kind == "mixnorm":
                    for j in range(2):
                        act.wait_ge(rstd_ready, 3 + j)
                        empty(AT[s + (j,)], std[:, :], ACT.Sqrt, scale=1.0 / 512, bias=eps_c[:, 0:1])
                elif kind == "wq":
                    for j in range(KC):
                        while k_hi <= min(first_wq + j + 1, NSPLIT - 1):
                            for b in range(2):
                                high_slot(k_hi, b, SLOT_OF_SPLIT[k_hi])
                            k_hi += 1
                        empty(AT[s + (j,)], blk(QP + j))
                elif kind == "route":
                    for n in range(2):
                        high_u(n, n, True)
                    for x in range(4):
                        i, first = x // 2, 4 * (x % 2)
                        act.wait_ge(key_done, x + 1)
                        banks = psum[:, 2 + 2 * (x % 2):4 + 2 * (x % 2), :]
                        nc.scalar.activation(scores_of(i)[:, :, first:first + 4, :],
                                             banks.rearrange("p m (j k) -> p m j k", j=4), ACT.Copy)\
                            .then_inc(key_read, 1)

            def gelu(s, n):
                act.wait_ge(act_done, n + 1)
                nc.scalar.activation(arena[:, n, :], psum[:, UBANKS[s % 4], 0:T], ACT.Gelu_apprx_tanh)\
                    .then_inc(act_read, 1)

            def u_loop(a, b):
                with act.Fori(a // 4, b // 4) as it:
                    for s in range(4):
                        high_u(s, it * 4 + s, False)
                        gelu(s + 2, it * 4 + s - 2)

            act.wait_ge(key_done, 4)
            for s in range(4):
                if s >= 2:
                    high_u(s, s, False)
                    gelu(s + 2, s - 2)
            u_loop(4, SOFT_TILE)
            act.wait_ge(topk_step, SOFT_STEP)
            nc.scalar.activation(blk(106), blk(106), ACT.Exp).then_inc(soft_exp, 1)
            u_loop(SOFT_TILE, POOL_TILES + COPY_LAG)
            act.wait_ge(sel_done, 1)

            def copy_quad(s, q, more):
                if s % 2 == 0 and more is not None:
                    act.wait_ge(spilled[s // 2], 16 * more)
                act.wait_ge(route_done, q + 1)
                dst = stage[:, s // 2, :, 4 * (s % 2):4 * (s % 2) + 4, :].rearrange("p r t g -> p t r g")
                src = psum[:, 2 + s, :].rearrange("p (t r g) -> p t r g", t=4, r=GROUPS)
                nc.scalar.activation(dst, src, ACT.Copy).then_inc(g_read, 1)

            first = POOL_TILES + COPY_LAG
            for s in range(4):
                high_u(s, first + s, False)
                gelu(s + 2, first + s - 2)
                copy_quad(s, s, None)
            with act.Fori(first // 4 + 1, (first + QUADS) // 4) as it:
                for s in range(4):
                    high_u(s, it * 4 + s, False)
                    gelu(s + 2, it * 4 + s - 2)
                    copy_quad(s, it * 4 + s - first, it - first // 4)
            u_loop(first + QUADS, P)
            for s in range(2):
                gelu(s + 2, P - 2 + s)

            def high_v(s, n, first):
                for b in range(2):
                    act.wait_ge(slot_in[(NSLOT + P + s) % RING], slot_count(NSLOT + P + s, n - s))
                    if first:
                        act.wait_ge(*((half_used, NHALF + P + n - 1), (act_done, P + n - 1))[b])
                    elif b:
                        act.wait_ge(y_done, n - 1)
                    else:
                        act.wait_ge(half_used, NHALF + P + n - 1)
                    at = b * HSLOT
                    high((2 * (NSPLIT + P + s) + b) % 4, ring[:, (NSLOT + P + s) % RING, at:at + HSLOT])

            def high_act(s, n, count, first):
                act.wait_ge(weighted, count)
                if first:
                    act.wait_ge(act_done, P)
                else:
                    act.wait_ge(y_done, n - 3)
                nc.scalar.activation(h_hi[:, s, :], arena[:, n, :], ACT.Copy).then_inc(act_hi, 1)

            for s in range(4):
                high_v(s, s, s < 2)
                high_act(s, s, s // 2 + 1, True)
            with act.Fori(1, P // 4) as it:
                for s in range(4):
                    high_v(s, it * 4 + s, False)
                    high_act(s, it * 4 + s, it * 2 + s // 2 + 1, False)

            act.wait_ge(y_done, P)
            for c in range(KC):
                act.wait_ge(x_ready, KC + c + 1)
                square(xres[:, c, :], blk(SQ + c), squared)
            act.wait_ge(rstd_ready, 6)
            empty(AT[("norm", 4, "ssq")], std[:, :], ACT.Sqrt, scale=1.0 / D, bias=eps_c[:, 0:1])

        @block.gpsimd
        def _(pool):
            def low(k, half, src, hi_value, done):
                pool.wait_ge(hi_done, hi_value)
                nc.gpsimd.tensor_tensor(w_lo[:, half, :], src, w_hi[:, half, :].bitcast(F32), ALU.subtract)\
                    .then_inc(done, 1)

            def load_mod(m):
                if m >= 2:
                    pool.wait_ge(mod_done, m - 1)
                pool.dma_start(flat(MODR[m // 24] + 4 * (m % 2), 4), mods[m]).then_inc(mod_in[m % 2], 16)

            k_lo = 0
            for s in STEPS:
                kind = s[0]
                while k_lo <= ahead(s):
                    src = ring[:, SLOT_OF_SPLIT[k_lo] % RING, HSLOT:D]
                    low(k_lo, (2 * k_lo + 1) % 4, src, 2 * k_lo + 2, lo1_done)
                    k_lo += 1
                if kind == "small":
                    load_mod(0)
                    load_mod(1)
                elif kind == "mod" and s[1] + 2 < 24:
                    load_mod(s[1] + 2)
                elif kind == "bias" and s[1]:
                    pool.wait_ge(v_read, VT[("bias_row", 7)] + 1)
                    pool.dma_start(bias_dram, bias_rows).then_inc(sheet_in, 16)
                elif s == ("proj", "nq1"):
                    pool.wait_ge(sheet_in, 16)
                    pool.wait_ge(turn_done, 8)
                    skew = bass.AP(bias_dram.tensor, bias_dram.offset + P - 1,
                                   [[HEADS * TRI - 1, P], [TRI, HEADS], [1, T]])
                    pool.dma_start(sheet, skew).then_inc(sheet_in, 16)
                elif kind == "ple":
                    pool.wait_ge(a_done, filled("pv", 7))
                    for m in range(24, 48):
                        load_mod(m)
                elif kind == "proj" and s[1] in rope_blocks:
                    b = rope_blocks.index(s[1])
                    pool.wait_ge(small_in, 16 * 10)
                    pool.wait_ge(a_read, filled(*s))
                    nc.gpsimd.tensor_tensor(blk(QK + b), blk(RAW + b), cos_t, ALU.mult).then_inc(cos_done, 1)
                elif kind == "soft" and s[1] >= 4:
                    p = s[1]
                    if p < 8:
                        pool.wait_ge(inv_done, p + 1)
                    else:
                        pool.wait_ge(gated_done, p - 7)
                    for m in range(2):
                        for i in range(TT):
                            cols = slice(0, P) if i == 0 else slice(P, TRI)
                            n = 2 * m + i
                            e = ex_of(p)[:, m, cols]
                            last = nc.gpsimd.tensor_scalar(e, e, rsum[:, p % 2, n:n + 1], 1.0, ALU.mult, ALU.mult)
                    last.then_inc(probs_done, 1)
                elif kind == "norm" and s[1] == 1:
                    pool.wait_ge(x_ready, KC)
                    nc.gpsimd.memset(blk(BD, 3), 0.0).then_inc(zero_set, 1)
                elif kind == "conv":
                    for b in range(4):
                        pool.wait_ge(a_read, filled("proj", f"ch{b}"))
                        nc.gpsimd.tensor_tensor(blk(CONV + 4 + b), blk(CONV + 4 + b), blk(CONV + 8 + b), ALU.mult)\
                            .then_inc(z_done, 1)
                    for b in range(4):
                        pool.wait_ge(conv_step, 3 * b + 3)
                        nc.gpsimd.tensor_tensor(blk(OT + 4 + b), blk(PROD + b), blk(CONV + b), ALU.mult)\
                            .then_inc(conv_done, 1)
                elif kind == "mixnorm":
                    pool.wait_ge(masked_done, 8)
                    pool.wait_ge(rope_done, 16)
                    pool.dma_start(ring_keys, keys).then_inc(peer_in, 16)

            def low_tile(base, s, n, both):
                src = ring[:, (NSLOT + base + s) % RING, :]
                k = NSPLIT + base + s
                if both:
                    low(k, 2 * k % 4, src[:, 0:HSLOT], 2 * (NSPLIT + base + n) + 1, lo2_done)
                else:
                    pool.wait_ge(lo0_done, NSPLIT + base - POOL_TILES + n + 1)
                low(k, (2 * k + 1) % 4, src[:, HSLOT:D], 2 * (NSPLIT + base + n) + 2, lo1_done)

            with pool.Fori(0, POOL_TILES // 4) as it:
                for s in range(4):
                    low_tile(0, s, it * 4 + s, True)
            with pool.Fori(POOL_TILES // 4, (POOL_TILES + QUADS) // 4) as it:
                for s in range(4):
                    low_tile(0, s, it * 4 + s, False)
                    q = it * 4 + s - POOL_TILES
                    pool.wait_ge(hot2_ready, q + 1)
                    for x in (1, 2):
                        w = sel_w[x][:, bass.ds(q * 4, 4)].unsqueeze(2).to_broadcast([P, 4, P])
                        last = nc.gpsimd.tensor_tensor(wgt[x][:, s % 2, :, :], hot2[:, s % 2, :, :], w, ALU.mult)
                    last.then_inc(wgt_ready, 1)
            with pool.Fori((POOL_TILES + QUADS) // 4, P // 4) as it:
                for s in range(4):
                    low_tile(0, s, it * 4 + s, False)
            with pool.Fori(0, P // 4) as it:
                for s in range(4):
                    low_tile(P, s, it * 4 + s, False)

        @block.vector
        def _(dve):
            v = nc.vector

            def bc(ap, shape):
                return ap.to_broadcast(shape)

            def inverse(std_value, ready):
                dve.wait_ge(a_read, std_value)
                v.reciprocal(rstd[:, :], std[:, :]).then_inc(rstd_ready, 1)
                dve.wait_ge(rstd_ready, ready)

            def low(half, src, hi_value):
                dve.wait_ge(hi_done, hi_value)
                v.tensor_tensor(w_lo[:, half, :], src, w_hi[:, half, :].bitcast(F32), ALU.subtract)\
                    .then_inc(lo0_done, 1)

            def modulation(m):
                dve.wait_ge(mod_in[m % 2], 16 * (m // 2 + 1))
                dve.wait_ge(cact_ready, 2)
                if m:
                    dve.wait_ge(mod_done, m)
                v.tensor_tensor_reduce(junk, flat(MODR[m // 24] + 4 * (m % 2), 4), c_act, 1.0, pcol("b_mod", m),
                                       ALU.mult, ALU.add, mod[:, m:m + 1]).then_inc(mod_done, 1)

            def rope(b):
                n = VT[("rope", rope_blocks[b])]
                dve.wait_ge(v_done, n + 1)
                tmp = blk(SIG + b)
                v.tensor_tensor(tmp, vbuf(n), sin_t, ALU.mult).then_inc(v_read, 1)
                dve.wait_ge(v_read, n + 1)
                dve.wait_ge(cos_done, b + 1)
                v.tensor_tensor(blk(QK + b), blk(QK + b), tmp, ALU.add).then_inc(rope_done, 1)

            v.memset(ones[:, :], 1.0).then_inc(const_set, 1)
            v.memset(eps_c[:, 0:1], EPS)
            v.memset(eps_c[:, 1:2], SUBLN_EPS).then_inc(const_set, 1)

            k_lo, ropes = 0, []
            for s in STEPS:
                kind = s[0]
                while ropes and not (kind == "mod" or kind == "proj" and s[1] in rope_blocks):
                    rope(ropes.pop(0))
                while k_lo <= ahead(s):
                    low(2 * k_lo % 4, ring[:, SLOT_OF_SPLIT[k_lo] % RING, 0:HSLOT], 2 * k_lo + 1)
                    k_lo += 1
                if kind == "small":
                    dve.wait_ge(small_in, 16 * 10)
                    for j in range(2):
                        a, b = pcol("lam", 128 * j, 64), pcol("lam", 128 * j + 64, 64)
                        v.tensor_tensor_reduce(s_sb[:, 2048 + 64 * j:2112 + 64 * j], a, b, 1.0, 0.0, ALU.mult, ALU.add,
                                               small[:, j:j + 1]).then_inc(lam_step, 1)
                    dve.wait_ge(cact_ready, 1)
                    v.tensor_tensor(small[:, 4:5], small[:, 3:4], small[:, 2:3], ALU.subtract).then_inc(lam_step, 1)
                    dve.wait_ge(lam_step, 3)
                    v.tensor_scalar(small[:, 5:6], small[:, 4:5], -LAM_INIT, None, ALU.add).then_inc(lam_step, 1)
                    v.tensor_scalar(small[:, 6:7], pcol("subln_g"), 1.0 - LAM_INIT, None, ALU.mult).then_inc(lam_step, 1)
                elif kind == "bias":
                    dve.wait_ge(mod_done, 48)
                    for hd in range(4 * s[1], 4 * s[1] + 4):
                        n = VT[("bias_row", hd)]
                        dve.wait_ge(v_done, n + 1)
                        v.tensor_copy(bias_rows[:, hd, :], psum[:, 2 + n % 4, 0:TRI]).then_inc(v_read, 1)
                    if s[1]:
                        dve.wait_ge(o_ready, 4)
                        v.memset(flat(CBIAS, 2), NEG).then_inc(const_set, 1)
                        dve.wait_ge(const_set, 3)
                        dve.wait_ge(rel_done, 1)
                        for i in range(TT):
                            src = psum[:, 7, 8 * (1 - i) * HEADS:(8 * (1 - i) + CMP_N) * HEADS]
                            last = v.tensor_copy(cbias[:, i, :, 0:CMP_N], src.rearrange("p (n h) -> p h n", h=HEADS))
                        last.then_inc(cmp_vec, 1)
                elif kind == "norm":
                    k = s[1]
                    if k == 0:
                        dve.wait_ge(x_in, 32)
                    if k >= 2:
                        dve.wait_ge(mod_done, 24 * (k - 1))
                        at = (8, 32)[k - 2]
                        v.scalar_tensor_tensor(gm[:, k - 2, :], mod[:, at:at + 8], 1.0,
                                               pcol(("ln_mix_g", "ln_ffn_g")[k - 2], 0, 8), ALU.add, ALU.mult)\
                            .then_inc(mod_ready, 1)
                        dve.wait_ge(mod_ready, k - 1)
                    if k == 1:
                        dve.wait_ge(h_ready, 8)
                        dve.wait_ge(x_ready, 8)
                        dve.wait_ge(a_done, filled("gate", KC - 1))
                    if k == 2:
                        dve.wait_ge(x1_ready, 8)
                    if k == 3:
                        dve.wait_ge(o_ready, 12)
                    inverse(filled(*s, "ssq"), {0: 1, 1: 2, 2: 3, 3: 6}[k])
                    if k == 1:
                        for c in range(KC):
                            v.scalar_tensor_tensor(xres[:, c, :], blk(MERGED + c), pcol("final_g", c), rstd[:, :],
                                                   ALU.mult, ALU.mult).then_inc(x1_ready, 1)
                        continue
                    first = {0: 0, 2: 8, 3: 16}[k]
                    for c in range(KC + 1):
                        if c < KC:
                            t = blk(NTMP + c)
                            gain = pcol("norm_g", c) if k == 0 else gm[:, k - 2, c:c + 1]
                            ins = v.scalar_tensor_tensor(t, xres[:, c, :], gain, rstd[:, :], ALU.mult, ALU.mult)
                            if k:
                                ins.then_inc(shift_in, 1)
                                sh = (0 if k == 2 else 24) + c
                                dve.wait_ge(shift_in, KC * (k - 2) + c + 1)
                                ins = v.tensor_scalar(t, t, mod[:, sh:sh + 1], None, ALU.add)
                            ins.then_inc(t_ready, 1)
                        if c:
                            dve.wait_ge(th_done, first + c)
                            v.tensor_tensor(h_lo[:, c - 1, :], blk(NTMP + c - 1), h_hi[:, c - 1, :].bitcast(F32),
                                            ALU.subtract).then_inc(h_ready, 1)
                elif kind == "mod":
                    modulation(s[1])
                elif kind == "proj" and s[1] in ("dv", "mv"):
                    rows = flat(DV if s[1] == "dv" else MV, 4).rearrange("p (i n) -> p i n", i=TT)
                    for j in range(4):
                        n = VT[s + (j,)]
                        dve.wait_ge(v_done, n + 1)
                        v.tensor_copy(rows[:, j // 2, (j % 2) * T:(j % 2) * T + T], vbuf(n)).then_inc(v_read, 1)
                elif kind == "proj" and s[1] in rope_blocks:
                    ropes.append(rope_blocks.index(s[1]))
                    if len(ropes) > 1:
                        rope(ropes.pop(0))
                elif kind == "scores":
                    p = s[1]
                    dve.wait_ge(scores_done, p + 1)
                    if p >= 2:
                        dve.wait_ge(exp_done, 4 * (p - 1))
                    sc = sc_of(p)
                    if p < 8:
                        m3 = bc(mask.unsqueeze(1), [P, 2, TRI])
                        v.scalar_tensor_tensor(sc, scb(p), SCALE, m3, ALU.mult, ALU.add).then_inc(masked_done, 1)
                    else:
                        if p == 8:
                            dve.wait_ge(sheet_in, 32)
                        j = (p - 8) // 2
                        bias = sheet[:, j:j + 5:4, :]
                        v.scalar_tensor_tensor(sc[:, :, 0:P], scb(p)[:, :, 0:P], SCALE, bias[:, :, P:T], ALU.mult, ALU.add)
                        v.scalar_tensor_tensor(sc[:, :, P:TRI], scb(p)[:, :, P:TRI], SCALE, bias, ALU.mult, ALU.add)\
                            .then_inc(masked_done, 1)
                    dve.wait_ge(masked_done, p + 1)
                    nm = nmax[:, p % 2, :].rearrange("p (m i) -> p m i", m=2)
                    v.tensor_reduce(nm[:, :, 0], sc[:, :, 0:P], AX, ALU.max, negate=True).then_inc(max_done, 1)
                    v.tensor_reduce(nm[:, :, 1], sc[:, :, P:TRI], AX, ALU.max, negate=True).then_inc(max_done, 1)
                elif kind == "soft":
                    p = s[1]
                    dve.wait_ge(exp_done, 4 * p + 4)
                    rs = rsum[:, p % 2, :]
                    if p >= 2:
                        dve.wait_ge(probs_done, p - 1)
                    v.reciprocal(rs, sums[:, p % 2, :]).then_inc(inv_done, 1)
                    dve.wait_ge(inv_done, p + 1)
                    if p < 4:
                        e = ex_of(p)
                        v.tensor_scalar(rs[:, 2:4], rs[:, 2:4], small[:, 5:6], None, ALU.mult).then_inc(lam_scaled, 1)
                        for i in range(TT):
                            cols = slice(0, P) if i == 0 else slice(P, TRI)
                            v.tensor_scalar(e[:, 0, cols], e[:, 0, cols], rs[:, i:i + 1], None, ALU.mult)\
                                .then_inc(map0_done, 1)
                        dve.wait_ge(lam_scaled, p + 1)
                        dve.wait_ge(map0_done, 2 * p + 2)
                        for i in range(TT):
                            cols = slice(0, P) if i == 0 else slice(P, TRI)
                            last = v.scalar_tensor_tensor(e[:, 0, cols], e[:, 1, cols], rs[:, 2 + i:3 + i], e[:, 0, cols],
                                                          ALU.mult, ALU.add)
                        last.then_inc(probs_done, 1)
                    elif p >= 8:
                        j, br = (p - 8) // 2, 1 + p % 2
                        g = gsig[:, :, :].rearrange("p i (h b) -> p h i b", b=3)[:, j:j + 5:4, :, br]
                        dve.wait_ge(a_read, filled("proj", "gt", TT - 1))
                        rr = rs.rearrange("p (m i) -> p m i", m=2)
                        v.tensor_tensor(rr, rr, g, ALU.mult).then_inc(gated_done, 1)
                elif kind == "pv" and 4 <= s[1] < 8:
                    p = s[1]
                    dve.wait_ge(a_read, filled(*s))
                    dve.wait_ge(gates_ready, 1)
                    v.tensor_tensor(blk(OT + p), blk(OT + p), blk(SIL + p), ALU.mult).then_inc(o_ready, 1)
                elif kind == "subln":
                    for hd in range(4):
                        dve.wait_ge(a_read, filled(*s, hd // 2))
                        v.reciprocal(blk(SQ + hd), blk(SQ + hd)).then_inc(sub_done, 1)
                        dve.wait_ge(sub_done, 3 * hd + 1)
                        v.scalar_tensor_tensor(blk(OT + hd), blk(OT + hd), small[:, 6:7], blk(SQ + hd), ALU.mult, ALU.mult)\
                            .then_inc(sub_done, 1)
                        dve.wait_ge(sub_done, 3 * hd + 2)
                        v.tensor_tensor(blk(OT + hd), blk(OT + hd), blk(SIL + hd), ALU.mult).then_inc(sub_done, 1)
                elif kind == "merge":
                    dve.wait_ge(gates_ready, 3)
                    for nb in range(KC):
                        na, nb_ = VT[s + (2 * nb,)], VT[s + (2 * nb + 1,)]
                        m_, sa, sb_ = blk(MERGED + nb), blk(SIG + nb), blk(SIG + 8 + nb)
                        dve.wait_ge(v_done, na + 1)
                        v.tensor_tensor(m_, vbuf(na), sa, ALU.mult).then_inc(v_read, 1)
                        dve.wait_ge(v_done, nb_ + 1)
                        v.tensor_tensor(sb_, vbuf(nb_), sb_, ALU.mult).then_inc(v_read, 1)
                        dve.wait_ge(v_read, nb_ + 1)
                        v.tensor_tensor(m_, m_, sb_, ALU.add).then_inc(merged_ready, 1)
                        modulation(24 + nb)
                elif kind == "out1":
                    for nb in range(KC):
                        n = VT[s + (nb,)]
                        dve.wait_ge(v_done, n + 1)
                        v.tensor_tensor(xres[:, nb, :], vbuf(n), xres[:, nb, :], ALU.add).then_inc(v_read, 1)
                        modulation(32 + nb)
                elif kind == "gate":
                    for nb in range(KC):
                        dve.wait_ge(a_read, filled(*s, nb))
                        v.tensor_tensor(blk(PLE + nb), blk(PLE + nb), blk(SIG + nb), ALU.mult).then_inc(ple_step, 1)
                        modulation(40 + nb)
                        dve.wait_ge(ple_step, nb + 1)
                        v.tensor_tensor(blk(MERGED + nb), xres[:, nb, :], blk(PLE + nb), ALU.add).then_inc(x_ready, 1)
                elif kind == "cmps":
                    dve.wait_ge(cmp_step, 1)
                    dve.wait_ge(cmp_vec, 1)
                    for g in range(2):
                        src = psum[:, 6 + g, 0:T].rearrange("p (i c) -> p i c", i=TT)
                        b = cbias[:, :, 4 * g:4 * g + 4, :].rearrange("p i h n -> p i (h n)")
                        last = v.scalar_tensor_tensor(csc[:, :, g, :], src, SCALE, b, ALU.mult, ALU.add)
                    last.then_inc(cmp_vec, 1)
                    dve.wait_ge(cmp_vec, 2)
                    maps = flat(CSC, 2).rearrange("p (k n) -> p k n", n=CMP_PAD)
                    v.tensor_reduce(cst1[:, 0, :], maps, AX, ALU.max).then_inc(cmp_vec, 1)
                    dve.wait_ge(cmp_vec, 3)
                    v.tensor_tensor(maps, maps, bc(cst1[:, 0, :].unsqueeze(2), [P, 16, CMP_PAD]), ALU.subtract)\
                        .then_inc(cmp_vec, 1)
                    dve.wait_ge(cmp_exp, 1)
                    v.tensor_reduce(cst1[:, 1, :], maps, AX, ALU.add).then_inc(cmp_vec, 1)
                    dve.wait_ge(cmp_vec, 5)
                    v.reciprocal(cst1[:, 2, :], cst1[:, 1, :]).then_inc(cmp_vec, 1)
                    dve.wait_ge(cmp_vec, 6)
                    for i in range(TT):
                        g = gsig[:, i, :].rearrange("p (h b) -> p h b", b=3)[:, :, 0]
                        dve.wait_ge(a_read, filled("proj", "gt", TT - 1))
                        last = v.scalar_tensor_tensor(cst1[:, 1, 8 * i:8 * i + 8], cst1[:, 2, 8 * i:8 * i + 8],
                                                      valid[:, i:i + 1], g, ALU.mult, ALU.mult)
                    last.then_inc(cmp_vec, 1)
                    dve.wait_ge(cmp_vec, 7)
                    v.tensor_tensor(maps, maps, bc(cst1[:, 1, :].unsqueeze(2), [P, 16, CMP_PAD]), ALU.mult)\
                        .then_inc(cmp_vec, 1)
                elif kind == "conv":
                    for b in range(4):
                        dve.wait_ge(z_done, b + 1)
                        z, y = blk(CONV + 4 + b), blk(PROD + b)
                        w = [pcol("conv_w", 4 * k + b) for k in range(3)]
                        v.tensor_scalar(y, z, w[2], None, ALU.mult).then_inc(conv_step, 1)
                        dve.wait_ge(conv_step, 3 * b + 1)
                        v.scalar_tensor_tensor(y[:, 1:T], z[:, 0:T - 1], w[1], y[:, 1:T], ALU.mult, ALU.add)\
                            .then_inc(conv_step, 1)
                        dve.wait_ge(conv_step, 3 * b + 2)
                        v.scalar_tensor_tensor(y[:, 2:T], z[:, 0:T - 2], w[0], y[:, 2:T], ALU.mult, ALU.add)\
                            .then_inc(conv_step, 1)
                elif kind == "mixnorm":
                    for j in range(2):
                        if j:
                            dve.wait_ge(o_ready, 8)
                        inverse(filled(*s, j), 4 + j)
                        for c in range(4):
                            g = pcol(("attn_g", "conv_g")[j], c)
                            o = blk(OT + 4 * j + c)
                            v.scalar_tensor_tensor(o, o, g, rstd[:, :], ALU.mult, ALU.mult).then_inc(o_ready, 1)
                elif kind == "out2":
                    for nb in range(KC):
                        n = VT[s + (nb,)]
                        dve.wait_ge(v_done, n + 1)
                        v.scalar_tensor_tensor(xres[:, nb, :], vbuf(n), mod[:, 16 + nb:17 + nb], xres[:, nb, :],
                                               ALU.mult, ALU.add).then_inc(v_read, 1)

            def best16(pieces, values, index):
                for s_, v_ in zip(pieces, values):
                    last = v.max(v_[:, 0:8], s_)
                last.then_inc(topk_step, 1)
                yield
                for s_, v_, i_ in zip(pieces, values, index):
                    v.max_index(i_[:, 0:8], v_[:, 0:8], s_)
                for s_, v_ in zip(pieces, values):
                    last = v.match_replace(s_, v_[:, 0:8], s_, LOWEST)
                last.then_inc(topk_step, 1)
                yield
                for s_, v_ in zip(pieces, values):
                    last = v.max(v_[:, 8:16], s_)
                last.then_inc(topk_step, 1)
                yield
                for s_, v_, i_ in zip(pieces, values, index):
                    last = v.max_index(i_[:, 8:16], v_[:, 8:16], s_)
                last.then_inc(topk_step, 1)
                yield

            for i in range(TT):
                dve.wait_ge(key_read, 2 * i + 2)
                at = TILE_STEPS * i
                mh = [(m, hd) for m in range(2) for hd in range(HEADS)]
                for _ in best16([scores_of(i)[:, m, hd, :] for m, hd in mh], [top_v[:, m, hd, :] for m, hd in mh],
                                [top_i[:, m, hd, :] for m, hd in mh]):
                    at += 1
                    dve.wait_ge(topk_step, at)
                v.tensor_copy(top_f[:, :, :, :], top_i[:, :, :, :])
                n = 2 * HEADS * NKEYS
                cand = s_sb[:, n * i:n * i + n].rearrange("p (h a b) -> p h a b", h=HEADS, a=TOPK)
                v.tensor_tensor(cand, bc(top_v[:, 0, :, :].unsqueeze(3), [P, HEADS, TOPK, TOPK]),
                                bc(top_v[:, 1, :, :].unsqueeze(2), [P, HEADS, TOPK, TOPK]), ALU.add)\
                    .then_inc(topk_step, 1)
                at += 1
                dve.wait_ge(topk_step, at)
                cands = s_sb[:, n * i:n * i + n].rearrange("p (h c) -> p h c", h=HEADS)
                for _ in best16([cands[:, hd, :] for hd in range(HEADS)], [best_v[:, i, hd, :] for hd in range(HEADS)],
                                [best_i[:, hd, :] for hd in range(HEADS)]):
                    at += 1
                    dve.wait_ge(topk_step, at)
                v.tensor_single_scalar(best_p[:, 0, :, :], best_i[:, :, :], 4, ALU.logical_shift_right)
                v.tensor_single_scalar(best_p[:, 1, :, :], best_i[:, :, :], 15, ALU.bitwise_and).then_inc(topk_step, 1)
                dve.wait_ge(topk_step, at + 1)
                v.tensor_copy(best_f[:, :, :, :], best_p[:, :, :, :]).then_inc(topk_step, 1)
                dve.wait_ge(topk_step, at + 2)
                dve.wait_ge(key_done, 4)
                for k in range(2):
                    v.tensor_tensor(cmp_of(k), bc(best_f[:, k, :, :].unsqueeze(3), [P, HEADS, TOPK, TOPK]),
                                    bc(iota[:, 0:TOPK].unsqueeze(1).unsqueeze(1), [P, HEADS, TOPK, TOPK]), ALU.is_equal)\
                        .then_inc(picked, 1)
                for k in range(2):
                    dve.wait_ge(picked, 4 * i + k + 1)
                    v.tensor_tensor(cmp_of(k), cmp_of(k), bc(top_f[:, k, :, :].unsqueeze(2), [P, HEADS, TOPK, TOPK]),
                                    ALU.mult).then_inc(picked, 1)
                for k in range(2):
                    dve.wait_ge(picked, 4 * i + k + 3)
                    last = v.tensor_reduce(sel[:, i, k, :].rearrange("p (h k) -> p h k", h=HEADS), cmp_of(k), AX, ALU.add)
                last.then_inc(topk_step, 1)
                dve.wait_ge(topk_step, at + 3)
            low_u = lambda s, n: low(2 * (NSPLIT + s) % 4, ring[:, (NSLOT + s) % RING, 0:HSLOT], 2 * (NSPLIT + n) + 1)
            at = 2 * TILE_STEPS
            best = best_v[:, :, :, :].rearrange("p i h k -> p (i h) k")
            v.tensor_copy(gsum[:, 0, :], best[:, :, 0]).then_inc(topk_step, 1)
            dve.wait_ge(topk_step, at + 1)
            v.tensor_tensor(best, best, bc(gsum[:, 0, :].unsqueeze(2), [P, TT * HEADS, TOPK]), ALU.subtract)\
                .then_inc(topk_step, 1)
            dve.wait_ge(soft_exp, 1)
            v.tensor_reduce(gsum[:, 1, :], best, AX, ALU.add).then_inc(topk_step, 1)
            dve.wait_ge(topk_step, at + 3)
            v.reciprocal(gsum[:, 2, :], gsum[:, 1, :]).then_inc(topk_step, 1)
            dve.wait_ge(topk_step, at + 4)
            for i in range(TT):
                last = v.tensor_tensor(sel[:, i, 2, :].rearrange("p (h k) -> p h k", h=HEADS), best_v[:, i, :, :],
                                       bc(gsum[:, 2, HEADS * i:HEADS * i + HEADS].unsqueeze(2), [P, HEADS, TOPK]), ALU.mult)
            last.then_inc(topk_step, 1)
            dve.wait_ge(sel_done, 1)
            v.tensor_copy(sel_1[:, :], psum[:, 4, 0:T])
            v.tensor_copy(sel_2[:, :], psum[:, 4, T:2 * T])
            v.tensor_copy(sel_w[0], psum[:, 5, 0:T]).then_inc(sel_read, 1)
            dve.wait_ge(sel_read, 1)
            for x, whole in enumerate((psum[:, 5, 0:T], rest[0])):
                v.tensor_tensor(rest[x], whole, sel_w[x], ALU.subtract).then_inc(sel_read, 1)
                dve.wait_ge(sel_read, 2 * x + 2)
                v.tensor_copy(sel_w[x + 1], rest[x]).then_inc(sel_read, 1)
                dve.wait_ge(sel_read, 2 * x + 3)

            def one_hots(s, q, first):
                def of(x):
                    return bc(x[:, bass.ds(q * 4, 4)].unsqueeze(2), [P, 4, P])

                if not first:
                    dve.wait_ge(route_done, q - 1)
                columns = bc(iota[:, :].unsqueeze(1), [P, 4, P])
                v.tensor_tensor(hot2[:, s % 2, :, :], columns, of(sel_2), ALU.is_equal).then_inc(hot2_ready, 1)
                v.tensor_tensor(hot1[:, s % 2, :, :], columns, of(sel_1), ALU.is_equal).then_inc(hot1_ready, 1)
                dve.wait_ge(hot2_ready, q + 1)
                v.tensor_tensor(wgt[0][:, s % 2, :, :], hot2[:, s % 2, :, :], of(sel_w[0]), ALU.mult)\
                    .then_inc(wgt0_ready, 1)

            for s in range(4):
                low_u(s, POOL_TILES + s)
                one_hots(s, s, s < 2)
            with dve.Fori(POOL_TILES // 4 + 1, (POOL_TILES + QUADS) // 4) as it:
                for s in range(4):
                    low_u(s, it * 4 + s)
                    one_hots(s, it * 4 + s - POOL_TILES, False)
            with dve.Fori((POOL_TILES + QUADS) // 4, P // 4 - 2) as it:
                for s in range(4):
                    low_u(s, it * 4 + s)

            def weigh(j, k):
                dve.wait_ge(g_in, j * 16 + 16)
                a = arena[:, bass.ds(j * GRP + 2 * k, 2), :]
                v.tensor_tensor(a, a, g_back[:, 2 * k:2 * k + 2, :], ALU.mult).then_inc(weighted, 1)

            dve.wait_ge(act_read, GRP)
            for k in range(GRP // 2):
                low_u(k % 4, P - GRP // 2 + k)
                weigh(0, k)

            def low_v(s, n):
                low(2 * (NSPLIT + P + s) % 4, ring[:, (NSLOT + P + s) % RING, 0:HSLOT], 2 * (NSPLIT + P + n) + 1)
                dve.wait_ge(act_hi, n + 1)
                v.tensor_tensor(h_lo[:, s % 4, :], arena[:, n, :], h_hi[:, s % 4, :].bitcast(F32), ALU.subtract)\
                    .then_inc(act_lo, 1)

            dve.wait_ge(act_read, P)
            with dve.Fori(0, GROUPS - 1) as j:
                for s in range(GRP):
                    low_v(s, j * GRP + s)
                    if 4 <= s < 12:
                        weigh(j + 1, s - 4)
            for s in range(GRP):
                low_v(s, (GROUPS - 1) * GRP + s)

            dve.wait_ge(y_done, P)
            for nb in range(KC):
                v.scalar_tensor_tensor(xres[:, nb, :], psum[:, 2 + nb // 2, (nb % 2) * T:(nb % 2) * T + T],
                                       mod[:, 40 + nb:41 + nb], xres[:, nb, :], ALU.mult, ALU.add).then_inc(x_ready, 1)
            dve.wait_ge(x_ready, 2 * KC)
            inverse(filled("norm", 4, "ssq"), 7)
            for c in range(KC):
                v.scalar_tensor_tensor(blk(OUT + c), xres[:, c, :], pcol("ln_final_g", c), rstd[:, :], ALU.mult, ALU.mult)\
                    .then_inc(out_ready, 1)


def rel_bucket(dist):
    n = np.maximum(dist, 0)
    ratio = (np.log(np.maximum(n, 1).astype(np.float32) / np.float32(16)) / np.float32(np.log(8.0))).astype(np.float32)
    large = 16 + (ratio * np.float32(16)).astype(np.int32)
    return np.where(n < 16, n, np.minimum(large, 31))


def constants():
    c = np.zeros((P, NCST), np.float32)

    def put(name, a):
        c[:a.shape[0], CST[name][0]:CST[name][0] + a.shape[1]] = a

    put("ident", np.eye(P, dtype=np.float32))
    put("iota", np.tile(np.arange(P, dtype=np.float32), (P, 1)))
    inv = np.float32(500000.0) ** (-np.arange(0, 16, 2, dtype=np.float32) / np.float32(16))
    ang = np.arange(T, dtype=np.float32)[:, None] * inv[None, :]
    cos, sin = np.ones((P, T), np.float32), np.zeros((P, T), np.float32)
    swap = np.eye(P, dtype=np.float32)
    for base in (0, DH):
        for d in range(8):
            cos[base + d] = cos[base + 8 + d] = np.cos(ang[:, d])
            sin[base + d], sin[base + 8 + d] = -np.sin(ang[:, d]), np.sin(ang[:, d])
            a, b = base + d, base + 8 + d
            swap[a, a] = swap[b, b] = 0
            swap[a, b] = swap[b, a] = 1
    put("perm", swap)
    put("cos", cos)
    put("sin", sin)
    q, k = np.arange(P)[:, None], np.arange(T)[None, :]
    put("mask", np.concatenate([np.where(k[:, :P] <= q, 0, NEG), np.where(k <= q + P, 0, NEG)], 1).astype(np.float32))
    t = np.arange(TT)[None, :] * P + np.arange(P)[:, None]
    put("valid", (t >= 31).astype(np.float32))

    def one_hot(dist):
        o = np.zeros((33, dist.size), np.float32)
        o[rel_bucket(dist), np.arange(dist.size)] = 1
        o[32] = np.where(dist < 0, NEG, 0)
        return o

    put("rev", one_hot(255 - np.arange(TRI)))
    put("fwd", one_hot(np.arange(512) - 272))
    return c


def stream(x):
    w1, w2 = x["w_in"][0], x["w_in_2"][0]
    heads = [0, 4, 1, 5, 2, 6, 3, 7]
    at = np.cumsum([0, 512, 128, 128, 128, 128, 128, 128, 24, 512, 512, 512])

    def cols(w):
        return w.reshape(-1, P, w.shape[1]).transpose(1, 0, 2).reshape(P, -1)

    def head_rows(w):
        return w.reshape(8, DH, -1)[heads].reshape(512, -1)

    base1 = {"dq": 0, "dk": 512, "dg": 1536, "mq": 2048, "mk": 2560, "mg": 3584, "ga": 4096, "gb": 5120}
    nq = w2[:, :512].reshape(D, 8, DH)[:, heads].reshape(D, 512)
    wo2 = np.concatenate([head_rows(x["w_out_2"][0][:512]), x["w_out_2"][0][512:]])
    out = np.empty((NSLOT, P, D), np.float32)
    for n, (s, i) in enumerate(SLOTS):
        k, a = s[0], s[1] if len(s) > 1 else None
        if k == "proj" and a in ("dv", "mv"):
            v = cols(w1[:, 1024:1536] if a == "dv" else w1[:, 3072:3584])
            out[n] = v[:, i * D:i * D + D]
        elif k == "proj" and a == "nv":
            v = cols(np.concatenate([w2[:, at[4]:at[5]], w2[:, at[6]:at[7]]], 1))
            out[n] = v[:, i * D:i * D + D]
        elif k == "proj" and a == "gt":
            v = np.zeros((D, P), np.float32)
            v[:, 0:24] = w2[:, at[7]:at[8]]
            out[n] = cols(v)
        elif k == "proj" and a[:2] in base1:
            c = base1[a[:2]] + P * int(a[2:])
            out[n] = cols(w1[:, c:c + P])
        elif k == "proj" and a[:2] == "nq":
            out[n] = cols(nq[:, P * int(a[2:]):][:, :P])
        elif k == "proj" and a in ("kc", "vc", "ks", "kw"):
            c = at[{"kc": 1, "vc": 2, "ks": 3, "kw": 5}[a]]
            out[n] = cols(w2[:, c:c + P])
        elif k == "proj":
            c = at[{"cb": 8, "cc": 9, "ch": 10}[a[:2]]] + P * int(a[2:])
            out[n] = cols(w2[:, c:c + P])
        elif k == "ple":
            out[n] = np.concatenate([cols(x["w_ple"][0][:, P * j:P * j + P]) for j in range(4 * i, 4 * i + 4)], 1)
        elif k == "merge":
            w = x["w_branch_moba" if i % 2 else "w_branch_diff"][0]
            out[n] = np.concatenate([cols(w[:, P * j:P * j + P]) for j in (2 * (i // 2), 2 * (i // 2) + 1)], 1)
        elif k in ("cmpk", "cmpv"):
            w = x["cmp_wk1_2" if k == "cmpk" else "cmp_wv1_2"][0]
            out[n] = w.reshape(16, P, DH).transpose(1, 0, 2).reshape(P, D)
        else:
            w = {"out1": x["w_out"][0], "gate": x["w_ple_gate"][0], "out2": wo2, "wq": x["peer_wq_2"][0]}[k]
            out[n] = cols(w[:, P * i:P * i + P])
    return out


def kernel(**inputs):
    import concourse.bacc as bacc
    from concourse.bass_utils import run_bass_kernel_spmd

    x = {k: np.asarray(v) for k, v in inputs.items()}
    heads = [0, 4, 1, 5, 2, 6, 3, 7]

    def col(v):
        return np.asarray(v).reshape(-1, P).T

    par = np.zeros((P, NPAR), np.float32)
    rel = np.ones((33, 8), np.float32)
    rel[:32] = x["rel_table_2"]
    lam = np.concatenate([x[n][0] for n in ("lambda_q1", "lambda_k1", "lambda_q2", "lambda_k2")])
    for name, v in (("norm_g", col(x["norm_g"])), ("final_g", col(x["final_g"])), ("ln_mix_g", col(x["ln_mix_g_2"])),
                    ("ln_ffn_g", col(x["ln_ffn_g_2"])), ("ln_final_g", col(x["ln_final_g_2"])),
                    ("attn_g", col(x["norm_attn_g_2"].reshape(8, DH)[heads])), ("conv_g", col(x["norm_conv_g_2"])),
                    ("subln_g", col(x["subln_g"])), ("conv_w", col(x["conv_w_2"])), ("b_mod", col(x["b_mod_2"])),
                    ("lam", np.tile(lam, (P, 1))), ("rel", rel)):
        par[:v.shape[0], PAR[name][0]:PAR[name][1]] = v
    pe = np.zeros((2, P, T), np.float32)
    for w, n in enumerate(("cmp_pe_k_2", "cmp_pe_v_2")):
        pe[w, :, 0:32:2] = x[n][0].reshape(16, P).T
    arrays = {
        "x_t": x["x"][0].T.reshape(KC, P, T).transpose(1, 0, 2),
        "p_t": x["p"][0, 0].T.reshape(2, P, T).transpose(1, 0, 2),
        "params": par,
        "consts": constants(),
        "weights": stream(x),
        "c_rows": np.tile(x["c_2"], (P, 1)),
        "mods": x["w_mod_2"][0].T.reshape(48, P, D),
        "w2k": x["cmp_wk2_2"][0],
        "w2v": x["cmp_wv2_2"][0],
        "pe": pe,
        "keys": x["peer_keys_2"][0].transpose(1, 3, 0, 2).reshape(P, HEADS, NKEYS),
        "u_t": x["peer_u_2"][0].reshape(P, P, KC, P).transpose(1, 3, 2, 0).reshape(P, P, D),
        "v_rows": x["peer_v_2"][0].reshape(P, P, D).transpose(1, 0, 2),
    }
    nc = bacc.Bacc("TRN2", target_bir_lowering=False, num_devices=1)
    arrays = {k: np.ascontiguousarray(v) for k, v in arrays.items()}
    args = [nc.dram_tensor(k, v.shape, F32, kind="ExternalInput").ap() for k, v in arrays.items()]
    bias_dram = nc.dram_tensor("bias_rows", (P, HEADS, TRI), F32, kind="Internal").ap()
    g_dram = nc.dram_tensor("routing_weights", (P, GROUPS, T * GRP), F32, kind="Internal").ap()
    out_t = nc.dram_tensor("out_t", (KC, P, T), F32, kind="ExternalOutput").ap()
    names = list(arrays)
    block_program(nc, **dict(zip(names, args)), bias_dram=bias_dram, g_dram=g_dram, out_t=out_t)
    r = run_bass_kernel_spmd(nc, [arrays], core_ids=[0])
    return r.results[0]["out_t"].reshape(D, T).T.reshape(1, T, D)
```

```python
from contextlib import ExitStack

import numpy as np

import concourse.bass as bass
from concourse import mybir

F32 = mybir.dt.float32
F32R = mybir.dt.float32r
BF16 = mybir.dt.bfloat16
U32 = mybir.dt.uint32
ALU = mybir.AluOpType
ACT = mybir.ActivationFunctionType
AX = mybir.AxisListType.X

P = 128
T = 256
TT = T // P
D = 1024
KC = D // P
DH = 64
HEADS = 8
HALF = HEADS // 2
NKEYS = 128
TOPK = 16
NEG = -1e30
LOWEST = -3.0e38
LAM_INIT = 0.8 - 0.6 * float(np.exp(-0.3 * 0))
EPS, SUBLN_EPS = 1e-6, 1e-5
SCALE = DH ** -0.5
UBANKS = (0, 1, 6, 7)
SOFT_TILE, SEL_TILE = 40, 44
TILE_STEPS = 12
SOFT_STEP = 2 * TILE_STEPS + 2
TOPK_STEPS = SOFT_STEP + 3
CMP_N, CMP_PAD = (T - 32) // 16 + 1, 32
RING = 4
HSLOT = D // 2
TRI = P + T

FILL1 = [f"{n}{b}" for n, k in (("dg", 4), ("mg", 4), ("ga", 8), ("gb", 8)) for b in range(k)]
FILL2 = [f"{n}{b}" for b in range(4) for n in ("cb", "cc", "ch")]
FIRST1 = [f"{n}{b}" for n in ("dq", "dk") for b in range(4)] + ["dv"] \
    + [f"{n}{b}" for n in ("mq", "mk") for b in range(4)] + ["mv"]
FIRST2 = [f"nq{b}" for b in range(4)] + ["kc", "vc", "ks", "kw", "nv", "gt"]
SLOTS_OF = {"dv": 4, "mv": 4, "nv": 2}
ROWS = {"dv": (4, 512, T), "mv": (4, 512, T), "nv": (2, T, T)}


def plan():
    steps = [("norm", 0), ("small",)]
    fill, mod = list(FILL1), list(range(24))
    for n in FIRST1:
        steps += [("proj", n)]
        if n[0] == "m" and n != "mv":
            steps.append(("mod", mod.pop(0)))
    steps += [("scores", 0), ("scores", 1)]
    for p in range(8):
        steps += [("soft", p), ("proj", fill.pop(0))] + [("subh", p - 5)] * (p >= 5) + [("proj", fill.pop(0))]
        steps += [("mod", mod.pop(0)) for _ in range(2)]
        steps.append(("turn", p))
        if p + 2 < 8:
            steps.append(("scores", p + 2))
        steps += [("proj", fill.pop(0))]
        steps.append(("pv", p))
        if p == 4:
            steps.append(("subln",))
    steps += [("subh", 3), ("ple",), ("merge",), ("out1",), ("gate",)]
    steps += [("norm", 1), ("bias", 0), ("norm", 2), ("bias", 1)]
    steps += [("proj", n) for n in FIRST2]
    steps += [("scores", 8), ("gates",), ("scores", 9), ("cmpk",), ("cmpv",)]
    fill = list(FILL2)
    steps += [("proj", fill.pop(0)), ("cmpk1",), ("cmpv1",), ("proj", fill.pop(0)), ("cmps",)]
    steps += [("soft", 8), ("proj", fill.pop(0)), ("cmpt",)]
    for p in range(8, 16):
        steps.append(("turn", p))
        if p + 2 < 16:
            steps.append(("scores", p + 2))
        if p == 15:
            steps += [("mod", 47), ("mix", 0)]
        if p + 1 < 16:
            steps += [("soft", p + 1), ("proj", fill.pop(0)), ("mod", 32 + p)]
        if p in (10, 12):
            steps.append(("proj", fill.pop(0)))
        if p in (9, 11, 13, 14):
            steps.append(("conv", (p - 8) // 2))
        if p % 2 == 1:
            steps.append(("pv", p))
    steps += [("mix", 1), ("out2",), ("norm", 3), ("wq",), ("route",)]
    assert not mod and not fill
    order = []
    for s in steps:
        k = {"proj": SLOTS_OF.get(s[-1], 1), "ple": 2, "merge": 8, "out1": 8, "gate": 8,
             "cmpk": 1, "cmpv": 1, "out2": 8, "wq": 8}.get(s[0], 0)
        order += [(s, i) for i in range(k)]
    return steps, order


STEPS, SLOTS = plan()
NSLOT = len(SLOTS)
SLOT_AT = {}
for _n, (_s, _i) in enumerate(SLOTS):
    SLOT_AT.setdefault(_s, _n)
SPLIT = {_n: _k for _k, _n in enumerate(n for n, (s, _) in enumerate(SLOTS) if s[0] not in ("ple", "cmpk", "cmpv"))}
NSPLIT = len(SPLIT)
SLOT_OF_SPLIT = {_k: _n for _n, _k in SPLIT.items()}
POOL_TILES = 48
QUADS = T // 4
COPY_LAG = 4
GRP = 16
GROUPS = P // GRP

PAR = {}
_at = 0
for _name, _w in (("norm_g", 8), ("final_g", 8), ("ln_mix_g", 8), ("ln_ffn_g", 8), ("ln_final_g", 8),
                  ("attn_g", 4), ("conv_g", 4), ("subln_g", 1), ("conv_w", 12), ("b_mod", 48),
                  ("lam", 256), ("rel", 8)):
    PAR[_name] = (_at, _at + _w)
    _at += _w
NPAR = _at
CST = {}
_at = 0
for _name, _w in (("ident", P), ("perm", P), ("cos", T), ("sin", T), ("mask", TRI), ("iota", P),
                  ("valid", TT), ("rev", TRI), ("fwd", 512)):
    CST[_name] = (_at, _at + _w)
    _at += _w
NCST = _at


def block_program(nc, x_t, p_t, params, consts, weights, c_rows, mods, w2k, w2v, pe, keys, u_t, v_rows, bias_dram,
                  g_dram, out_t):
    with ExitStack() as ctx:
        def sb(name, shape, dt=F32):
            return ctx.enter_context(nc.sbuf_tensor(name, shape, dt))

        def sem(name):
            return ctx.enter_context(nc.semaphore(name))

        psum = ctx.enter_context(nc.psum_tensor("psum", [P, 8, 512], F32))
        arena = sb("arena", [P, P, T])
        ring = sb("ring", [P, RING, D])
        xres = sb("xres", [P, KC, T])
        w_hi = sb("w_hi", [P, 4, HSLOT], F32R)
        w_lo = sb("w_lo", [P, 4, HSLOT], F32R)
        h_hi = sb("h_hi", [P, KC, T], F32R)
        h_lo = sb("h_lo", [P, KC, T], F32R)
        s_sb = sb("s_sb", [P, TT * 2 * HEADS * NKEYS])
        par = sb("par", [P, NPAR])
        ident = sb("ident", [P, P])
        iota = sb("iota", [P, P])
        ones = sb("ones", [P, P])
        valid = sb("valid", [P, TT])
        mod = sb("mod", [P, 48])
        gm = sb("gm", [P, 2, KC])
        std = sb("std", [P, T])
        rstd = sb("rstd", [P, T])
        small = sb("small", [P, 64])
        nmax = sb("nmax", [P, 2, 4])
        sums = sb("sums", [P, 2, 4])
        rsum = sb("rsum", [P, 2, 4])
        gsig = sb("gsig", [P, TT, 24])
        cst1 = sb("cst1", [P, 3, 16])
        top_v = sb("top_v", [P, 2, HEADS, TOPK])
        gsum = sb("gsum", [P, 3, TT * HEADS])
        eps_c = sb("eps_c", [P, 2])

        def pcol(name, a=0, n=1):
            return par[:, PAR[name][0] + a:PAR[name][0] + a + n]

        def blk(a, n=1):
            return arena[:, a, :] if n == 1 else arena[:, a:a + n, :]

        def flat(a, n):
            return arena[:, a:a + n, :].rearrange("p a b -> p (a b)")

        QK, RAW, DV, MV, SIL, SIG, OT = 0, 16, 32, 36, 40, 48, 64
        SC, PT, EX, SQ, MERGED, PLE, PTOK, TAB, MSK, REL = 72, 78, 88, 94, 102, 110, 118, 120, 122, 124
        SHEET, NQ, KS, KW, KCW, VCW, NV, CONV = 0, 16, 20, 21, 22, 25, 28, 30
        CSC, CPT, CBIAS, BD, H1, PROD = 42, 44, 46, 48, 50, 52
        QP = 112
        MODR = MERGED, PT + 6
        OUT = 0
        GT = SQ + 7
        NTMP = SQ
        top_f = blk(104).rearrange("p (m h k) -> p m h k", m=2, h=HEADS)
        top_i = blk(105).bitcast(U32).rearrange("p (m h k) -> p m h k", m=2, h=HEADS)
        best_v = blk(106).rearrange("p (i h k) -> p i h k", i=TT, h=HEADS)
        best_p = blk(107).bitcast(U32).rearrange("p (m h k) -> p m h k", m=2, h=HEADS)
        best_f = blk(108).rearrange("p (m h k) -> p m h k", m=2, h=HEADS)
        best_i = blk(109)[:, 0:P].bitcast(U32).rearrange("p (h k) -> p h k", h=HEADS)
        sel = flat(100, 3).rearrange("p (i k j) -> p i k j", i=TT, k=3)
        cos_t, sin_t = blk(TAB), blk(TAB + 1)
        mask = flat(MSK, 2)[:, 0:TRI]
        rel_c = flat(REL, 4)[:, 0:TRI + 512]
        perm = flat(MSK, 2)[:, TRI:TRI + P]
        sheet = flat(SHEET, 8).rearrange("p (h j) -> p h j", h=HEADS)
        cbias = flat(CBIAS, 2).rearrange("p (i h n) -> p i h n", i=TT, h=HEADS)
        csc = flat(CSC, 2).rearrange("p (i g c) -> p i g c", i=TT, g=2)
        cpt = flat(CPT, 2).rearrange("p (g q) -> p g q", g=2)
        bd = flat(BD, 2).rearrange("p (g r d) -> p g r d", g=2, r=4)
        h1 = blk(H1)[0:DH, :].rearrange("p (w g n) -> p w g n", w=2, g=2)[:, :, :, 0:CMP_PAD]
        kct = blk(H1 + 1)[:, 0:CMP_PAD]
        pebias = blk(H1 + 1)[0:DH, 40:42]
        w2s = blk(H1 + 1)[0:DH, 64:192].rearrange("p (w d) -> p w d", w=2)
        junk = s_sb[:, 0:D]
        c_act = s_sb[:, 2560:2560 + D]

        def sc_of(p):
            return flat(SC + 3 * (p % 2), 3).rearrange("p (m c) -> p m c", m=2)

        def ex_of(p):
            return flat(EX + 3 * (p % 2), 3).rearrange("p (m c) -> p m c", m=2)

        def pt_of(p):
            return flat(PT + 3 * (p % 3), 3).rearrange("p (m c) -> p m c", m=2)

        bias_rows = flat(SC, 12).rearrange("p (h j) -> p h j", h=HEADS)

        def scores_of(i):
            n = 2 * HEADS * NKEYS
            return s_sb[:, n * i:n * i + n].rearrange("p (m h k) -> p m h k", m=2, h=HEADS)

        def cmp_of(k):
            return flat(P - 16 + 8 * k, 8).rearrange("p (h k a) -> p h k a", h=HEADS, k=TOPK)

        ring_keys = flat(120, 4).rearrange("p (h k) -> p h k", h=HEADS)
        def quads(a):
            return a.bitcast(BF16).rearrange("p (b t k) -> p b t k", b=2, t=4)

        hot1, hot2 = quads(flat(120, 2)), quads(s_sb[:, 0:512])
        wgt = [quads(flat(122 + 2 * x, 2)) for x in range(3)]
        sel_w = [s_sb[:, 512 + 128 * x:640 + 128 * x].bitcast(BF16) for x in range(3)]
        rest = [s_sb[:, 1024 + T * x:1024 + T * x + T] for x in range(2)]
        sel_1, sel_2 = std, rstd
        stage = s_sb[:, 2048:4096].rearrange("p (b r t g) -> p b r t g", b=2, r=GROUPS, t=8)
        g_back = s_sb[:, :].rearrange("p (t g) -> p g t", g=GRP)

        def win_of(which):
            return arena[:, (KCW, VCW)[which]:(KCW, VCW)[which] + 3, :]

        def abuf(n):
            return psum[:, n % 2, 0:T]

        def vbuf(n):
            return psum[:, 2 + n % 4, 0:T]

        def scb(p):
            return psum[:, 2 + 2 * (p % 2):4 + 2 * (p % 2), 0:TRI]

        turned = psum[:, 6:8, 0:TRI]

        x_in = sem("x_in")
        small_in = sem("small_in")
        sheet_in = sem("sheet_in")
        cmp_in = sem("cmp_in")
        peer_in = sem("peer_in")
        slot_in = [sem(f"slot_in{i}") for i in range(RING)]
        const_set = sem("const_set")
        zero_set = sem("zero_set")
        cact_ready = sem("cact_ready")
        lam_step = sem("lam_step")
        rel_read = sem("rel_read")
        rel_done = sem("rel_done")
        a_done = sem("a_done")
        a_read = sem("a_read")
        v_done = sem("v_done")
        v_read = sem("v_read")
        mod_in = [sem(f"mod_in{i}") for i in range(2)]
        mod_done = sem("mod_done")
        mod_ready = sem("mod_ready")
        hi_done = sem("hi_done")
        lo0_done = sem("lo0_done")
        lo1_done = sem("lo1_done")
        lo2_done = sem("lo2_done")
        half_used = sem("half_used")
        t_ready = sem("t_ready")
        th_done = sem("th_done")
        part_hi = sem("part_hi")
        part_lo = sem("part_lo")
        x1_ready = sem("x1_ready")
        squared = sem("squared")
        ssq1_done = sem("ssq1_done")
        std1_ready = sem("std1_ready")
        rstd_ready = sem("rstd_ready")
        h_ready = sem("h_ready")
        cos_done = sem("cos_done")
        sin_done = sem("sin_done")
        rope_done = sem("rope_done")
        scores_done = sem("scores_done")
        masked_done = sem("masked_done")
        max_done = sem("max_done")
        exp_done = sem("exp_done")
        inv_done = sem("inv_done")
        lam_scaled = sem("lam_scaled")
        map0_done = sem("map0_done")
        gated_done = sem("gated_done")
        probs_done = sem("probs_done")
        turn_done = sem("turn_done")
        pt_done = sem("pt_done")
        gates_ready = sem("gates_ready")
        osq_done = sem("osq_done")
        sub_done = sem("sub_done")
        o_ready = sem("o_ready")
        x_ready = sem("x_ready")
        merged_ready = sem("merged_ready")
        ple_step = sem("ple_step")
        cmp_step = sem("cmp_step")
        cmp_bias = sem("cmp_bias")
        cmp_exp = sem("cmp_exp")
        cmp_vec = sem("cmp_vec")
        z_done = sem("z_done")
        conv_step = sem("conv_step")
        conv_done = sem("conv_done")
        key_done = sem("key_done")
        key_read = sem("key_read")
        topk_step = sem("topk_step")
        picked = sem("picked")
        soft_exp = sem("soft_exp")
        act_done = sem("act_done")
        act_read = sem("act_read")
        sel_done = sem("sel_done")
        sel_read = sem("sel_read")
        hot2_ready = sem("hot2_ready")
        hot1_ready = sem("hot1_ready")
        wgt0_ready = sem("wgt0_ready")
        wgt_ready = sem("wgt_ready")
        route_done = sem("route_done")
        g_read = sem("g_read")
        spilled = [sem(f"spilled{i}") for i in range(2)]
        g_in = sem("g_in")
        weighted = sem("weighted")
        act_hi = sem("act_hi")
        act_lo = sem("act_lo")
        y_done = sem("y_done")
        fin_step = sem("fin_step")
        out_ready = sem("out_ready")
        stored = sem("stored")

        a_order, v_order = [], []
        for s in STEPS:
            k = s[0]
            if k == "norm":
                a_order += [s + ("ssq",)] if s[1] != 1 else []
            elif k == "proj" and s[1] in ("dv", "mv"):
                v_order += [s + (j,) for j in range(4)]
            elif k == "proj" and s[1] in ROWS:
                a_order += [s + (j,) for j in range(TT)]
            elif k == "proj":
                a_order += [s]
                if s[1] in FIRST1:
                    v_order += [("rope", s[1])]
            elif k in ("pv", "gates"):
                a_order += [s]
            elif k == "subln":
                a_order += [s + (j,) for j in range(2)]
            elif k in ("ple", "gate", "wq"):
                a_order += [s + (j,) for j in range(KC)]
            elif k in ("cmpk", "cmpv"):
                a_order += [s + (0,)]
            elif k in ("cmpk1", "cmpv1"):
                a_order += [(k[:4], 1)]
            elif k == "mix":
                a_order += [s]
            if k == "merge":
                v_order += [s + (j,) for j in range(2 * KC)]
            if k in ("out1", "out2"):
                v_order += [s + (j,) for j in range(KC)]
            if k == "bias":
                v_order += [("bias_row", 4 * s[1] + j) for j in range(4)]
        a_order.append(("norm", 4, "ssq"))
        AT = {s: n for n, s in enumerate(a_order)}
        rope_blocks = [n for n in FIRST1 if n[1] in "qk" and n[0] in "dm"]
        VT = {s: n for n, s in enumerate(v_order)}
        NA, NVB = len(a_order), len(v_order)
        NORM_BASE = {0: 0, 1: 8, 2: 16, 3: 24, 4: 32}

        def filled(*s):
            return AT[s] + 1

        def part_of(kind, c):
            return {"merge": (blk(OT + c), (sub_done, 3 * c + 3) if c < 4 else (o_ready, c - 3),
                              (a_done, filled("proj", "gb7"))),
                    "out1": (blk(MERGED + c), (merged_ready, c + 1), (v_done, VT["merge", 14 + c // 4] + 1)),
                    "gate": (xres[:, c, :], (v_read, VT["out1", c] + 1), (v_done, VT["out1", 7] + 1)),
                    "out2": (blk(OT + c), (o_ready, 4 + c + 1), (a_done, filled("proj", "ch3")))}[kind]

        PART_BASE = {"merge": 0, "out1": 8, "gate": 16, "out2": 24}

        def slot_of(n):
            return n % RING, 16 * (n // RING + 1)

        def slot_count(n, more):
            return 16 * (n // RING + 1) + (16 // RING) * more

        def freer(n):
            s, i = SLOTS[n]
            k = s[0]
            if k == "ple":
                return a_done, filled(*s, 4 * i + 3)
            return a_done, filled(*s, 0)

        half_free = {}
        n_half = 0
        for k in range(NSPLIT):
            s, i = SLOTS[SLOT_OF_SPLIT[k]]
            if s[0] == "merge":
                half_free[k, 0] = v_done, VT[s + (2 * i,)] + 1
                half_free[k, 1] = v_done, VT[s + (2 * i + 1,)] + 1
                continue
            last = i == SLOTS_OF.get(s[-1], 1) - 1 or s[0] != "proj"
            n_half += 1
            half_free[k, 0] = half_used, n_half
            if not last:
                n_half += 1
                half_free[k, 1] = half_used, n_half
            elif s[0] in ("wq", "gate"):
                half_free[k, 1] = a_done, filled(*s, i)
            elif s[0] in ("out1", "out2"):
                half_free[k, 1] = v_done, VT[s + (i,)] + 1
            elif s[1] in ("dv", "mv"):
                half_free[k, 1] = v_done, VT[s + (3,)] + 1
            elif s[1] in ROWS:
                half_free[k, 1] = a_done, filled(*s, TT - 1)
            else:
                half_free[k, 1] = a_done, filled(*s)
        NHALF = n_half

        first_wq = SPLIT[SLOT_AT[("wq",)]]
        first_2 = SPLIT[SLOT_AT[("proj", "nq0")]]
        WIDE = ("merge", "out1", "gate", "out2", "wq")

        def ahead(s):
            if s[0] == "soft":
                later = [x for x in STEPS[STEPS.index(s):] if x[0] == "proj"]
                return ahead(later[0]) if later else -1
            if s == ("scores", 9):
                return SPLIT[SLOT_AT[("proj", "cb0")]]
            if s == ("proj", "gt"):
                return SPLIT[SLOT_AT[s]]
            if s[0] == "small":
                return 1
            if s[0] == "norm":
                return first_2 if s[1] == 2 else -1
            if s[0] == "proj":
                return SPLIT[SLOT_AT[s]] + SLOTS_OF.get(s[1], 1)
            return -1

        def ahead_in(s, job):
            return min(SPLIT[SLOT_AT[s]] + job + 1, first_2 - 1 if s[0] == "gate" else NSPLIT - 1)

        block = ctx.enter_context(nc.Block())

        @block.sync
        def _(sp):
            def load_slot(n):
                if n >= RING:
                    if n - RING in SPLIT:
                        k = SPLIT[n - RING]
                        sp.wait_ge(lo0_done, k + 1)
                        sp.wait_ge(lo1_done, k + 1)
                    else:
                        who, value = freer(n - RING)
                        sp.wait_ge(who, value)
                sp.dma_start(ring[:, n % RING, :], weights[n]).then_inc(slot_in[n % RING], 16)

            sp.dma_start(xres[:, :, :], x_t).then_inc(x_in, 16)
            sp.dma_start(par[:, :], params).then_inc(x_in, 16)
            load_slot(0)
            load_slot(1)
            for name, dst in (("ident", ident[:, :]), ("iota", iota[:, :]), ("valid", valid[:, :]),
                              ("cos", cos_t), ("sin", sin_t), ("mask", mask), ("perm", perm)):
                sp.dma_start(dst, consts[:, CST[name][0]:CST[name][1]]).then_inc(small_in, 16)
            sp.dma_start(rel_c[0:33, :], consts[0:33, CST["rev"][0]:CST["fwd"][1]]).then_inc(small_in, 16)
            sp.dma_start(blk(PTOK, 2), p_t).then_inc(small_in, 16)
            sp.dma_start(c_act, c_rows).then_inc(small_in, 16)
            for n in range(2, RING):
                load_slot(n)
            first2 = SLOT_AT[("proj", "nq0")]
            for n in range(RING, NSLOT):
                if n == first2:
                    sp.wait_ge(x_ready, KC)
                    sp.dma_start(w2s[:, 0, :], w2k).then_inc(cmp_in, 16)
                    sp.dma_start(w2s[:, 1, :], w2v).then_inc(cmp_in, 16)
                    for w in range(2):
                        sp.dma_start(win_of(w)[:, 2, :], pe[w]).then_inc(cmp_in, 16)
                load_slot(n)

            def load_tile(src, base, s, n, waits):
                for who, value in waits:
                    sp.wait_ge(who, value)
                sp.dma_start(ring[:, (base + s) % RING, :], src[n]).then_inc(slot_in[(base + s) % RING], 16)

            for s in range(RING):
                k = NSPLIT - RING + s
                load_tile(u_t, NSLOT, s, s, ((lo0_done, k + 1), (lo1_done, k + 1)))
            spill_from = POOL_TILES + 2 * COPY_LAG
            with sp.Fori(1, spill_from // RING) as it:
                for s in range(RING):
                    n = it * RING + s
                    load_tile(u_t, NSLOT, s, n, ((lo1_done, NSPLIT + n - RING + 1),))
            with sp.Fori(spill_from // RING, (spill_from + QUADS) // RING) as it:
                for s in range(RING):
                    n = it * RING + s
                    load_tile(u_t, NSLOT, s, n, ((lo1_done, NSPLIT + n - RING + 1),))
                    if s % 2:
                        sp.wait_ge(g_read, n - spill_from + 1)
                        at = (it * 2 + s // 2 - spill_from // 2) * (8 * GRP)
                        sp.dma_start(g_dram[:, :, bass.ds(at, 8 * GRP)],
                                     stage[:, s // 2].rearrange("p r t g -> p r (t g)")).then_inc(spilled[s // 2], 16)

            def reload(j):
                sp.dma_start(s_sb[:, :], g_dram[:, j, :]).then_inc(g_in, 16)

            for n in range(spill_from + QUADS, P):
                load_tile(u_t, NSLOT, n % RING, n, ((lo1_done, NSPLIT + n - RING + 1),))
                if n == spill_from + QUADS:
                    for i in range(2):
                        sp.wait_ge(spilled[i], 16 * (QUADS // 4))
                    sp.wait_ge(route_done, QUADS)
                    reload(0)

            def load_v_group(j, more):
                for s in range(GRP):
                    n = j * GRP + s
                    load_tile(v_rows, NSLOT + P, s, n, ((lo1_done, NSPLIT + P + n - RING + 1),))
                    if s == 0 and more == 2:
                        sp.wait_ge(weighted, GRP // 2)
                        reload(1)
                    if s == GRP - 1 and more:
                        sp.wait_ge(weighted, j * (GRP // 2) + GRP)
                        reload(j + 2)

            load_v_group(0, 2)
            with sp.Fori(1, GROUPS - 2) as j:
                load_v_group(j, 1)
            with sp.Fori(GROUPS - 2, GROUPS) as j:
                load_v_group(j, 0)
            for c in range(KC):
                sp.wait_ge(out_ready, c + 1)
                sp.dma_start(out_t[c], blk(OUT + c)).then_inc(stored, 16)
            sp.wait_ge(stored, 16 * KC)

        @block.tensor
        def _(pe_):
            def slot_ready(n):
                i, value = slot_of(n)
                pe_.wait_ge(slot_in[i], value)
                return ring[:, i, :]

            def take_a(n):
                if n >= 2:
                    pe_.wait_ge(a_read, n - 1)
                return abuf(n)

            def take_v(n):
                if n >= 4:
                    pe_.wait_ge(v_read, n - 3)
                return vbuf(n)

            def mm(out, lhs, rhs, start, stop, **kw):
                return nc.tensor.matmul(out, lhs, rhs, start=start, stop=stop, **kw)

            def sum_squares(n, sq, chunks, ready):
                out = take_a(n)
                for c in range(chunks):
                    ready(c)
                    last = mm(out, ones[:, :], sq[:, c, :], c == 0, c == chunks - 1)
                last.then_inc(a_done, 1)

            def add_square(k, c):
                if k == 1:
                    if c == 0:
                        pe_.wait_ge(pt_done, 8)
                    out = psum[:, 6, 0:T]
                else:
                    n = AT[("norm", 3, "ssq")]
                    out = take_a(n) if c == 0 else abuf(n)
                pe_.wait_ge(squared, NORM_BASE[k] + c + 1)
                return mm(out, ones[:, :], blk(SQ + c), c == 0, c == KC - 1)

            def projection(n, slot, chunks, width, rhs, ready, take, done):
                w = slot_ready(slot)
                out = take(n)
                for c in range(chunks):
                    ready(c)
                    last = mm(out, w[:, width + c * P:width + c * P + P], rhs[:, c, :], c == 0, c == chunks - 1)
                last.then_inc(done, 1)

            def split_mms(out, half, at, rhs, first, last):
                w1, w0 = w_hi[:, half, at:at + P], w_lo[:, half, at:at + P]
                mm(out, w1, rhs[0], first, False)
                mm(out, w1, rhs[1], False, False)
                return mm(out, w0, rhs[0], False, last)

            def half_ready(k, b, low=None):
                pe_.wait_ge(hi_done, 2 * k + b + 1)
                who, value = low or ((lo0_done, lo1_done)[b], k + 1)
                pe_.wait_ge(who, value)
                return (2 * k + b) % 4

            def split_projection(n, k, ready, take=take_a, done=a_done):
                out = take(n)
                for b in range(2):
                    half = half_ready(k, b)
                    for c4 in range(4):
                        c = 4 * b + c4
                        ready(c)
                        last = split_mms(out, half, c4 * P, (h_hi[:, c, :], h_lo[:, c, :]), c == 0, c == KC - 1)
                    last.then_inc(done if b else half_used, 1)

            def part_ready(kind):
                return lambda c: pe_.wait_ge(part_lo, PART_BASE[kind] + c + 1)

            def rope_turn(b):
                pe_.wait_ge(a_read, filled("proj", rope_blocks[b]))
                out = take_v(VT[("rope", rope_blocks[b])])
                mm(out, perm, blk(RAW + b), True, True).then_inc(v_done, 1)

            pending = []
            for s in STEPS:
                kind = s[0]
                if kind == "small":
                    pe_.wait_ge(small_in, 16 * 10)
                    rel = par[0:33, PAR["rel"][0]:PAR["rel"][1]]
                    for n in range(CMP_N + 8):
                        at = TRI - 16 * (n - 8) - 31 + 272
                        last = mm(psum[:, 7, n * HEADS:(n + 1) * HEADS], rel_c[0:33, at:at + P], rel, True, True)
                    last.then_inc(rel_done, 1)
                elif kind == "bias":
                    rel = par[0:33, PAR["rel"][0]:PAR["rel"][1]]
                    for hd in range(4 * s[1], 4 * s[1] + 4):
                        n = VT[("bias_row", hd)]
                        take_v(n)
                        lhs = rel[:, hd:hd + 1].to_broadcast([33, P])
                        mm(psum[:, 2 + n % 4, 0:TRI], lhs, rel_c[0:33, 0:TRI], True, True).then_inc(v_done, 1)
                elif kind == "norm":
                    k = s[1]
                    pe_.wait_ge(const_set, 1)
                    if k in (0, 2):
                        sum_squares(AT[s + ("ssq",)], blk(SQ, 8), KC,
                                    lambda c, k=k: pe_.wait_ge(squared, NORM_BASE[k] + c + 1))
                    else:
                        for c in (6, 7):
                            last = add_square(k, c)
                        last.then_inc(ssq1_done if k == 1 else a_done, 1)
                elif kind == "proj" and s[1] in ROWS:
                    while pending:
                        rope_turn(pending.pop(0))
                    jobs, width, cols = ROWS[s[1]]
                    k0, slots = SPLIT[SLOT_AT[s]], SLOTS_OF.get(s[1], 1)
                    take, at, done = (take_v, VT, v_done) if jobs == 4 else (take_a, AT, a_done)
                    pe_.wait_ge(h_ready, 8 if jobs == 4 else 16)
                    out = [take(at[s + (j,)]) for j in range(jobs)]
                    each = HSLOT // width
                    for x in range(2 * slots):
                        half = half_ready(k0 + x // 2, x % 2)
                        for j in range(jobs):
                            i, col = (j // 2, (j % 2) * T) if jobs == 4 else (j, 0)
                            for y in range(each):
                                c = x * each + y
                                t = slice(P * i, P * i + P)
                                w = slice(y * width + col, y * width + col + cols)
                                o, end = out[j][:, 0:cols], c == KC - 1
                                mm(o, h_hi[:, c, t], w_hi[:, half, w], c == 0, False)
                                mm(o, h_lo[:, c, t], w_hi[:, half, w], False, False)
                                last = mm(o, h_hi[:, c, t], w_lo[:, half, w], False, end)
                            if x == 2 * slots - 1:
                                last.then_inc(done, 1)
                        if x < 2 * slots - 1:
                            last.then_inc(half_used, 1)
                elif kind == "proj":
                    base = 0 if s[1] in FIRST1 + FILL1 else 8
                    split_projection(AT[s], SPLIT[SLOT_AT[s]], lambda c, base=base: pe_.wait_ge(h_ready, base + c + 1))
                    if s[1] in rope_blocks:
                        pending.append(rope_blocks.index(s[1]))
                        if len(pending) > 1:
                            rope_turn(pending.pop(0))
                elif kind == "gates":
                    pe_.wait_ge(a_read, filled("proj", "gt"))
                    out = take_a(AT[s])
                    for i in range(TT):
                        last = nc.tensor.transpose(out[:, P * i:P * i + P], blk(GT)[:, P * i:P * i + P], ident[:, :])
                    last.then_inc(a_done, 1)
                elif kind == "scores":
                    p = s[1]
                    while pending:
                        rope_turn(pending.pop(0))
                    if p < 8:
                        pe_.wait_ge(rope_done, 16)
                        pe_.wait_ge(v_read, VT[("proj", "mv", 3)] + 1)
                        base = QK if p < 4 else QK + 8
                        b = p % 4
                        q, k = blk(base + b), blk(base + 4 + b)
                    else:
                        pe_.wait_ge(a_read, filled("proj", "kw"))
                        pe_.wait_ge(v_read, VT[("bias_row", 7)] + 1)
                        q, k = blk(NQ + (p - 8) // 2), blk(KS if p % 2 == 0 else KW)
                    if p >= 2:
                        pe_.wait_ge(masked_done, p - 1)
                    out = scb(p)
                    for m in range(2):
                        r = slice(DH * m, DH * m + DH)
                        mm(out[:, m, 0:P], q[r, 0:P], k[r, 0:P], True, True)
                        last = mm(out[:, m, P:TRI], q[r, P:T], k[r, :], True, True)
                    last.then_inc(scores_done, 1)
                elif kind == "turn":
                    p = s[1]
                    pe_.wait_ge(probs_done, p + 1)
                    if p:
                        pe_.wait_ge(pt_done, p if p < 8 else p + 1)
                    if p == 0:
                        pe_.wait_ge(rel_read, 1)
                    for m in range(1 if p < 4 else 2):
                        for c in range(3):
                            last = nc.tensor.transpose(turned[:, m, c * P:c * P + P],
                                                       ex_of(p)[:, m, c * P:c * P + P], ident[:, :])
                    last.then_inc(turn_done, 1)
                elif kind == "pv":
                    p = s[1]
                    pe_.wait_ge(pt_done, p + 1 if p < 8 else p + 2)
                    if p < 8:
                        pe_.wait_ge(v_read, VT[("proj", "dv" if p < 4 else "mv", 3)] + 1)
                    out = take_a(AT[s])
                    pt = pt_of(p)
                    if p < 4:
                        v = flat(DV, 4).rearrange("p (i n) -> p i n", i=TT)
                        mm(out, v[:, 0, P * p:P * p + P], pt[:, 0, 0:T], True, False)
                        last = mm(out[:, P:T], v[:, 1, P * p:P * p + P], pt[:, 0, T:TRI], False, True)
                    elif p < 8:
                        v = flat(MV, 4).rearrange("p (i n) -> p i n", i=TT)
                        for m in range(2):
                            o, at = out[DH * m:DH * m + DH, :], P * (p - 4) + DH * m
                            mm(o, v[:, 0, at:at + DH], pt[:, m, 0:T], True, False)
                            last = mm(o[:, P:T], v[:, 1, at:at + DH], pt[:, m, T:TRI], False, True)
                    else:
                        pe_.wait_ge(a_read, filled("proj", "nv", TT - 1))
                        v = flat(NV, 2).rearrange("p (i n) -> p i n", i=TT)
                        for m in range(2):
                            o = out[DH * m:DH * m + DH, :]
                            mm(o, bd[:, m, (p - 8) // 2, :], cpt[:, m, :], True, False)
                            for w, pp in ((0, pt_of(p - 1)), (1, pt)):
                                at = P * w + DH * m
                                mm(o, v[:, 0, at:at + DH], pp[:, m, 0:T], False, False)
                                last = mm(o[:, P:T], v[:, 1, at:at + DH], pp[:, m, T:TRI], False, w == 1)
                    last.then_inc(a_done, 1)
                elif kind == "subln":
                    for j in range(2):
                        pe_.wait_ge(osq_done, 2 * j + 2)
                        take_a(AT[s + (j,)])
                        mm(psum[:, AT[s + (j,)] % 2, :], ones[:, :], flat(SQ + 2 * j, 2), True, True).then_inc(a_done, 1)
                elif kind == "ple":
                    for j in range(KC):
                        projection(AT[s + (j,)], SLOT_AT[s] + j // 4, 2, (j % 4) * T, blk(PTOK, 2), lambda c: None,
                                   take_a, a_done)
                elif kind == "merge":
                    pe_.wait_ge(masked_done, 8)
                    for nb in range(KC):
                        k = SPLIT[SLOT_AT[s]] + nb
                        for ab in range(2):
                            n = VT[s + (2 * nb + ab,)]
                            out = take_v(n)
                            half = half_ready(k, ab)
                            for c4 in range(4):
                                c = 4 * ab + c4
                                part_ready(kind)(c)
                                last = split_mms(out, half, c4 * P, (h_hi[:, c, :], h_lo[:, c, :]), c4 == 0, c4 == 3)
                            last.then_inc(v_done, 1)
                elif kind in ("out1", "out2"):
                    for nb in range(KC):
                        split_projection(VT[s + (nb,)], SPLIT[SLOT_AT[s]] + nb, part_ready(kind), take_v, v_done)
                        if kind == "out2" and nb >= 2:
                            add_square(3, nb - 2)
                elif kind == "gate":
                    for nb in range(KC):
                        split_projection(AT[s + (nb,)], SPLIT[SLOT_AT[s]] + nb, part_ready(kind))
                        if nb >= 2:
                            add_square(1, nb - 2)
                elif kind in ("cmpk", "cmpv"):
                    which = 0 if kind == "cmpk" else 1
                    w1 = slot_ready(SLOT_AT[s])
                    pe_.wait_ge(a_read, filled("proj", ("kc", "vc")[which]))
                    pe_.wait_ge(cmp_in, 16 * 4)
                    win = win_of(which)
                    out = take_a(AT[s + (0,)])
                    for l2 in range(16):
                        last = mm(out[0:DH, 0:3 * CMP_N], w1[:, l2 * DH:l2 * DH + DH],
                                  win[:, :, 2 * l2:2 * l2 + 16 * (CMP_N - 1) + 1:16], l2 == 0, l2 == 15)
                    last.then_inc(a_done, 1)
                elif kind in ("cmpk1", "cmpv1"):
                    s = (kind[:4],)
                    which = 0 if kind == "cmpk1" else 1
                    pe_.wait_ge(a_read, filled(*s, 0))
                    out = take_a(AT[s + (1,)])
                    if which == 0:
                        for g in range(2):
                            last = mm(out[DH * g:DH * g + DH, 0:CMP_PAD], w2s[:, 0, :], h1[:, 0, g, :], True, True)
                    else:
                        for r in range(4):
                            for g in range(2):
                                last = mm(out[32 * r:32 * r + 32, DH * g:DH * g + DH], h1[:, 1, g, :], w2s[:, 1, :],
                                          True, True)
                    last.then_inc(a_done, 1)
                elif kind == "cmps":
                    pe_.wait_ge(a_read, filled("cmpk", 1))
                    pe_.wait_ge(pt_done, 8)
                    for g in range(2):
                        for i in range(TT):
                            for r in range(4):
                                at = (i * 4 + r) * CMP_PAD
                                last = mm(psum[:, 6 + g, at:at + CMP_PAD], blk(NQ + r)[DH * g:DH * g + DH, P * i:P * i + P],
                                          kct[DH * g:DH * g + DH, :], True, True)
                    last.then_inc(cmp_step, 1)
                elif kind == "cmpt":
                    pe_.wait_ge(cmp_vec, 8)
                    for g in range(2):
                        for i in range(TT):
                            last = nc.tensor.transpose(turned[:, g, P * i:P * i + P], csc[:, i, g, :], ident[:, :])
                    last.then_inc(cmp_step, 1)
                elif kind == "mix":
                    counts = ((8, 9, 10, 11), (5, 6, 7, 12))[s[1]]
                    sum_squares(AT[s], blk(SQ + 4 * s[1], 4), 4, lambda c, n=counts: pe_.wait_ge(osq_done, n[c]))
                elif kind == "wq":
                    for nb in range(KC):
                        split_projection(AT[s + (nb,)], SPLIT[SLOT_AT[s]] + nb,
                                         lambda c: pe_.wait_ge(h_ready, 16 + c + 1))
                elif kind == "route":
                    pe_.wait_ge(peer_in, 16)
                    pe_.wait_ge(v_read, NVB)
                    for x in range(4):
                        i, first = x // 2, 4 * (x % 2)
                        if x >= 2:
                            pe_.wait_ge(key_read, x - 1)
                        for m in range(2):
                            for j in range(4):
                                hd = first + j
                                pe_.wait_ge(a_read, filled("wq", hd))
                                last = mm(psum[:, 2 + 2 * (x % 2) + m, j * P:j * P + P],
                                          blk(QP + hd)[DH * m:DH * m + DH, P * i:P * i + P],
                                          ring_keys[DH * m:DH * m + DH, hd, :], True, True)
                        last.then_inc(key_done, 1)

            def u_tile(s, n, first, by_pool):
                k = NSPLIT + s
                if not first:
                    pe_.wait_ge(act_read, n - 3)
                out = psum[:, UBANKS[s % 4], 0:T]
                for b in range(2):
                    pe_.wait_ge(hi_done, 2 * (NSPLIT + n) + b + 1)
                    if b:
                        pe_.wait_ge(lo1_done, NSPLIT + n + 1)
                    elif by_pool:
                        pe_.wait_ge(lo2_done, n + 1)
                    else:
                        pe_.wait_ge(lo0_done, NSPLIT + n - POOL_TILES + 1)
                    for c4 in range(4):
                        c = 4 * b + c4
                        last = split_mms(out, (2 * k + b) % 4, c4 * P, (h_hi[:, c, :], h_lo[:, c, :]), c == 0, c == KC - 1)
                    last.then_inc(act_done if b else half_used, 1)

            def u_tiles(a, b):
                with pe_.Fori(a // 4, b // 4) as it:
                    for s in range(4):
                        u_tile(s, it * 4 + s, False, b <= POOL_TILES)

            pe_.wait_ge(a_read, NA - 1)
            for s in range(4):
                u_tile(s, s, True, True)
            u_tiles(4, SEL_TILE)

            pe_.wait_ge(topk_step, TOPK_STEPS)
            for k in range(3):
                for i in range(TT):
                    last = nc.tensor.transpose(psum[:, 4 + k // 2, ((k % 2) * TT + i) * P:((k % 2) * TT + i + 1) * P],
                                               sel[:, i, k, :], ident[:, :])
            last.then_inc(sel_done, 1)
            u_tiles(SEL_TILE, POOL_TILES)

            def quad(s, q, first):
                pe_.wait_ge(hot1_ready, q + 1)
                pe_.wait_ge(wgt0_ready, q + 1)
                pe_.wait_ge(wgt_ready, q + 1)
                if not first:
                    pe_.wait_ge(g_read, q - 3)
                for j in range(4):
                    out = psum[:, 2 + s, j * P:j * P + P]
                    for x in range(3):
                        last = mm(out, hot1[:, s % 2, j, :], wgt[x][:, s % 2, j, :], x == 0, x == 2)
                last.then_inc(route_done, 1)

            for s in range(4):
                u_tile(s, POOL_TILES + s, False, False)
                quad(s, s, True)
            with pe_.Fori(POOL_TILES // 4 + 1, (POOL_TILES + QUADS) // 4) as it:
                for s in range(4):
                    u_tile(s, it * 4 + s, False, False)
                    quad(s, it * 4 + s - POOL_TILES, False)
            u_tiles(POOL_TILES + QUADS, P)

            def v_tile(s, n, first, final):
                k = NSPLIT + P + s
                pe_.wait_ge(act_hi, n + 1)
                pe_.wait_ge(act_lo, n + 1)
                for b in range(2):
                    pe_.wait_ge(hi_done, 2 * (NSPLIT + P + n) + b + 1)
                    if b:
                        pe_.wait_ge(lo1_done, NSPLIT + P + n + 1)
                    else:
                        pe_.wait_ge(lo0_done, NSPLIT + P - POOL_TILES + n + 1)
                    for x in range(4):
                        nb = 4 * b + x
                        out = psum[:, 2 + nb // 2, (nb % 2) * T:(nb % 2) * T + T]
                        w1, w0 = (w[:, (2 * k + b) % 4, x * P:x * P + P] for w in (w_hi, w_lo))
                        mm(out, w1, h_hi[:, s % 4, :], first and nb % 2 == 0, False, skip_group_check=True)
                        mm(out, w1, h_lo[:, s % 4, :], False, False, skip_group_check=True)
                        last = mm(out, w0, h_hi[:, s % 4, :], False, final, skip_group_check=True)
                    last.then_inc(y_done if b else half_used, 1)

            for s in range(4):
                v_tile(s, s, s == 0, False)
            with pe_.Fori(1, P // 4 - 1) as it:
                for s in range(4):
                    v_tile(s, it * 4 + s, False, False)
            for s in range(4):
                v_tile(s, P - 4 + s, False, True)

            sum_squares(AT[("norm", 4, "ssq")], blk(SQ, 8), KC, lambda c: pe_.wait_ge(squared, NORM_BASE[4] + c + 1))

        @block.scalar
        def _(act):
            def empty(n, dst, func=ACT.Copy, cols=None, **kw):
                act.wait_ge(a_done, n + 1)
                src = abuf(n) if cols is None else abuf(n)[:, 0:cols]
                nc.scalar.activation(dst, src, func, **kw).then_inc(a_read, 1)

            def square(src, dst, done):
                nc.scalar.activation(dst, src, ACT.Square).then_inc(done, 1)

            dest = {}
            for b in range(4):
                dest[f"dq{b}"], dest[f"dk{b}"] = RAW + b, RAW + 4 + b
                dest[f"mq{b}"], dest[f"mk{b}"] = RAW + 8 + b, RAW + 12 + b
                dest[f"dg{b}"], dest[f"mg{b}"] = SIL + b, SIL + 4 + b
                dest[f"nq{b}"] = NQ + b
                dest[f"cb{b}"], dest[f"cc{b}"], dest[f"ch{b}"] = CONV + b, CONV + 4 + b, CONV + 8 + b
            for b in range(8):
                dest[f"ga{b}"], dest[f"gb{b}"] = SIG + b, SIG + 8 + b
            dest["ks"], dest["kw"], dest["gt"] = KS, KW, GT

            def high(half, src):
                nc.scalar.activation(w_hi[:, half, :], src, ACT.Copy).then_inc(hi_done, 1)

            def high_slot(k, b, n):
                i, value = slot_of(n)
                act.wait_ge(slot_in[i], value)
                if k >= 2:
                    who, value = half_free[k - 2, b]
                    act.wait_ge(who, value)
                high((2 * k + b) % 4, ring[:, i, b * HSLOT:b * HSLOT + HSLOT])

            def high_u(s, n, first):
                for b in range(2):
                    act.wait_ge(slot_in[(NSLOT + s) % RING], slot_count(NSLOT + s, n - s))
                    if first:
                        act.wait_ge(*half_free[NSPLIT - 2 + s, b])
                    elif b:
                        act.wait_ge(act_done, n - 1)
                    else:
                        act.wait_ge(half_used, NHALF + n - 1)
                    at = b * HSLOT
                    high((2 * (NSPLIT + s) + b) % 4, ring[:, (NSLOT + s) % RING, at:at + HSLOT])

            def high_parts(kind, chunks):
                for c in chunks:
                    src, made, free = part_of(kind, c)
                    act.wait_ge(*made)
                    act.wait_ge(*free)
                    nc.scalar.activation(h_hi[:, c, :], src, ACT.Copy).then_inc(part_hi, 1)

            def norm_square(k, c):
                if k:
                    act.wait_ge(*{1: (x_ready, c + 1), 2: (x1_ready, c + 1),
                                  3: (v_read, VT[("out2", c)] + 1)}[k])
                if k == 1 and c == 0:
                    act.wait_ge(sub_done, 12)
                if k and c == 0:
                    act.wait_ge(*{1: (a_done, filled("subln", 1)), 2: (ssq1_done, 1), 3: (a_done, filled("mix", 1))}[k])
                square(xres[:, c, :] if k != 1 else blk(MERGED + c), blk(SQ + c), squared)

            def highs(last):
                nonlocal k_hi
                while k_hi <= last:
                    for b in range(2):
                        high_slot(k_hi, b, SLOT_OF_SPLIT[k_hi])
                    k_hi += 1

            k_hi = 0
            for s in STEPS:
                kind = s[0]
                if kind != "norm":
                    highs(ahead(s))
                if kind in ("merge", "out1", "gate"):
                    high_parts(kind, range(KC))
                if kind in WIDE:
                    for j in range(KC):
                        highs(ahead_in(s, j))
                        if kind == "merge" and j == 0:
                            nc.scalar.activation(blk(SIG + 8, 8), blk(SIG + 8, 8), ACT.Sigmoid).then_inc(gates_ready, 1)
                        if kind == "gate":
                            act.wait_ge(v_read, VT[("merge", 2 * j + 1)] + 1)
                            empty(AT[s + (j,)], blk(SIG + j), ACT.Sigmoid)
                        if kind == "wq":
                            empty(AT[s + (j,)], blk(QP + j))
                        if kind in ("gate", "out2") and j:
                            norm_square(1 if kind == "gate" else 3, j - 1)
                if kind == "small":
                    act.wait_ge(small_in, 16 * 10)
                    act.wait_ge(lam_step, 2)
                    nc.scalar.activation(small[:, 2:4], small[:, 0:2], ACT.Exp).then_inc(cact_ready, 1)
                    nc.scalar.activation(c_act, c_act, ACT.Silu).then_inc(cact_ready, 1)
                elif kind == "norm":
                    k = s[1]
                    if k == 0:
                        act.wait_ge(x_in, 32)
                        act.wait_ge(const_set, 2)
                    for c in range(KC) if k in (0, 2) else (KC - 1,):
                        norm_square(k, c)
                    if k:
                        act.wait_ge(rstd_ready, {1: 1, 2: 2, 3: 5}[k])
                    if k == 1:
                        act.wait_ge(ssq1_done, 1)
                        nc.scalar.activation(std[:, :], psum[:, 6, 0:T], ACT.Sqrt, scale=1.0 / D, bias=eps_c[:, 0:1])\
                            .then_inc(std1_ready, 1)
                    else:
                        empty(AT[s + ("ssq",)], std[:, :], ACT.Sqrt, scale=1.0 / D, bias=eps_c[:, 0:1])
                    highs(ahead(s))
                    if k != 1:
                        first = {0: 0, 2: 8, 3: 16}[k]
                        for c in range(KC):
                            act.wait_ge(t_ready, first + c + 1)
                            if c == 0 and k:
                                act.wait_ge(*((a_done, filled("gate", 7)) if k == 2 else (v_done, VT["out2", 7] + 1)))
                            if k:
                                sh = (0 if k == 2 else 24) + c
                                nc.scalar.activation(h_hi[:, c, :], blk(NTMP + c), ACT.Identity,
                                                     bias=mod[:, sh:sh + 1]).then_inc(th_done, 1)
                            else:
                                nc.scalar.activation(h_hi[:, c, :], blk(NTMP + c), ACT.Copy).then_inc(th_done, 1)
                elif kind == "proj" and s[1] in ("dv", "mv"):
                    pass
                elif kind == "gates":
                    act.wait_ge(a_done, AT[s] + 1)
                    nc.scalar.activation(gsig[:, :, :], abuf(AT[s]).rearrange("p (i n) -> p i n", i=TT)[:, :, 0:24],
                                         ACT.Sigmoid).then_inc(a_read, 1)
                elif kind == "proj" and s[1] == "nv":
                    for j in range(TT):
                        empty(AT[s + (j,)], blk(NV + j))
                elif kind == "proj" and s[1] in ("kc", "vc"):
                    act.wait_ge(a_done, AT[s] + 1)
                    win = win_of(0 if s[1] == "kc" else 1)
                    for g in range(2):
                        src = abuf(AT[s])[DH * g:DH * g + DH, :]
                        nc.scalar.activation(win[0:DH, g, :], src, ACT.Copy)
                        last = nc.scalar.activation(win[DH:P, g, 0:T - 1], src[:, 1:T], ACT.Copy)
                    last.then_inc(a_read, 1)
                elif kind == "proj":
                    if s[1] == "ga0":
                        act.wait_ge(rope_done, 16)
                    empty(AT[s], blk(dest[s[1]]))
                elif kind == "soft":
                    p = s[1]
                    act.wait_ge(max_done, 2 * p + 2)
                    if p >= 2:
                        act.wait_ge(turn_done, p - 1)
                    for m in range(2):
                        for i in range(TT):
                            cols = slice(0, P) if i == 0 else slice(P, TRI)
                            n = 2 * m + i
                            nc.scalar.activation(ex_of(p)[:, m, cols], sc_of(p)[:, m, cols], ACT.Exp,
                                                 bias=nmax[:, p % 2, n:n + 1], accum_out=sums[:, p % 2, n:n + 1])\
                                .then_inc(exp_done, 1)
                elif kind == "turn":
                    p = s[1]
                    if p == 8:
                        act.wait_ge(cmp_step, 2)
                        nc.scalar.activation(cpt, turned[:, :, 0:T], ACT.Copy).then_inc(pt_done, 1)
                    act.wait_ge(turn_done, p + 1)
                    if p >= 3:
                        act.wait_ge(a_done, filled("pv", p - 3) if p < 11 else filled("pv", (p - 3) | 1))
                    m = 1 if p < 4 else 2
                    nc.scalar.activation(pt_of(p)[:, 0:m, :], turned[:, 0:m, :], ACT.Copy).then_inc(pt_done, 1)
                    if p == 3:
                        nc.scalar.activation(blk(SIL, 8), blk(SIL, 8), ACT.Silu).then_inc(gates_ready, 1)
                    if p == 7:
                        nc.scalar.activation(blk(SIG, 8), blk(SIG, 8), ACT.Sigmoid).then_inc(gates_ready, 1)
                elif kind == "pv":
                    p = s[1]
                    empty(AT[s], blk(OT + (p if p < 8 else 4 + (p - 9) // 2)))
                    if p < 4:
                        act.wait_ge(a_read, filled("pv", p))
                        act.wait_ge(a_done, filled("norm", 0, "ssq"))
                        square(blk(OT + p), blk(SQ + p), osq_done)
                    if p > 8:
                        act.wait_ge(a_read, filled("pv", p))
                        act.wait_ge(a_done, filled("norm", 2, "ssq"))
                        square(blk(OT + 4 + (p - 9) // 2), blk(SQ + 4 + (p - 9) // 2), osq_done)
                elif kind == "subln":
                    for j in range(2):
                        n = AT[s + (j,)]
                        act.wait_ge(a_done, n + 1)
                        nc.scalar.activation(flat(SQ + 2 * j, 2), psum[:, n % 2, :], ACT.Sqrt, scale=1.0 / P,
                                             bias=eps_c[:, 1:2]).then_inc(a_read, 1)
                elif kind == "ple":
                    for j in range(KC):
                        empty(AT[s + (j,)], blk(PLE + j))
                elif kind in ("cmpk", "cmpv"):
                    which = 0 if kind == "cmpk" else 1
                    n = AT[s + (0,)]
                    act.wait_ge(a_done, n + 1)
                    hid = abuf(n)[0:DH, 0:3 * CMP_N].rearrange("p (g n) -> p g n", g=3)
                    nc.scalar.activation(pebias[:, which:which + 1], hid[:, 2, 0:1], ACT.Copy).then_inc(cmp_bias, 1)
                    act.wait_ge(cmp_bias, which + 1)
                    act.wait_ge(zero_set, 1)
                    nc.scalar.activation(h1[:, which, :, 0:CMP_N], hid[:, 0:2, :], ACT.Gelu_apprx_tanh,
                                         bias=pebias[:, which:which + 1]).then_inc(a_read, 1)
                elif kind in ("cmpk1", "cmpv1"):
                    s = (kind[:4],)
                    if kind == "cmpk1":
                        empty(AT[s + (1,)], kct, cols=CMP_PAD)
                    else:
                        n = AT[s + (1,)]
                        act.wait_ge(a_done, n + 1)
                        for r in range(4):
                            rows = slice(32 * r, 32 * r + 32)
                            last = nc.scalar.activation(bd[rows, :, r, :],
                                                        abuf(n)[rows, 0:P].rearrange("p (g d) -> p g d", g=2), ACT.Copy)
                        last.then_inc(a_read, 1)
                elif kind == "cmps":
                    act.wait_ge(cmp_vec, 4)
                    nc.scalar.activation(flat(CSC, 2), flat(CSC, 2), ACT.Exp).then_inc(cmp_exp, 1)
                elif kind == "mix":
                    if s[1] == 0:
                        act.wait_ge(a_done, filled("gates"))
                        for b in range(4):
                            act.wait_ge(conv_done, b + 1)
                            square(blk(OT + b), blk(SQ + b), osq_done)
                    else:
                        high_parts("out2", range(4))
                    act.wait_ge(rstd_ready, 3 + s[1])
                    empty(AT[s], std[:, :], ACT.Sqrt, scale=1.0 / 512, bias=eps_c[:, 0:1])
                    if s[1]:
                        high_parts("out2", range(4, KC))
                elif kind == "route":
                    for n in range(2):
                        high_u(n, n, True)
                    for x in range(4):
                        i, first = x // 2, 4 * (x % 2)
                        act.wait_ge(key_done, x + 1)
                        banks = psum[:, 2 + 2 * (x % 2):4 + 2 * (x % 2), :]
                        nc.scalar.activation(scores_of(i)[:, :, first:first + 4, :],
                                             banks.rearrange("p m (j k) -> p m j k", j=4), ACT.Copy)\
                            .then_inc(key_read, 1)

            def gelu(s, n):
                act.wait_ge(act_done, n + 1)
                nc.scalar.activation(arena[:, n, :], psum[:, UBANKS[s % 4], 0:T], ACT.Gelu_apprx_tanh)\
                    .then_inc(act_read, 1)

            def u_loop(a, b):
                with act.Fori(a // 4, b // 4) as it:
                    for s in range(4):
                        high_u(s, it * 4 + s, False)
                        gelu(s + 2, it * 4 + s - 2)

            act.wait_ge(key_done, 4)
            for s in range(4):
                if s >= 2:
                    high_u(s, s, False)
                    gelu(s + 2, s - 2)
            u_loop(4, SOFT_TILE)
            act.wait_ge(topk_step, SOFT_STEP)
            nc.scalar.activation(blk(106), blk(106), ACT.Exp).then_inc(soft_exp, 1)
            u_loop(SOFT_TILE, POOL_TILES + COPY_LAG)
            act.wait_ge(sel_done, 1)

            def copy_quad(s, q, more):
                if s % 2 == 0 and more is not None:
                    act.wait_ge(spilled[s // 2], 16 * more)
                act.wait_ge(route_done, q + 1)
                dst = stage[:, s // 2, :, 4 * (s % 2):4 * (s % 2) + 4, :].rearrange("p r t g -> p t r g")
                src = psum[:, 2 + s, :].rearrange("p (t r g) -> p t r g", t=4, r=GROUPS)
                nc.scalar.activation(dst, src, ACT.Copy).then_inc(g_read, 1)

            first = POOL_TILES + COPY_LAG
            for s in range(4):
                high_u(s, first + s, False)
                gelu(s + 2, first + s - 2)
                copy_quad(s, s, None)
            with act.Fori(first // 4 + 1, (first + QUADS) // 4) as it:
                for s in range(4):
                    high_u(s, it * 4 + s, False)
                    gelu(s + 2, it * 4 + s - 2)
                    copy_quad(s, it * 4 + s - first, it - first // 4)
            u_loop(first + QUADS, P)
            for s in range(2):
                gelu(s + 2, P - 2 + s)

            def high_v(s, n, first):
                for b in range(2):
                    act.wait_ge(slot_in[(NSLOT + P + s) % RING], slot_count(NSLOT + P + s, n - s))
                    if first:
                        act.wait_ge(*((half_used, NHALF + P + n - 1), (act_done, P + n - 1))[b])
                    elif b:
                        act.wait_ge(y_done, n - 1)
                    else:
                        act.wait_ge(half_used, NHALF + P + n - 1)
                    at = b * HSLOT
                    high((2 * (NSPLIT + P + s) + b) % 4, ring[:, (NSLOT + P + s) % RING, at:at + HSLOT])

            def high_act(s, n, count, first):
                act.wait_ge(weighted, count)
                if first:
                    act.wait_ge(act_done, P)
                else:
                    act.wait_ge(y_done, n - 3)
                nc.scalar.activation(h_hi[:, s, :], arena[:, n, :], ACT.Copy).then_inc(act_hi, 1)

            for s in range(4):
                high_v(s, s, s < 2)
                high_act(s, s, s // 2 + 1, True)
            with act.Fori(1, P // 4) as it:
                for s in range(4):
                    high_v(s, it * 4 + s, False)
                    high_act(s, it * 4 + s, it * 2 + s // 2 + 1, False)

            nc.scalar.activation(small[:, 60:62], eps_c[:, :], ACT.Sqrt)
            act.wait_ge(y_done, P)
            for c in range(KC):
                act.wait_ge(x_ready, KC + c + 1)
                square(xres[:, c, :], blk(SQ + c), squared)
            act.wait_ge(rstd_ready, 6)
            empty(AT[("norm", 4, "ssq")], std[:, :], ACT.Sqrt, scale=1.0 / D, bias=eps_c[:, 0:1])

        @block.gpsimd
        def _(pool):
            def low(k, half, src, hi_value, done):
                pool.wait_ge(hi_done, hi_value)
                nc.gpsimd.tensor_tensor(w_lo[:, half, :], src, w_hi[:, half, :].bitcast(F32), ALU.subtract)\
                    .then_inc(done, 1)

            def load_mod(m):
                if m >= 2:
                    pool.wait_ge(mod_done, m - 1)
                pool.dma_start(flat(MODR[24 <= m < 40] + 4 * (m % 2), 4), mods[m]).then_inc(mod_in[m % 2], 16)

            k_lo = 0
            for s in STEPS:
                kind = s[0]
                while k_lo <= ahead(s):
                    src = ring[:, SLOT_OF_SPLIT[k_lo] % RING, HSLOT:D]
                    low(k_lo, (2 * k_lo + 1) % 4, src, 2 * k_lo + 2, lo1_done)
                    k_lo += 1
                if kind in WIDE:
                    for j in range(KC):
                        while k_lo <= ahead_in(s, j):
                            src = ring[:, SLOT_OF_SPLIT[k_lo] % RING, HSLOT:D]
                            low(k_lo, (2 * k_lo + 1) % 4, src, 2 * k_lo + 2, lo1_done)
                            k_lo += 1
                        m = {"out1": 26, "gate": 34}.get(kind, 40) + j
                        if m < 40:
                            load_mod(m)
                elif kind == "small":
                    load_mod(0)
                    load_mod(1)
                elif kind == "mod" and s[1] + 2 not in (24, 25, 48, 49):
                    load_mod(s[1] + 2)
                elif s == ("scores", 9):
                    pool.wait_ge(x1_ready, KC)
                    pool.wait_ge(squared, 2 * KC)
                    load_mod(40)
                    load_mod(41)
                elif kind == "bias" and s[1]:
                    pool.wait_ge(v_read, VT[("bias_row", 7)] + 1)
                    pool.dma_start(bias_dram, bias_rows).then_inc(sheet_in, 16)
                elif s == ("proj", "vc"):
                    pool.wait_ge(sheet_in, 16)
                    pool.wait_ge(turn_done, 8)
                    skew = bass.AP(bias_dram.tensor, bias_dram.offset + P - 1,
                                   [[HEADS * TRI - 1, P], [TRI, HEADS], [1, T]])
                    pool.dma_start(sheet, skew).then_inc(sheet_in, 16)
                elif kind == "ple":
                    pool.wait_ge(a_done, filled("pv", 7))
                    load_mod(24)
                    load_mod(25)
                elif kind == "proj" and s[1] in rope_blocks:
                    b = rope_blocks.index(s[1])
                    pool.wait_ge(small_in, 16 * 10)
                    pool.wait_ge(a_read, filled(*s))
                    nc.gpsimd.tensor_tensor(blk(QK + b), blk(RAW + b), cos_t, ALU.mult).then_inc(cos_done, 1)
                elif kind == "soft" and s[1] >= 4:
                    p = s[1]
                    if p < 8:
                        pool.wait_ge(inv_done, p + 1)
                    else:
                        pool.wait_ge(gated_done, p - 7)
                    for m in range(2):
                        for i in range(TT):
                            cols = slice(0, P) if i == 0 else slice(P, TRI)
                            n = 2 * m + i
                            e = ex_of(p)[:, m, cols]
                            last = nc.gpsimd.tensor_scalar(e, e, rsum[:, p % 2, n:n + 1], 1.0, ALU.mult, ALU.mult)
                    last.then_inc(probs_done, 1)
                elif kind == "norm" and s[1] == 1:
                    pool.wait_ge(x_ready, KC)
                    nc.gpsimd.memset(blk(BD, 3), 0.0).then_inc(zero_set, 1)
                elif kind == "conv":
                    for b in s[1:]:
                        pool.wait_ge(a_read, filled("proj", f"ch{b}"))
                        nc.gpsimd.tensor_tensor(blk(CONV + 4 + b), blk(CONV + 4 + b), blk(CONV + 8 + b), ALU.mult)\
                            .then_inc(z_done, 1)
                    for b in s[1:]:
                        pool.wait_ge(conv_step, 3 * b + 3)
                        nc.gpsimd.tensor_tensor(blk(OT + b), blk(PROD + b), blk(CONV + b), ALU.mult)\
                            .then_inc(conv_done, 1)
                elif s == ("mix", 0):
                    pool.wait_ge(masked_done, 8)
                    pool.wait_ge(rope_done, 16)
                    pool.dma_start(ring_keys, keys).then_inc(peer_in, 16)

            def low_tile(base, s, n, both):
                src = ring[:, (NSLOT + base + s) % RING, :]
                k = NSPLIT + base + s
                if both:
                    low(k, 2 * k % 4, src[:, 0:HSLOT], 2 * (NSPLIT + base + n) + 1, lo2_done)
                else:
                    pool.wait_ge(lo0_done, NSPLIT + base - POOL_TILES + n + 1)
                low(k, (2 * k + 1) % 4, src[:, HSLOT:D], 2 * (NSPLIT + base + n) + 2, lo1_done)

            with pool.Fori(0, POOL_TILES // 4) as it:
                for s in range(4):
                    low_tile(0, s, it * 4 + s, True)
            with pool.Fori(POOL_TILES // 4, (POOL_TILES + QUADS) // 4) as it:
                for s in range(4):
                    low_tile(0, s, it * 4 + s, False)
                    q = it * 4 + s - POOL_TILES
                    pool.wait_ge(hot2_ready, q + 1)
                    for x in (1, 2):
                        w = sel_w[x][:, bass.ds(q * 4, 4)].unsqueeze(2).to_broadcast([P, 4, P])
                        last = nc.gpsimd.tensor_tensor(wgt[x][:, s % 2, :, :], hot2[:, s % 2, :, :], w, ALU.mult)
                    last.then_inc(wgt_ready, 1)
            with pool.Fori((POOL_TILES + QUADS) // 4, P // 4) as it:
                for s in range(4):
                    low_tile(0, s, it * 4 + s, False)
            with pool.Fori(0, P // 4) as it:
                for s in range(4):
                    low_tile(P, s, it * 4 + s, False)

        @block.vector
        def _(dve):
            v = nc.vector

            def bc(ap, shape):
                return ap.to_broadcast(shape)

            def inverse(std_value, ready):
                dve.wait_ge(a_read, std_value)
                v.reciprocal(rstd[:, :], std[:, :]).then_inc(rstd_ready, 1)
                dve.wait_ge(rstd_ready, ready)

            def low(half, src, hi_value):
                dve.wait_ge(hi_done, hi_value)
                v.tensor_tensor(w_lo[:, half, :], src, w_hi[:, half, :].bitcast(F32), ALU.subtract)\
                    .then_inc(lo0_done, 1)

            def modulation(m):
                dve.wait_ge(mod_in[m % 2], 16 * (m // 2 + 1))
                dve.wait_ge(cact_ready, 2)
                if m:
                    dve.wait_ge(mod_done, m)
                v.tensor_tensor_reduce(junk, flat(MODR[24 <= m < 40] + 4 * (m % 2), 4), c_act, 1.0, pcol("b_mod", m),
                                       ALU.mult, ALU.add, mod[:, m:m + 1]).then_inc(mod_done, 1)

            def rope(b):
                n = VT[("rope", rope_blocks[b])]
                dve.wait_ge(v_done, n + 1)
                tmp = blk(SIG + b)
                v.tensor_tensor(tmp, vbuf(n), sin_t, ALU.mult).then_inc(v_read, 1)
                dve.wait_ge(v_read, n + 1)
                dve.wait_ge(cos_done, b + 1)
                v.tensor_tensor(blk(QK + b), blk(QK + b), tmp, ALU.add).then_inc(rope_done, 1)

            v.memset(ones[:, :], 1.0).then_inc(const_set, 1)
            v.memset(eps_c[:, 0:1], EPS)
            v.memset(eps_c[:, 1:2], SUBLN_EPS).then_inc(const_set, 1)

            def lows(last):
                nonlocal k_lo
                while k_lo <= last:
                    low(2 * k_lo % 4, ring[:, SLOT_OF_SPLIT[k_lo] % RING, 0:HSLOT], 2 * k_lo + 1)
                    k_lo += 1

            def low_parts(kind, chunks):
                for c in chunks:
                    dve.wait_ge(part_hi, PART_BASE[kind] + c + 1)
                    v.tensor_tensor(h_lo[:, c, :], part_of(kind, c)[0], h_hi[:, c, :].bitcast(F32), ALU.subtract)\
                        .then_inc(part_lo, 1)

            k_lo, ropes = 0, []
            for s in STEPS:
                kind = s[0]
                while ropes and not (kind == "mod" or kind == "proj" and s[1] in rope_blocks):
                    rope(ropes.pop(0))
                if kind != "norm":
                    lows(ahead(s))
                if kind in ("merge", "out1", "gate"):
                    low_parts(kind, range(KC))
                if kind == "small":
                    dve.wait_ge(small_in, 16 * 10)
                    for j in range(2):
                        a, b = pcol("lam", 128 * j, 64), pcol("lam", 128 * j + 64, 64)
                        v.tensor_tensor_reduce(s_sb[:, 2048 + 64 * j:2112 + 64 * j], a, b, 1.0, 0.0, ALU.mult, ALU.add,
                                               small[:, j:j + 1]).then_inc(lam_step, 1)
                    dve.wait_ge(cact_ready, 1)
                    v.tensor_tensor(small[:, 4:5], small[:, 3:4], small[:, 2:3], ALU.subtract).then_inc(lam_step, 1)
                    dve.wait_ge(lam_step, 3)
                    v.tensor_scalar(small[:, 5:6], small[:, 4:5], -LAM_INIT, None, ALU.add).then_inc(lam_step, 1)
                    v.tensor_scalar(small[:, 6:7], pcol("subln_g"), 1.0 - LAM_INIT, None, ALU.mult).then_inc(lam_step, 1)
                    cb = s_sb[:, 1536:2048].rearrange("p (i h n) -> p i h n", i=TT, h=HEADS)
                    v.memset(s_sb[:, 1536:2048], NEG).then_inc(const_set, 1)
                    dve.wait_ge(const_set, 3)
                    dve.wait_ge(rel_done, 1)
                    for i in range(TT):
                        src = psum[:, 7, 8 * (1 - i) * HEADS:(8 * (1 - i) + CMP_N) * HEADS]
                        last = v.tensor_copy(cb[:, i, :, 0:CMP_N], src.rearrange("p (n h) -> p h n", h=HEADS))
                    last.then_inc(rel_read, 1)
                elif kind == "bias":
                    dve.wait_ge(mod_done, 39)
                    for hd in range(4 * s[1], 4 * s[1] + 4):
                        n = VT[("bias_row", hd)]
                        dve.wait_ge(v_done, n + 1)
                        v.tensor_copy(bias_rows[:, hd, :], psum[:, 2 + n % 4, 0:TRI]).then_inc(v_read, 1)
                    if s[1]:
                        modulation(39)
                elif kind == "norm":
                    k = s[1]
                    if k == 0:
                        dve.wait_ge(x_in, 32)
                    if k >= 2:
                        dve.wait_ge(mod_done, (24, 48)[k - 2])
                        at = (8, 32)[k - 2]
                        v.scalar_tensor_tensor(gm[:, k - 2, :], mod[:, at:at + 8], 1.0,
                                               pcol(("ln_mix_g", "ln_ffn_g")[k - 2], 0, 8), ALU.add, ALU.mult)\
                            .then_inc(mod_ready, 1)
                        dve.wait_ge(mod_ready, k - 1)
                    if k == 1:
                        dve.wait_ge(h_ready, 8)
                        dve.wait_ge(x_ready, 8)
                        dve.wait_ge(a_done, filled("gate", KC - 1))
                    if k == 2:
                        dve.wait_ge(x1_ready, 8)
                    if k == 3:
                        dve.wait_ge(o_ready, 12)
                    if k == 1:
                        dve.wait_ge(std1_ready, 1)
                        v.reciprocal(rstd[:, :], std[:, :]).then_inc(rstd_ready, 1)
                        dve.wait_ge(rstd_ready, 2)
                    else:
                        inverse(filled(*s, "ssq"), {0: 1, 2: 3, 3: 6}[k])
                        lows(ahead(s))
                    if k == 1:
                        for c in range(KC):
                            v.scalar_tensor_tensor(xres[:, c, :], blk(MERGED + c), pcol("final_g", c), rstd[:, :],
                                                   ALU.mult, ALU.mult).then_inc(x1_ready, 1)
                        continue
                    first = {0: 0, 2: 8, 3: 16}[k]
                    for c in range(KC + 1):
                        if c < KC:
                            t = blk(NTMP + c)
                            gain = pcol("norm_g", c) if k == 0 else gm[:, k - 2, c:c + 1]
                            v.scalar_tensor_tensor(t, xres[:, c, :], gain, rstd[:, :], ALU.mult, ALU.mult)\
                                .then_inc(t_ready, 1)
                        if c:
                            dve.wait_ge(th_done, first + c)
                            t, hi, lo = blk(NTMP + c - 1), h_hi[:, c - 1, :].bitcast(F32), h_lo[:, c - 1, :]
                            if k:
                                sh = (0 if k == 2 else 24) + c - 1
                                v.scalar_tensor_tensor(lo, t, mod[:, sh:sh + 1], hi, ALU.add, ALU.subtract)\
                                    .then_inc(h_ready, 1)
                            else:
                                v.tensor_tensor(lo, t, hi, ALU.subtract).then_inc(h_ready, 1)
                elif kind == "mod":
                    modulation(s[1])
                elif kind == "wq":
                    lows(NSPLIT - 1)
                elif kind == "proj" and s[1] in ("dv", "mv"):
                    rows = flat(DV if s[1] == "dv" else MV, 4).rearrange("p (i n) -> p i n", i=TT)
                    for j in range(4):
                        n = VT[s + (j,)]
                        dve.wait_ge(v_done, n + 1)
                        v.tensor_copy(rows[:, j // 2, (j % 2) * T:(j % 2) * T + T], vbuf(n)).then_inc(v_read, 1)
                elif kind == "proj" and s[1] in rope_blocks:
                    ropes.append(rope_blocks.index(s[1]))
                    if len(ropes) > 1:
                        rope(ropes.pop(0))
                elif kind == "scores":
                    p = s[1]
                    dve.wait_ge(scores_done, p + 1)
                    if p >= 2:
                        dve.wait_ge(exp_done, 4 * (p - 1))
                    sc = sc_of(p)
                    if p < 8:
                        m3 = bc(mask.unsqueeze(1), [P, 2, TRI])
                        v.scalar_tensor_tensor(sc, scb(p), SCALE, m3, ALU.mult, ALU.add).then_inc(masked_done, 1)
                    else:
                        if p == 8:
                            dve.wait_ge(sheet_in, 32)
                        j = (p - 8) // 2
                        bias = sheet[:, j:j + 5:4, :]
                        v.scalar_tensor_tensor(sc[:, :, 0:P], scb(p)[:, :, 0:P], SCALE, bias[:, :, P:T], ALU.mult, ALU.add)
                        v.scalar_tensor_tensor(sc[:, :, P:TRI], scb(p)[:, :, P:TRI], SCALE, bias, ALU.mult, ALU.add)\
                            .then_inc(masked_done, 1)
                    dve.wait_ge(masked_done, p + 1)
                    nm = nmax[:, p % 2, :].rearrange("p (m i) -> p m i", m=2)
                    v.tensor_reduce(nm[:, :, 0], sc[:, :, 0:P], AX, ALU.max, negate=True).then_inc(max_done, 1)
                    v.tensor_reduce(nm[:, :, 1], sc[:, :, P:TRI], AX, ALU.max, negate=True).then_inc(max_done, 1)
                elif kind == "soft":
                    p = s[1]
                    dve.wait_ge(exp_done, 4 * p + 4)
                    rs = rsum[:, p % 2, :]
                    if p >= 2:
                        dve.wait_ge(probs_done, p - 1)
                    v.reciprocal(rs, sums[:, p % 2, :]).then_inc(inv_done, 1)
                    dve.wait_ge(inv_done, p + 1)
                    if p < 4:
                        e = ex_of(p)
                        v.tensor_scalar(rs[:, 2:4], rs[:, 2:4], small[:, 5:6], None, ALU.mult).then_inc(lam_scaled, 1)
                        for i in range(TT):
                            cols = slice(0, P) if i == 0 else slice(P, TRI)
                            v.tensor_scalar(e[:, 0, cols], e[:, 0, cols], rs[:, i:i + 1], None, ALU.mult)\
                                .then_inc(map0_done, 1)
                        dve.wait_ge(lam_scaled, p + 1)
                        dve.wait_ge(map0_done, 2 * p + 2)
                        for i in range(TT):
                            cols = slice(0, P) if i == 0 else slice(P, TRI)
                            last = v.scalar_tensor_tensor(e[:, 0, cols], e[:, 1, cols], rs[:, 2 + i:3 + i], e[:, 0, cols],
                                                          ALU.mult, ALU.add)
                        last.then_inc(probs_done, 1)
                    elif p >= 8:
                        j, br = (p - 8) // 2, 1 + p % 2
                        g = gsig[:, :, :].rearrange("p i (h b) -> p h i b", b=3)[:, j:j + 5:4, :, br]
                        dve.wait_ge(a_read, filled("gates"))
                        rr = rs.rearrange("p (m i) -> p m i", m=2)
                        v.tensor_tensor(rr, rr, g, ALU.mult).then_inc(gated_done, 1)
                elif kind == "pv" and 4 <= s[1] < 8:
                    p = s[1]
                    dve.wait_ge(a_read, filled(*s))
                    dve.wait_ge(gates_ready, 1)
                    v.tensor_tensor(blk(OT + p), blk(OT + p), blk(SIL + p), ALU.mult).then_inc(o_ready, 1)
                elif kind == "subh":
                    hd = s[1]
                    dve.wait_ge(a_read, filled("subln", hd // 2))
                    v.reciprocal(blk(SQ + hd), blk(SQ + hd)).then_inc(sub_done, 1)
                    dve.wait_ge(sub_done, 3 * hd + 1)
                    v.scalar_tensor_tensor(blk(OT + hd), blk(OT + hd), small[:, 6:7], blk(SQ + hd), ALU.mult, ALU.mult)\
                        .then_inc(sub_done, 1)
                    dve.wait_ge(sub_done, 3 * hd + 2)
                    v.tensor_tensor(blk(OT + hd), blk(OT + hd), blk(SIL + hd), ALU.mult).then_inc(sub_done, 1)
                elif kind == "merge":
                    for nb in range(KC):
                        lows(ahead_in(s, nb))
                        na, nb_ = VT[s + (2 * nb,)], VT[s + (2 * nb + 1,)]
                        m_, sa, sb_ = blk(MERGED + nb), blk(SIG + nb), blk(SIG + 8 + nb)
                        dve.wait_ge(gates_ready, 2)
                        dve.wait_ge(v_done, na + 1)
                        v.tensor_tensor(m_, vbuf(na), sa, ALU.mult).then_inc(v_read, 1)
                        dve.wait_ge(gates_ready, 3)
                        dve.wait_ge(v_done, nb_ + 1)
                        v.tensor_tensor(sb_, vbuf(nb_), sb_, ALU.mult).then_inc(v_read, 1)
                        dve.wait_ge(v_read, nb_ + 1)
                        v.tensor_tensor(m_, m_, sb_, ALU.add).then_inc(merged_ready, 1)
                elif kind == "out1":
                    for nb in range(KC):
                        lows(ahead_in(s, nb))
                        n = VT[s + (nb,)]
                        dve.wait_ge(v_done, n + 1)
                        v.tensor_tensor(xres[:, nb, :], vbuf(n), xres[:, nb, :], ALU.add).then_inc(v_read, 1)
                        modulation(24 + nb)
                elif kind == "gate":
                    for nb in range(KC):
                        lows(ahead_in(s, nb))
                        dve.wait_ge(a_read, filled(*s, nb))
                        v.tensor_tensor(blk(PLE + nb), blk(PLE + nb), blk(SIG + nb), ALU.mult).then_inc(ple_step, 1)
                        dve.wait_ge(ple_step, nb + 1)
                        v.tensor_tensor(blk(MERGED + nb), xres[:, nb, :], blk(PLE + nb), ALU.add).then_inc(x_ready, 1)
                        if nb < KC - 1:
                            modulation(32 + nb)
                elif kind == "cmps":
                    dve.wait_ge(rel_read, 1)
                    v.tensor_copy(flat(CBIAS, 2), s_sb[:, 1536:2048]).then_inc(cmp_vec, 1)
                    dve.wait_ge(cmp_step, 1)
                    dve.wait_ge(cmp_vec, 1)
                    for g in range(2):
                        src = psum[:, 6 + g, 0:T].rearrange("p (i c) -> p i c", i=TT)
                        b = cbias[:, :, 4 * g:4 * g + 4, :].rearrange("p i h n -> p i (h n)")
                        last = v.scalar_tensor_tensor(csc[:, :, g, :], src, SCALE, b, ALU.mult, ALU.add)
                    last.then_inc(cmp_vec, 1)
                    dve.wait_ge(cmp_vec, 2)
                    maps = flat(CSC, 2).rearrange("p (k n) -> p k n", n=CMP_PAD)
                    v.tensor_reduce(cst1[:, 0, :], maps, AX, ALU.max).then_inc(cmp_vec, 1)
                    dve.wait_ge(cmp_vec, 3)
                    v.tensor_tensor(maps, maps, bc(cst1[:, 0, :].unsqueeze(2), [P, 16, CMP_PAD]), ALU.subtract)\
                        .then_inc(cmp_vec, 1)
                    dve.wait_ge(cmp_exp, 1)
                    v.tensor_reduce(cst1[:, 1, :], maps, AX, ALU.add).then_inc(cmp_vec, 1)
                    dve.wait_ge(cmp_vec, 5)
                    v.reciprocal(cst1[:, 2, :], cst1[:, 1, :]).then_inc(cmp_vec, 1)
                    dve.wait_ge(cmp_vec, 6)
                    for i in range(TT):
                        g = gsig[:, i, :].rearrange("p (h b) -> p h b", b=3)[:, :, 0]
                        dve.wait_ge(a_read, filled("gates"))
                        last = v.scalar_tensor_tensor(cst1[:, 1, 8 * i:8 * i + 8], cst1[:, 2, 8 * i:8 * i + 8],
                                                      valid[:, i:i + 1], g, ALU.mult, ALU.mult)
                    last.then_inc(cmp_vec, 1)
                    dve.wait_ge(cmp_vec, 7)
                    v.tensor_tensor(maps, maps, bc(cst1[:, 1, :].unsqueeze(2), [P, 16, CMP_PAD]), ALU.mult)\
                        .then_inc(cmp_vec, 1)
                elif kind == "conv":
                    for b in s[1:]:
                        dve.wait_ge(z_done, b + 1)
                        z, y = blk(CONV + 4 + b), blk(PROD + b)
                        w = [pcol("conv_w", 4 * k + b) for k in range(3)]
                        v.tensor_scalar(y, z, w[2], None, ALU.mult).then_inc(conv_step, 1)
                        dve.wait_ge(conv_step, 3 * b + 1)
                        v.scalar_tensor_tensor(y[:, 1:T], z[:, 0:T - 1], w[1], y[:, 1:T], ALU.mult, ALU.add)\
                            .then_inc(conv_step, 1)
                        dve.wait_ge(conv_step, 3 * b + 2)
                        v.scalar_tensor_tensor(y[:, 2:T], z[:, 0:T - 2], w[0], y[:, 2:T], ALU.mult, ALU.add)\
                            .then_inc(conv_step, 1)
                elif kind == "mix":
                    j = s[1]
                    if j:
                        low_parts("out2", range(4))
                        dve.wait_ge(o_ready, 8)
                    inverse(filled(*s), 4 + j)
                    for c in range(4):
                        g = pcol(("conv_g", "attn_g")[j], c)
                        o = blk(OT + 4 * j + c)
                        v.scalar_tensor_tensor(o, o, g, rstd[:, :], ALU.mult, ALU.mult).then_inc(o_ready, 1)
                    if j:
                        low_parts("out2", range(4, KC))
                elif kind == "out2":
                    for nb in range(KC):
                        lows(ahead_in(s, nb))
                        n = VT[s + (nb,)]
                        dve.wait_ge(v_done, n + 1)
                        v.scalar_tensor_tensor(xres[:, nb, :], vbuf(n), mod[:, 16 + nb:17 + nb], xres[:, nb, :],
                                               ALU.mult, ALU.add).then_inc(v_read, 1)

            def best16(pieces, values, index):
                for s_, v_ in zip(pieces, values):
                    last = v.max(v_[:, 0:8], s_)
                last.then_inc(topk_step, 1)
                yield
                for s_, v_, i_ in zip(pieces, values, index):
                    v.max_index(i_[:, 0:8], v_[:, 0:8], s_)
                for s_, v_ in zip(pieces, values):
                    last = v.match_replace(s_, v_[:, 0:8], s_, LOWEST)
                last.then_inc(topk_step, 1)
                yield
                for s_, v_ in zip(pieces, values):
                    last = v.max(v_[:, 8:16], s_)
                last.then_inc(topk_step, 1)
                yield
                for s_, v_, i_ in zip(pieces, values, index):
                    last = v.max_index(i_[:, 8:16], v_[:, 8:16], s_)
                last.then_inc(topk_step, 1)
                yield

            for i in range(TT):
                dve.wait_ge(key_read, 2 * i + 2)
                at = TILE_STEPS * i
                mh = [(m, hd) for m in range(2) for hd in range(HEADS)]
                for _ in best16([scores_of(i)[:, m, hd, :] for m, hd in mh], [top_v[:, m, hd, :] for m, hd in mh],
                                [top_i[:, m, hd, :] for m, hd in mh]):
                    at += 1
                    dve.wait_ge(topk_step, at)
                v.tensor_copy(top_f[:, :, :, :], top_i[:, :, :, :])
                n = 2 * HEADS * NKEYS
                cand = s_sb[:, n * i:n * i + n].rearrange("p (h a b) -> p h a b", h=HEADS, a=TOPK)
                v.tensor_tensor(cand, bc(top_v[:, 0, :, :].unsqueeze(3), [P, HEADS, TOPK, TOPK]),
                                bc(top_v[:, 1, :, :].unsqueeze(2), [P, HEADS, TOPK, TOPK]), ALU.add)\
                    .then_inc(topk_step, 1)
                at += 1
                dve.wait_ge(topk_step, at)
                cands = s_sb[:, n * i:n * i + n].rearrange("p (h c) -> p h c", h=HEADS)
                for _ in best16([cands[:, hd, :] for hd in range(HEADS)], [best_v[:, i, hd, :] for hd in range(HEADS)],
                                [best_i[:, hd, :] for hd in range(HEADS)]):
                    at += 1
                    dve.wait_ge(topk_step, at)
                v.tensor_single_scalar(best_p[:, 0, :, :], best_i[:, :, :], 4, ALU.logical_shift_right)
                v.tensor_single_scalar(best_p[:, 1, :, :], best_i[:, :, :], 15, ALU.bitwise_and).then_inc(topk_step, 1)
                dve.wait_ge(topk_step, at + 1)
                v.tensor_copy(best_f[:, :, :, :], best_p[:, :, :, :]).then_inc(topk_step, 1)
                dve.wait_ge(topk_step, at + 2)
                dve.wait_ge(key_done, 4)
                for k in range(2):
                    v.tensor_tensor(cmp_of(k), bc(best_f[:, k, :, :].unsqueeze(3), [P, HEADS, TOPK, TOPK]),
                                    bc(iota[:, 0:TOPK].unsqueeze(1).unsqueeze(1), [P, HEADS, TOPK, TOPK]), ALU.is_equal)\
                        .then_inc(picked, 1)
                for k in range(2):
                    dve.wait_ge(picked, 4 * i + k + 1)
                    v.tensor_tensor(cmp_of(k), cmp_of(k), bc(top_f[:, k, :, :].unsqueeze(2), [P, HEADS, TOPK, TOPK]),
                                    ALU.mult).then_inc(picked, 1)
                for k in range(2):
                    dve.wait_ge(picked, 4 * i + k + 3)
                    last = v.tensor_reduce(sel[:, i, k, :].rearrange("p (h k) -> p h k", h=HEADS), cmp_of(k), AX, ALU.add)
                last.then_inc(topk_step, 1)
                dve.wait_ge(topk_step, at + 3)
            low_u = lambda s, n: low(2 * (NSPLIT + s) % 4, ring[:, (NSLOT + s) % RING, 0:HSLOT], 2 * (NSPLIT + n) + 1)
            at = 2 * TILE_STEPS
            best = best_v[:, :, :, :].rearrange("p i h k -> p (i h) k")
            v.tensor_copy(gsum[:, 0, :], best[:, :, 0]).then_inc(topk_step, 1)
            dve.wait_ge(topk_step, at + 1)
            v.tensor_tensor(best, best, bc(gsum[:, 0, :].unsqueeze(2), [P, TT * HEADS, TOPK]), ALU.subtract)\
                .then_inc(topk_step, 1)
            dve.wait_ge(soft_exp, 1)
            v.tensor_reduce(gsum[:, 1, :], best, AX, ALU.add).then_inc(topk_step, 1)
            dve.wait_ge(topk_step, at + 3)
            v.reciprocal(gsum[:, 2, :], gsum[:, 1, :]).then_inc(topk_step, 1)
            dve.wait_ge(topk_step, at + 4)
            for i in range(TT):
                last = v.tensor_tensor(sel[:, i, 2, :].rearrange("p (h k) -> p h k", h=HEADS), best_v[:, i, :, :],
                                       bc(gsum[:, 2, HEADS * i:HEADS * i + HEADS].unsqueeze(2), [P, HEADS, TOPK]), ALU.mult)
            last.then_inc(topk_step, 1)
            dve.wait_ge(sel_done, 1)
            v.tensor_copy(sel_1[:, :], psum[:, 4, 0:T])
            v.tensor_copy(sel_2[:, :], psum[:, 4, T:2 * T])
            v.tensor_copy(sel_w[0], psum[:, 5, 0:T]).then_inc(sel_read, 1)
            dve.wait_ge(sel_read, 1)
            for x, whole in enumerate((psum[:, 5, 0:T], rest[0])):
                v.tensor_tensor(rest[x], whole, sel_w[x], ALU.subtract).then_inc(sel_read, 1)
                dve.wait_ge(sel_read, 2 * x + 2)
                v.tensor_copy(sel_w[x + 1], rest[x]).then_inc(sel_read, 1)
                dve.wait_ge(sel_read, 2 * x + 3)

            def one_hots(s, q, first):
                def of(x):
                    return bc(x[:, bass.ds(q * 4, 4)].unsqueeze(2), [P, 4, P])

                if not first:
                    dve.wait_ge(route_done, q - 1)
                columns = bc(iota[:, :].unsqueeze(1), [P, 4, P])
                v.tensor_tensor(hot2[:, s % 2, :, :], columns, of(sel_2), ALU.is_equal).then_inc(hot2_ready, 1)
                v.tensor_tensor(hot1[:, s % 2, :, :], columns, of(sel_1), ALU.is_equal).then_inc(hot1_ready, 1)
                dve.wait_ge(hot2_ready, q + 1)
                v.tensor_tensor(wgt[0][:, s % 2, :, :], hot2[:, s % 2, :, :], of(sel_w[0]), ALU.mult)\
                    .then_inc(wgt0_ready, 1)

            for s in range(4):
                low_u(s, POOL_TILES + s)
                one_hots(s, s, s < 2)
            with dve.Fori(POOL_TILES // 4 + 1, (POOL_TILES + QUADS) // 4) as it:
                for s in range(4):
                    low_u(s, it * 4 + s)
                    one_hots(s, it * 4 + s - POOL_TILES, False)
            with dve.Fori((POOL_TILES + QUADS) // 4, P // 4 - 2) as it:
                for s in range(4):
                    low_u(s, it * 4 + s)

            def weigh(j, k):
                dve.wait_ge(g_in, j * 16 + 16)
                a = arena[:, bass.ds(j * GRP + 2 * k, 2), :]
                v.tensor_tensor(a, a, g_back[:, 2 * k:2 * k + 2, :], ALU.mult).then_inc(weighted, 1)

            dve.wait_ge(act_read, GRP)
            for k in range(GRP // 2):
                low_u(k % 4, P - GRP // 2 + k)
                weigh(0, k)

            def low_v(s, n):
                low(2 * (NSPLIT + P + s) % 4, ring[:, (NSLOT + P + s) % RING, 0:HSLOT], 2 * (NSPLIT + P + n) + 1)
                dve.wait_ge(act_hi, n + 1)
                v.tensor_tensor(h_lo[:, s % 4, :], arena[:, n, :], h_hi[:, s % 4, :].bitcast(F32), ALU.subtract)\
                    .then_inc(act_lo, 1)

            dve.wait_ge(act_read, P)
            with dve.Fori(0, GROUPS - 1) as j:
                for s in range(GRP):
                    low_v(s, j * GRP + s)
                    if 4 <= s < 12:
                        weigh(j + 1, s - 4)
            for s in range(GRP):
                low_v(s, (GROUPS - 1) * GRP + s)

            dve.wait_ge(y_done, P)
            for nb in range(KC):
                v.scalar_tensor_tensor(xres[:, nb, :], psum[:, 2 + nb // 2, (nb % 2) * T:(nb % 2) * T + T],
                                       mod[:, 40 + nb:41 + nb], xres[:, nb, :], ALU.mult, ALU.add).then_inc(x_ready, 1)
            dve.wait_ge(x_ready, 2 * KC)
            inverse(filled("norm", 4, "ssq"), 7)
            for c in range(KC):
                v.scalar_tensor_tensor(blk(OUT + c), xres[:, c, :], pcol("ln_final_g", c), rstd[:, :], ALU.mult, ALU.mult)\
                    .then_inc(out_ready, 1)


def rel_bucket(dist):
    n = np.maximum(dist, 0)
    ratio = (np.log(np.maximum(n, 1).astype(np.float32) / np.float32(16)) / np.float32(np.log(8.0))).astype(np.float32)
    large = 16 + (ratio * np.float32(16)).astype(np.int32)
    return np.where(n < 16, n, np.minimum(large, 31))


def constants():
    c = np.zeros((P, NCST), np.float32)

    def put(name, a):
        c[:a.shape[0], CST[name][0]:CST[name][0] + a.shape[1]] = a

    put("ident", np.eye(P, dtype=np.float32))
    put("iota", np.tile(np.arange(P, dtype=np.float32), (P, 1)))
    inv = np.float32(500000.0) ** (-np.arange(0, 16, 2, dtype=np.float32) / np.float32(16))
    ang = np.arange(T, dtype=np.float32)[:, None] * inv[None, :]
    cos, sin = np.ones((P, T), np.float32), np.zeros((P, T), np.float32)
    swap = np.eye(P, dtype=np.float32)
    for base in (0, DH):
        for d in range(8):
            cos[base + d] = cos[base + 8 + d] = np.cos(ang[:, d])
            sin[base + d], sin[base + 8 + d] = -np.sin(ang[:, d]), np.sin(ang[:, d])
            a, b = base + d, base + 8 + d
            swap[a, a] = swap[b, b] = 0
            swap[a, b] = swap[b, a] = 1
    put("perm", swap)
    put("cos", cos)
    put("sin", sin)
    q, k = np.arange(P)[:, None], np.arange(T)[None, :]
    put("mask", np.concatenate([np.where(k[:, :P] <= q, 0, NEG), np.where(k <= q + P, 0, NEG)], 1).astype(np.float32))
    t = np.arange(TT)[None, :] * P + np.arange(P)[:, None]
    put("valid", (t >= 31).astype(np.float32))

    def one_hot(dist):
        o = np.zeros((33, dist.size), np.float32)
        o[rel_bucket(dist), np.arange(dist.size)] = 1
        o[32] = np.where(dist < 0, NEG, 0)
        return o

    put("rev", one_hot(255 - np.arange(TRI)))
    put("fwd", one_hot(np.arange(512) - 272))
    return c


def stream(x):
    w1, w2 = x["w_in"][0], x["w_in_2"][0]
    heads = [0, 4, 1, 5, 2, 6, 3, 7]
    at = np.cumsum([0, 512, 128, 128, 128, 128, 128, 128, 24, 512, 512, 512])

    def cols(w):
        return w.reshape(-1, P, w.shape[1]).transpose(1, 0, 2).reshape(P, -1)

    def head_rows(w):
        return w.reshape(8, DH, -1)[heads].reshape(512, -1)

    base1 = {"dq": 0, "dk": 512, "dg": 1536, "mq": 2048, "mk": 2560, "mg": 3584, "ga": 4096, "gb": 5120}
    nq = w2[:, :512].reshape(D, 8, DH)[:, heads].reshape(D, 512)
    wo2 = np.concatenate([x["w_out_2"][0][512:], head_rows(x["w_out_2"][0][:512])])
    out = np.empty((NSLOT, P, D), np.float32)
    for n, (s, i) in enumerate(SLOTS):
        k, a = s[0], s[1] if len(s) > 1 else None
        if k == "proj" and a in ("dv", "mv"):
            v = cols(w1[:, 1024:1536] if a == "dv" else w1[:, 3072:3584])
            out[n] = v[:, i * D:i * D + D]
        elif k == "proj" and a == "nv":
            v = cols(np.concatenate([w2[:, at[4]:at[5]], w2[:, at[6]:at[7]]], 1))
            out[n] = v[:, i * D:i * D + D]
        elif k == "proj" and a == "gt":
            v = np.zeros((D, P), np.float32)
            v[:, 0:24] = w2[:, at[7]:at[8]]
            out[n] = cols(v)
        elif k == "proj" and a[:2] in base1:
            c = base1[a[:2]] + P * int(a[2:])
            out[n] = cols(w1[:, c:c + P])
        elif k == "proj" and a[:2] == "nq":
            out[n] = cols(nq[:, P * int(a[2:]):][:, :P])
        elif k == "proj" and a in ("kc", "vc", "ks", "kw"):
            c = at[{"kc": 1, "vc": 2, "ks": 3, "kw": 5}[a]]
            out[n] = cols(w2[:, c:c + P])
        elif k == "proj":
            c = at[{"cb": 8, "cc": 9, "ch": 10}[a[:2]]] + P * int(a[2:])
            out[n] = cols(w2[:, c:c + P])
        elif k == "ple":
            out[n] = np.concatenate([cols(x["w_ple"][0][:, P * j:P * j + P]) for j in range(4 * i, 4 * i + 4)], 1)
        elif k == "merge":
            out[n] = np.concatenate([cols(x[w][0][:, P * i:P * i + P]) for w in ("w_branch_diff", "w_branch_moba")], 1)
        elif k in ("cmpk", "cmpv"):
            w = x["cmp_wk1_2" if k == "cmpk" else "cmp_wv1_2"][0]
            out[n] = w.reshape(16, P, DH).transpose(1, 0, 2).reshape(P, D)
        else:
            w = {"out1": x["w_out"][0], "gate": x["w_ple_gate"][0], "out2": wo2, "wq": x["peer_wq_2"][0]}[k]
            out[n] = cols(w[:, P * i:P * i + P])
    return out


def kernel(**inputs):
    import concourse.bacc as bacc
    from concourse.bass_utils import run_bass_kernel_spmd

    x = {k: np.asarray(v) for k, v in inputs.items()}
    heads = [0, 4, 1, 5, 2, 6, 3, 7]

    def col(v):
        return np.asarray(v).reshape(-1, P).T

    par = np.zeros((P, NPAR), np.float32)
    rel = np.ones((33, 8), np.float32)
    rel[:32] = x["rel_table_2"]
    lam = np.concatenate([x[n][0] for n in ("lambda_q1", "lambda_k1", "lambda_q2", "lambda_k2")])
    for name, v in (("norm_g", col(x["norm_g"])), ("final_g", col(x["final_g"])), ("ln_mix_g", col(x["ln_mix_g_2"])),
                    ("ln_ffn_g", col(x["ln_ffn_g_2"])), ("ln_final_g", col(x["ln_final_g_2"])),
                    ("attn_g", col(x["norm_attn_g_2"].reshape(8, DH)[heads])), ("conv_g", col(x["norm_conv_g_2"])),
                    ("subln_g", col(x["subln_g"])), ("conv_w", col(x["conv_w_2"])), ("b_mod", col(x["b_mod_2"])),
                    ("lam", np.tile(lam, (P, 1))), ("rel", rel)):
        par[:v.shape[0], PAR[name][0]:PAR[name][1]] = v
    pe = np.zeros((2, P, T), np.float32)
    for w, n in enumerate(("cmp_pe_k_2", "cmp_pe_v_2")):
        pe[w, :, 0:32:2] = x[n][0].reshape(16, P).T
    arrays = {
        "x_t": x["x"][0].T.reshape(KC, P, T).transpose(1, 0, 2),
        "p_t": x["p"][0, 0].T.reshape(2, P, T).transpose(1, 0, 2),
        "params": par,
        "consts": constants(),
        "weights": stream(x),
        "c_rows": np.tile(x["c_2"], (P, 1)),
        "mods": x["w_mod_2"][0].T.reshape(48, P, D),
        "w2k": x["cmp_wk2_2"][0],
        "w2v": x["cmp_wv2_2"][0],
        "pe": pe,
        "keys": x["peer_keys_2"][0].transpose(1, 3, 0, 2).reshape(P, HEADS, NKEYS),
        "u_t": x["peer_u_2"][0].reshape(P, P, KC, P).transpose(1, 3, 2, 0).reshape(P, P, D),
        "v_rows": x["peer_v_2"][0].reshape(P, P, D).transpose(1, 0, 2),
    }
    nc = bacc.Bacc("TRN2", target_bir_lowering=False, num_devices=1)
    arrays = {k: np.ascontiguousarray(v) for k, v in arrays.items()}
    args = [nc.dram_tensor(k, v.shape, F32, kind="ExternalInput").ap() for k, v in arrays.items()]
    bias_dram = nc.dram_tensor("bias_rows", (P, HEADS, TRI), F32, kind="Internal").ap()
    g_dram = nc.dram_tensor("routing_weights", (P, GROUPS, T * GRP), F32, kind="Internal").ap()
    out_t = nc.dram_tensor("out_t", (KC, P, T), F32, kind="ExternalOutput").ap()
    names = list(arrays)
    block_program(nc, **dict(zip(names, args)), bias_dram=bias_dram, g_dram=g_dram, out_t=out_t)
    r = run_bass_kernel_spmd(nc, [arrays], core_ids=[0])
    return r.results[0]["out_t"].reshape(D, T).T.reshape(1, T, D)
```
